# Optimizing a Trainium2 kernel written in Bass

```python
import math
import jax, jax.numpy as jnp
from jax import lax
import numpy as np

D_MODEL = 1024
BATCH = 1
SEQ = 256
DEPTH = 1

HEAD_DIM = 64
DIFF_HEADS = 4
DIFF_V_DIM = 2 * HEAD_DIM
DSA_HEADS = 4
DSA_LATENT = 128
DSA_V_DIM = 64
IDX_HEADS = 8
IDX_DIM = 32
DSA_TOPK_MAX = 256
MOBA_HEADS = 4
MOBA_BLOCK = 256
MOBA_TOPK_MAX = 3
N_BUCKETS = 32
MAX_DISTANCE = 128
N_BIAS_HEADS = DIFF_HEADS + DSA_HEADS + MOBA_HEADS
D_FF = 4 * D_MODEL
Q_BLOCK = 128
MOBA_Q_CHUNK = 32
EPS = 1e-6

A_Q = DIFF_HEADS * 2 * HEAD_DIM
A_K = DIFF_HEADS * 2 * HEAD_DIM
A_V = DIFF_HEADS * DIFF_V_DIM
B_Q = DSA_HEADS * DSA_LATENT
B_KV = DSA_LATENT
B_IQ = IDX_HEADS * IDX_DIM
B_IK = IDX_DIM
B_IW = IDX_HEADS
C_QKV = MOBA_HEADS * HEAD_DIM
G_COLS = 3 * D_MODEL
SPLIT_SIZES = (A_Q, A_K, A_V, B_Q, B_KV, B_IQ, B_IK, B_IW, C_QKV, C_QKV, C_QKV, G_COLS)
IN_COLS = A_Q + A_K + A_V + B_Q + B_KV + B_IQ + B_IK + B_IW + 3 * C_QKV + G_COLS


def rmsnorm(x, g):
    xf = x.astype(jnp.float32)
    y = xf * lax.rsqrt(jnp.mean(xf * xf, axis=-1, keepdims=True) + EPS)
    return y.astype(x.dtype) * g

def split_cols(p):
    out = []
    off = 0
    for n in SPLIT_SIZES:
        out.append(p[..., off:off + n])
        off += n
    return out

def t5_bucket(dist):
    max_exact = N_BUCKETS // 2
    n = jnp.maximum(dist, 0)
    nf = jnp.maximum(n, 1).astype(jnp.float32)
    large = max_exact + (jnp.log(nf / max_exact) / math.log(MAX_DISTANCE / max_exact)
                         * (N_BUCKETS - max_exact)).astype(jnp.int32)
    large = jnp.minimum(large, N_BUCKETS - 1)
    return jnp.where(n < max_exact, n, large)

def diff_attention(q, k, v, lam, lam_init, subln_g, bias_a):
    B, S, H = q.shape[0], q.shape[1], q.shape[2]
    E = v.shape[-1]
    kpos = jnp.arange(S)
    scale = HEAD_DIM ** -0.5
    bias_t = bias_a.T

    def block(i):
        q0 = i * Q_BLOCK
        qb = lax.dynamic_slice_in_dim(q, q0, Q_BLOCK, axis=1)
        qpos = q0 + jnp.arange(Q_BLOCK)
        dist = qpos[:, None] - kpos[None, :]
        bias = bias_t[:, t5_bucket(dist)]
        logits = jnp.einsum('bqhmd,bkhmd->bhmqk', qb, k).astype(jnp.float32) * scale + bias[None, :, None]
        logits = jnp.where(dist >= 0, logits, -jnp.inf)
        p = jax.nn.softmax(logits, axis=-1)
        attn = p[:, :, 0] - lam * p[:, :, 1]
        return jnp.einsum('bhqk,bkhe->bqhe', attn.astype(v.dtype), v)

    o = lax.map(block, jnp.arange(S // Q_BLOCK))
    o = jnp.moveaxis(o, 0, 1).reshape(B, S, H, E)
    o = rmsnorm(o, subln_g) * (1.0 - lam_init)
    return o.reshape(B, S, H * E)

def dsa_attention(q_lat, kv_lat, iq, ik, iw, w_uv, bias_b):
    B, S, H, R = q_lat.shape
    topk = min(DSA_TOPK_MAX, S // 4)
    kpos = jnp.arange(S)
    bidx = jnp.arange(B)[:, None, None]
    hidx = jnp.arange(H)[None, None, :, None]
    bias_t = bias_b.T
    idx_scale = (IDX_HEADS ** -0.5) * (IDX_DIM ** -0.5)

    def block(i):
        q0 = i * Q_BLOCK
        qpos = q0 + jnp.arange(Q_BLOCK)
        qb = lax.dynamic_slice_in_dim(q_lat, q0, Q_BLOCK, axis=1)
        iqb = lax.dynamic_slice_in_dim(iq, q0, Q_BLOCK, axis=1)
        iwb = lax.dynamic_slice_in_dim(iw, q0, Q_BLOCK, axis=1)
        causal = qpos[:, None] >= kpos[None, :]
        s_idx = jax.nn.relu(jnp.einsum('bqhd,bkd->bqhk', iqb, ik))
        score = jnp.einsum('bqhk,bqh->bqk', s_idx, iwb).astype(jnp.float32) * idx_scale
        score = jnp.where(causal[None], score, -jnp.inf)
        _, sel = lax.top_k(score, topk)
        dist = qpos[None, :, None] - sel
        valid = dist >= 0
        kv_sel = kv_lat[bidx, sel]
        logits = jnp.einsum('bqhr,bqkr->bqhk', qb, kv_sel).astype(jnp.float32) * (R ** -0.5)
        bias = bias_t[hidx, t5_bucket(dist)[:, :, None, :]]
        logits = jnp.where(valid[:, :, None, :], logits + bias, -jnp.inf)
        p = jax.nn.softmax(logits, axis=-1)
        return jnp.einsum('bqhk,bqkr->bqhr', p.astype(kv_sel.dtype), kv_sel)

    o = lax.map(block, jnp.arange(S // Q_BLOCK))
    o = jnp.moveaxis(o, 0, 1).reshape(B, S, H, R)
    o = jnp.einsum('bshr,hre->bshe', o, w_uv)
    return o.reshape(B, S, H * DSA_V_DIM)

def moba_attention(q, k, v, bias_c):
    B, S, H, Dh = q.shape
    nb = -(-S // MOBA_BLOCK)
    sp = nb * MOBA_BLOCK
    pad = ((0, 0), (0, sp - S), (0, 0), (0, 0))
    k_bh = jnp.pad(k, pad).reshape(B, nb, MOBA_BLOCK, H, Dh).transpose(0, 3, 1, 2, 4)
    v_bh = jnp.pad(v, pad).reshape(B, nb, MOBA_BLOCK, H, Dh).transpose(0, 3, 1, 2, 4)
    k_mean = jnp.mean(k_bh, axis=3)
    topb = min(MOBA_TOPK_MAX, nb)
    bias_t = bias_c.T
    bi = jnp.arange(B)[:, None, None, None]
    hi = jnp.arange(H)[None, :, None, None]
    hi5 = jnp.arange(H)[None, :, None, None, None]
    blk_ids = jnp.arange(nb)
    in_blk = jnp.arange(MOBA_BLOCK)
    scale = Dh ** -0.5

    def chunk(i):
        q0 = i * MOBA_Q_CHUNK
        qpos = q0 + jnp.arange(MOBA_Q_CHUNK)
        j = q0 // MOBA_BLOCK
        qc = lax.dynamic_slice_in_dim(q, q0, MOBA_Q_CHUNK, axis=1).transpose(0, 2, 1, 3)
        gate = jnp.einsum('bhqd,bhnd->bhqn', qc, k_mean).astype(jnp.float32)
        gate = jnp.where(blk_ids < j, gate, -jnp.inf)
        _, sel = lax.top_k(gate, topb)
        sel_valid = sel < j
        k_sel = k_bh[bi, hi, sel]
        v_sel = v_bh[bi, hi, sel]
        lp = jnp.einsum('bhqd,bhqnkd->bhqnk', qc, k_sel).astype(jnp.float32) * scale
        dist_p = qpos[None, None, :, None, None] - (sel[..., None] * MOBA_BLOCK + in_blk)
        lp = lp + bias_t[hi5, t5_bucket(dist_p)]
        lp = jnp.where(sel_valid[..., None], lp, -jnp.inf).reshape(B, H, MOBA_Q_CHUNK, topb * MOBA_BLOCK)
        k_own = lax.dynamic_slice_in_dim(k_bh, j, 1, axis=2)[:, :, 0]
        v_own = lax.dynamic_slice_in_dim(v_bh, j, 1, axis=2)[:, :, 0]
        lo = jnp.einsum('bhqd,bhkd->bhqk', qc, k_own).astype(jnp.float32) * scale
        dist_o = qpos[:, None] - (j * MOBA_BLOCK + in_blk)[None, :]
        lo = jnp.where(dist_o >= 0, lo + bias_t[:, t5_bucket(dist_o)][None], -jnp.inf)
        p = jax.nn.softmax(jnp.concatenate([lp, lo], axis=-1), axis=-1)
        pp = p[..., :topb * MOBA_BLOCK].reshape(B, H, MOBA_Q_CHUNK, topb, MOBA_BLOCK)
        po = p[..., topb * MOBA_BLOCK:]
        o = (jnp.einsum('bhqnk,bhqnkd->bhqd', pp.astype(v.dtype), v_sel)
             + jnp.einsum('bhqk,bhkd->bhqd', po.astype(v.dtype), v_own))
        return o.transpose(0, 2, 1, 3)

    o = lax.map(chunk, jnp.arange(S // MOBA_Q_CHUNK))
    return jnp.moveaxis(o, 0, 1).reshape(B, S, H * Dh)

def first_inputs(seed: int = 0) -> dict:
    key = jax.random.key(seed)
    ks = jax.random.split(key, 20)

    def nrm(k, shape, s):
        return jax.random.normal(k, shape, jnp.float32) * s

    return {
        'x': nrm(ks[0], (BATCH, SEQ, D_MODEL), 1.0),
        'c': nrm(ks[1], (BATCH, D_MODEL), 1.0),
        'rel_bias': nrm(ks[2], (N_BUCKETS, N_BIAS_HEADS), 0.5),
        'ada_w': nrm(ks[3], (DEPTH, D_MODEL, 6 * D_MODEL), D_MODEL ** -0.5),
        'ada_b': nrm(ks[4], (DEPTH, 6 * D_MODEL), 0.02),
        'norm_mix': 1.0 + nrm(ks[5], (DEPTH, D_MODEL), 0.02),
        'w_in': nrm(ks[6], (DEPTH, D_MODEL, IN_COLS), D_MODEL ** -0.5),
        'gate_b': nrm(ks[7], (DEPTH, G_COLS), 0.02),
        'diff_lambda': nrm(ks[8], (DEPTH, 4, HEAD_DIM), 0.1),
        'diff_subln': 1.0 + nrm(ks[9], (DEPTH, DIFF_V_DIM), 0.02),
        'dsa_kv_norm': 1.0 + nrm(ks[10], (DEPTH, DSA_LATENT), 0.02),
        'dsa_w_uv': nrm(ks[11], (DEPTH, DSA_HEADS, DSA_LATENT, DSA_V_DIM), DSA_LATENT ** -0.5),
        'w_br_a': nrm(ks[12], (DEPTH, A_V, D_MODEL), A_V ** -0.5),
        'w_br_b': nrm(ks[13], (DEPTH, DSA_HEADS * DSA_V_DIM, D_MODEL), (DSA_HEADS * DSA_V_DIM) ** -0.5),
        'w_br_c': nrm(ks[14], (DEPTH, C_QKV, D_MODEL), C_QKV ** -0.5),
        'w_o': nrm(ks[15], (DEPTH, D_MODEL, D_MODEL), D_MODEL ** -0.5),
        'norm_mlp': 1.0 + nrm(ks[16], (DEPTH, D_MODEL), 0.02),
        'w_ff1': nrm(ks[17], (DEPTH, D_MODEL, D_FF), D_MODEL ** -0.5),
        'w_ff2': nrm(ks[18], (DEPTH, D_FF, D_MODEL), D_FF ** -0.5),
        'norm_final': 1.0 + nrm(ks[19], (D_MODEL,), 0.02),
    }

def first_block(x, c, rel_bias, ada_w, ada_b, norm_mix, w_in, gate_b, diff_lambda, diff_subln,
              dsa_kv_norm, dsa_w_uv, w_br_a, w_br_b, w_br_c, w_o, norm_mlp, w_ff1, w_ff2,
              norm_final):
    B, S, _ = x.shape
    bias_tab = rel_bias.astype(jnp.float32)
    bias_a = bias_tab[:, :DIFF_HEADS]
    bias_b = bias_tab[:, DIFF_HEADS:DIFF_HEADS + DSA_HEADS]
    bias_c = bias_tab[:, DIFF_HEADS + DSA_HEADS:]
    cond = jax.nn.silu(c)
    for l in range(DEPTH):
        mod = (cond @ ada_w[l] + ada_b[l]).reshape(B, 6, D_MODEL)[:, :, None, :]
        shift1, scale1, gate1 = mod[:, 0], mod[:, 1], mod[:, 2]
        shift2, scale2, gate2 = mod[:, 3], mod[:, 4], mod[:, 5]

        u = rmsnorm(x, norm_mix[l]) * (1.0 + scale1) + shift1
        aq, ak, av, bq, bkv, biq, bik, biw, cq, ck, cv, g = split_cols(u @ w_in[l])

        lam_init = 0.8 - 0.6 * math.exp(-0.3 * l)
        dl = diff_lambda[l].astype(jnp.float32)
        lam = jnp.exp(jnp.sum(dl[0] * dl[1])) - jnp.exp(jnp.sum(dl[2] * dl[3])) + lam_init
        y_a = diff_attention(aq.reshape(B, S, DIFF_HEADS, 2, HEAD_DIM),
                             ak.reshape(B, S, DIFF_HEADS, 2, HEAD_DIM),
                             av.reshape(B, S, DIFF_HEADS, DIFF_V_DIM),
                             lam, lam_init, diff_subln[l], bias_a) @ w_br_a[l]
        y_b = dsa_attention(bq.reshape(B, S, DSA_HEADS, DSA_LATENT),
                            rmsnorm(bkv, dsa_kv_norm[l]),
                            biq.reshape(B, S, IDX_HEADS, IDX_DIM), bik, biw,
                            dsa_w_uv[l], bias_b) @ w_br_b[l]
        y_c = moba_attention(cq.reshape(B, S, MOBA_HEADS, HEAD_DIM),
                             ck.reshape(B, S, MOBA_HEADS, HEAD_DIM),
                             cv.reshape(B, S, MOBA_HEADS, HEAD_DIM), bias_c) @ w_br_c[l]
        gates = jax.nn.sigmoid(g + gate_b[l]).reshape(B, S, 3, D_MODEL)
        merged = gates[:, :, 0] * y_a + gates[:, :, 1] * y_b + gates[:, :, 2] * y_c
        x = x + gate1 * (merged @ w_o[l])

        u2 = rmsnorm(x, norm_mlp[l]) * (1.0 + scale2) + shift2
        h = jnp.square(jax.nn.relu(u2 @ w_ff1[l]))
        x = x + gate2 * (h @ w_ff2[l])
    return rmsnorm(x, norm_final)


DEPTH_2 = 2

EXPAND = 2
D_MIX = EXPAND * D_MODEL
D_CONV = D_MIX // 2
D_RET = D_MIX - D_CONV
CONV_GROUPS = 8
CONV_K = 3
RET_HEADS = 8
RET_HEAD_DIM = D_RET // RET_HEADS
CHUNK = 128
ROPE_BASE = 10000.0
NORM_EPS = 1e-6
IN_COLS_2 = 4 * D_CONV + 4 * D_RET


def rms_norm(x, g, eps=NORM_EPS):
    xf = x.astype(jnp.float32)
    y = xf * lax.rsqrt(jnp.mean(xf * xf, axis=-1, keepdims=True) + eps)
    return (y * g.astype(jnp.float32)).astype(x.dtype)

def rotary_tables(positions):
    half = RET_HEAD_DIM // 2
    inv_freq = 1.0 / (ROPE_BASE ** (jnp.arange(half, dtype=jnp.float32) / half))
    ang = positions.astype(jnp.float32)[..., None] * inv_freq
    return jnp.cos(ang)[:, :, None, :], jnp.sin(ang)[:, :, None, :]

def apply_rotary(x, cos, sin):
    xf = x.astype(jnp.float32)
    x1, x2 = jnp.split(xf, 2, axis=-1)
    return jnp.concatenate([x1 * cos - x2 * sin, x2 * cos + x1 * sin], axis=-1).astype(x.dtype)

def causal_depthwise_conv(u, w):
    c = u.shape[-1]
    return lax.conv_general_dilated(
        u, w.astype(u.dtype)[:, None, :], window_strides=(1,), padding=[(CONV_K - 1, 0)],
        dimension_numbers=("NWC", "WIO", "NWC"), feature_group_count=c)

def retention_chunkwise(q, k, v, log_gamma):
    b, s, h, dh = q.shape
    n = s // CHUNK
    q = q.reshape(b, n, CHUNK, h, dh)
    k = k.reshape(b, n, CHUNK, h, dh) * (dh ** -0.5)
    v = v.reshape(b, n, CHUNK, h, dh)
    idx = jnp.arange(CHUNK, dtype=jnp.float32)
    diff = idx[:, None] - idx[None, :]
    causal = diff >= 0
    decay = jnp.where(causal[None], jnp.exp(log_gamma[:, None, None] * jnp.where(causal, diff, 0.0)[None]), 0.0)
    scores = jnp.einsum("bnihd,bnjhd->bnhij", q, k).astype(jnp.float32) * decay
    intra = jnp.einsum("bnhij,bnjhe->bnihe", scores, v.astype(jnp.float32))
    k_w = jnp.exp((CHUNK - 1 - idx)[:, None] * log_gamma[None, :])
    kv = jnp.einsum("bnjhd,bnjhe->nbhde", k.astype(jnp.float32) * k_w[:, :, None],
                    v.astype(jnp.float32))
    chunk_decay = jnp.exp(CHUNK * log_gamma)[None, :, None, None]

    def step(state, kv_n):
        return chunk_decay * state + kv_n, state

    init = jnp.zeros((b, h, dh, dh), jnp.float32)
    _, prev = lax.scan(step, init, kv)
    q_w = jnp.exp((idx + 1.0)[:, None] * log_gamma[None, :])
    cross = jnp.einsum("bnihd,nbhde->bnihe", q.astype(jnp.float32) * q_w[:, :, None], prev)
    return (intra + cross).reshape(b, s, h, dh)

def second_inputs(seed: int = 0) -> dict:
    key = jax.random.key(seed)
    kx, kp, kn1, kw1, kc, kw2, kn2 = jax.random.split(key, 7)
    x = jax.random.normal(kx, (BATCH, SEQ, D_MODEL), jnp.float32)
    offsets = jax.random.randint(kp, (BATCH, 1), 0, 1024, dtype=jnp.int32)
    positions = offsets + jnp.arange(SEQ, dtype=jnp.int32)[None, :]
    pre_norm = 1.0 + 0.05 * jax.random.normal(kn1, (DEPTH_2, D_MODEL), jnp.float32)
    w_in = jax.random.normal(kw1, (DEPTH_2, D_MODEL, IN_COLS_2), jnp.float32) * D_MODEL ** -0.5
    conv_w = jax.random.normal(kc, (DEPTH_2, CONV_K, D_CONV), jnp.float32) * CONV_K ** -0.5
    w_out = jax.random.normal(kw2, (DEPTH_2, D_MIX, D_MODEL), jnp.float32) * D_MIX ** -0.5
    post_norm = 1.0 + 0.05 * jax.random.normal(kn2, (DEPTH_2, D_MODEL), jnp.float32)
    return {"x": x, "positions": positions, "pre_norm": pre_norm, "w_in": w_in,
            "conv_w": conv_w, "w_out": w_out, "post_norm": post_norm}

def second_block(x, positions, pre_norm, w_in, conv_w, w_out, post_norm):
    b, s, _ = x.shape
    cos, sin = rotary_tables(positions)
    log_gamma = jnp.log1p(-jnp.exp2(-5.0 - jnp.arange(RET_HEADS, dtype=jnp.float32)))
    cuts = [D_CONV, 2 * D_CONV, 3 * D_CONV, 4 * D_CONV,
            4 * D_CONV + D_RET, 4 * D_CONV + 2 * D_RET, 4 * D_CONV + 3 * D_RET]
    for layer in range(DEPTH_2):
        h = rms_norm(x, pre_norm[layer])
        proj = jnp.einsum("bsd,dp->bsp", h, w_in[layer])
        c_b, c_c, c_x, c_z, r_q, r_k, r_v, r_z = jnp.split(proj, cuts, axis=-1)
        y_conv = c_b * causal_depthwise_conv(c_c * c_x, conv_w[layer])
        y_conv = y_conv * jax.nn.silu(c_z)
        q = apply_rotary(r_q.reshape(b, s, RET_HEADS, RET_HEAD_DIM), cos, sin)
        k = apply_rotary(r_k.reshape(b, s, RET_HEADS, RET_HEAD_DIM), cos, sin)
        v = r_v.reshape(b, s, RET_HEADS, RET_HEAD_DIM)
        ret = retention_chunkwise(q, k, v, log_gamma)
        ret = ret * lax.rsqrt(jnp.mean(ret * ret, axis=-1, keepdims=True) + NORM_EPS)
        y_ret = ret.reshape(b, s, D_RET).astype(h.dtype) * jax.nn.silu(r_z)
        mix = jnp.concatenate([y_conv.astype(h.dtype), y_ret], axis=-1)
        out = jnp.einsum("bse,ed->bsd", mix, w_out[layer])
        x = x + rms_norm(out, post_norm[layer]).astype(x.dtype)
    return x


def setup_inputs(seed=0):
    out = dict(first_inputs(seed))
    for name, value in second_inputs(seed + 1).items():
        if name != "x":
            out[name + "_2"] = value
    return out


def reference(
    x, c, rel_bias, ada_w, ada_b, norm_mix, w_in, gate_b, diff_lambda, diff_subln, dsa_kv_norm,
    dsa_w_uv, w_br_a, w_br_b, w_br_c, w_o, norm_mlp, w_ff1, w_ff2, norm_final, positions_2,
    pre_norm_2, w_in_2, conv_w_2, w_out_2, post_norm_2,
):
    x = first_block(
        x, c, rel_bias, ada_w, ada_b, norm_mix, w_in, gate_b, diff_lambda, diff_subln,
        dsa_kv_norm, dsa_w_uv, w_br_a, w_br_b, w_br_c, w_o, norm_mlp, w_ff1, w_ff2, norm_final,
    )
    return second_block(
        x, positions_2, pre_norm_2, w_in_2, conv_w_2, w_out_2, post_norm_2,
    )


_drawn_inputs = setup_inputs


def setup_inputs(seed=0):
    import zlib

    import numpy as np

    out = dict(_drawn_inputs(seed))
    spreads = {}
    factors = {'gate_b': 8.0, 'diff_subln': 3.589, 'dsa_kv_norm': 5.648}
    for name, (base, spread) in spreads.items():
        noise = np.random.default_rng([zlib.crc32(name.encode()), seed]).standard_normal(out[name].shape)
        drawn = base * np.exp(spread * noise) if base else spread * noise
        out[name] = __import__('jax').numpy.asarray(drawn.astype(out[name].dtype))
    for name, factor in factors.items():
        out[name] = (out[name] * factor).astype(out[name].dtype)
    return out
```

```python
import math
from contextlib import ExitStack

import numpy as np

import concourse.bass as bass
from concourse import mybir

F32 = mybir.dt.float32
F32R = mybir.dt.float32r
I32 = mybir.dt.int32
ALU = mybir.AluOpType
ACT = mybir.ActivationFunctionType
AX = mybir.AxisListType

P = 128
D = 1024
T = 256
KC = D // P
QT = T // P
HD = 64
NH = 4
LAYERS = 2
RH = 8
TOPK = 64
EPS = 1e-6
NEG = -1.0e30
TAKEN = -3.0e38
N_BUCKETS = 32
MAX_DISTANCE = 128
LAM_INIT = 0.8 - 0.6 * math.exp(0.0)

U_QKV = 0
N_QKV = 27
N_GATE = 24
U_BR = N_QKV + N_GATE
U_WO = U_BR + 8
U_F1 = U_WO + 8
U_F2 = U_F1 + 32
U_LAYER = U_F2 + 32
LAYER_UNITS = 80
UNITS = U_LAYER + LAYERS * LAYER_UNITS
O_BR = U_BR
O_WO = O_BR + 24
O_F1 = O_WO + 8
O_F2 = O_F1 + 32
O_LAYER = O_F2 + 8
LAYER_OUTS = 72
SLOTS = 4
RAW_PAIRS = 4

C_IW, C_IQ, C_IK, C_KV, C_BQ = 0, 1, 3, 4, 5
C_A = 9
C_C = 21

COLS = {}
_at = 0
for _name, _n in (("c", 8), ("ada_b", 48), ("norm_mix", 8), ("gate_b", 24), ("subln", 1), ("kv_norm", 1),
                  ("norm_mlp", 8), ("norm_final", 8), ("pre", 16), ("post", 16), ("conv", 48), ("freq", 2)):
    COLS[_name] = _at
    _at += _n
N_COLS = _at


def lin(g, per, const):
    return const if g is None else g * per + const


class Chain:

    def __init__(self, eng, sem):
        self.eng, self.sem, self.n, self.g, self.per, self.start = eng, sem, 0, None, 0, 0

    def __call__(self, ins):
        self.n += 1
        ins.then_inc(self.sem, 1)
        self.eng.wait_ge(self.sem, lin(self.g, self.per, self.n))

    def enter(self, g, per):
        self.g, self.per, self.start = g, per, self.n

    def leave(self, turns):
        assert self.n - self.start == self.per, (self.n - self.start, self.per)
        self.n = self.start + turns * self.per
        self.g = None


def build(nc, xT, weights, ada, cols, dl, relb, onehot, ident_d, flip_d, cmask_d, decay, positions, w_uv, out):
    with ExitStack() as ctx:
        _build(nc, ctx, xT, weights, ada, cols, dl, relb, onehot, ident_d, flip_d, cmask_d, decay, positions, w_uv, out)


def _build(nc, ctx, xT, weights, ada, cols, dl, relb, onehot, ident_d, flip_d, cmask_d, decay, positions, w_uv, out):
    def tile_in(stack, name, shape, dt=F32):
        return stack.enter_context(nc.sbuf_tensor(name, shape, dt))

    def keep(name, shape, dt=F32):
        return tile_in(ctx, name, shape, dt)

    def sem(name):
        return ctx.enter_context(nc.semaphore(name))

    x = keep("x", [P, KC, T])
    u_hi = keep("u_hi", [P, KC, T], F32R)
    u_lo = keep("u_lo", [P, KC, T], F32R)
    raw = keep("raw", [P, RAW_PAIRS, 2 * KC * P])
    w_hi = keep("w_hi", [P, SLOTS, KC * P], F32R)
    w_lo = keep("w_lo", [P, SLOTS, KC * P], F32R)
    vec = keep("vec", [P, N_COLS])
    mod = keep("mod", [P, 6, KC])
    ident = keep("ident", [P, P])
    ones = keep("ones", [P, P])
    flip = keep("flip", [P, P])
    cosT = keep("cosT", [P, T])
    sinT = keep("sinT", [P, T])
    a_mix = keep("a_mix", [P, 2, KC])
    half_gb = keep("half_gb", [P, 24])
    subln = keep("subln", [P, 1])
    cond = keep("cond", [P, KC])
    lam = keep("lam", [P, 8])
    t_u = keep("t_u", [P, 2, T])
    var = keep("var", [P, 2, T])
    rstd = keep("rstd", [P, 2, T])

    with ExitStack() as early:
        prob = tile_in(early, "prob", [P, 4, 3 * P])
    sq = keep("sq", [P, 2, 2, T])
    acc = keep("acc", [P, 2, T])
    ph1 = ExitStack()
    p1 = lambda name, shape, dt=F32: tile_in(ph1, name, shape, dt)
    ada_raw = p1("ada_raw", [P, 2, 2 * D])
    ada_acc = p1("ada_acc", [P, D])
    v_tok = p1("v_tok", [P, NH, QT, P])
    cv_tok = p1("cv_tok", [P, 2, QT, P])
    stA = ExitStack()
    pA = lambda name, shape, dt=F32: tile_in(stA, name, shape, dt)
    iwf = pA("iwf", [8, T])
    iw = pA("iw", [P, QT, 8])
    iqT = pA("iqT", [P, 2, T])
    ikT = pA("ikT", [P, T])
    relu_s = pA("relu_s", [P, 2, 2 * T])
    kvf = pA("kvf", [P, T])
    kv_sq = pA("kv_sq", [P, T])
    bias_rev = pA("bias_rev", [P, 12, T])
    stA.close()
    gates = p1("gates", [P, 24, T])
    wuv = p1("wuv", [P, NH, HD])
    kvT = p1("kvT", [P, T])
    kv_tok = p1("kv_tok", [P, QT, P])
    o_mid = p1("o_mid", [P, T])
    bqT = p1("bqT", [P, NH, T])
    ob_hi = p1("ob_hi", [P, 2, T], F32R)
    ob_lo = p1("ob_lo", [P, 2, T], F32R)
    oc_hi = p1("oc_hi", [P, 2, T], F32R)
    oc_lo = p1("oc_lo", [P, 2, T], F32R)
    stB = ExitStack()
    pB = lambda name, shape, dt=F32: tile_in(stB, name, shape, dt)
    bias = pB("bias", [P, 12, T])
    aqT = pB("aqT", [P, 2, T])
    akT = pB("akT", [P, 2, T])
    cqT = pB("cqT", [P, 2, T])
    ckT = pB("ckT", [P, 2, T])
    vf = pB("vf", [P, 2, T])
    score = pB("score", [P, 3 * P])
    top8 = pB("top8", [P, 8])
    o_raw = pB("o_raw", [P, NH, T])
    cmask = pB("cmask", [P, T])
    probT = pB("probT", [P, 2, 3 * P])
    o_var = pB("o_var", [P, NH, T])
    nmax = pB("nmax", [P, 16, 2])
    psum_ = pB("psum_", [P, 16, 2])
    rsum = pB("rsum", [P, 16, 2])
    lnorm = pB("lnorm", [P, 4, 2])
    stB.close()
    stC = ExitStack()
    pC = lambda name, shape, dt=F32: tile_in(stC, name, shape, dt)
    oa_hi = pC("oa_hi", [P, NH, T], F32R)
    oa_lo = pC("oa_lo", [P, NH, T], F32R)
    merged = pC("merged", [P, KC, T])
    part = pC("part", [P, 2, T])
    m_hi = pC("m_hi", [P, KC, T], F32R)
    m_lo = pC("m_lo", [P, KC, T], F32R)
    stC.close()
    ph1.close()

    st0 = ExitStack()
    p0 = lambda name, shape, dt=F32: tile_in(st0, name, shape, dt)
    ada_more = p0("ada_pad", [P, 2, 2 * D])
    pad2 = p0("pad2", [P, D])
    dlb = p0("dlb", [P, 4 * HD])
    dlp = p0("dlp", [P, 2 * HD])
    relb_s = p0("relb_s", [N_BUCKETS + 1, 12])
    hot = p0("hot", [N_BUCKETS + 1, 3 * P])
    tab_s = p0("tab_s", [12, 3 * P])
    pos_i = p0("pos_i", [P, T], I32)
    pos_f = p0("pos_f", [P, T])
    ang = p0("ang", [P, 2, T])
    turns = p0("turns", [P, 2, T])
    x_sq = p0("x_sq", [P, KC, T])
    st0.close()

    ph2 = ExitStack()
    p2 = lambda name, shape, dt=F32: tile_in(ph2, name, shape, dt)
    pad3 = p2("pad3", [P, 5, D])
    h_hi = p2("h_hi", [P, 32, T], F32R)
    h_lo = p2("h_lo", [P, 32, T], F32R)
    relu_h = p2("relu_h", [P, 2, T])
    h_full = p2("h_full", [P, 2, T])
    ph2.close()

    ph3 = ExitStack()
    p3 = lambda name, shape, dt=F32: tile_in(ph3, name, shape, dt)
    dec = p3("dec", [P, RH, 3 * P])
    mix_hi = p3("mix_hi", [P, 2 * KC, T], F32R)
    mix_lo = p3("mix_lo", [P, 2 * KC, T], F32R)
    ret = p3("ret", [P, RH, T])
    ret_sq = p3("ret_sq", [P, RH, T])
    zsil = p3("zsil", [P, RH, T])
    qr = p3("qr", [P, 2, T])
    kr = p3("kr", [P, 2, T])
    rt1 = p3("rt1", [P, T])
    rt2 = p3("rt2", [P, T])
    vfr = p3("vfr", [P, 2, T])
    vtr = p3("vtr", [P, 2, QT, P])
    sdec = p3("sdec", [P, 2, 3 * P])
    th = p3("th", [P, 2, T])
    th_c = p3("th_c", [P, 2, T])
    cc = p3("cc", [P, 2, T])
    cv = p3("cv", [P, 2, T + 2])
    cy = p3("cy", [P, 2, T])
    o_out = p3("o_out", [P, KC, T])
    ph3.close()

    tab_d = nc.dram_tensor("tab_scratch", [12, 3 * P], F32, kind="Internal").ap()

    mm = [ctx.enter_context(nc.psum_tensor(f"mm{i}", [P, 512], F32)) for i in range(4)]
    ps_s = [ctx.enter_context(nc.psum_tensor(f"ps_s{i}", [P, 512], F32)) for i in range(2)]
    ps_t = ctx.enter_context(nc.psum_tensor("ps_t", [P, 512], F32))
    ps_o = ctx.enter_context(nc.psum_tensor("ps_o", [P, 512], F32))

    names = """raw_in0 raw_in1 raw_in2 raw_in3 small_in x_in tab_out bias_in flip_done bias_ready decay_in stored
        hi_ready lo_pool lo_dve unit_done part_done taken0 taken1 taken2 taken3
        ada_in0 ada_in1 mod_done mod_ready
        ones_ready act_own dve_own start_act start_dve tab_done tab_evac
        x_squared stat_done var_ready rstd_ready t_ready uhi_ready ulo_ready
        iw_tr iw_ready idx_done relu_ready idx_used kv_squared kv_stat kv_var kv_rstd kvT_ready kv_tr kv_tok_ready
        s_done s_taken max_ready exp_ready p_ready t_done pt_ready o_done o_taken vt_done vt_ready
        uv_done uv_taken osq_ready ostat_done ovar_ready orstd_ready ofin_ready oah_ready oal_ready
        obh_ready
        m_ready mh_ready ml_ready sq_ready 
        hh_ready hl_ready x_final
        rot_ready rv_tr rv_ready rs_done rs_taken ro_done ret_taken retsq_ready th_ready
        rstat_done rvar_ready rrstd_ready yr_ready yrh_ready mixr_ready yc_ready ych_ready mixc_ready
        start_in ada_used och_ready sq_used rms2_ready rstd2_ready x_new""".split()
    S = {n: sem(n) for n in names}
    raw_in = [S[f"raw_in{i}"] for i in range(RAW_PAIRS)]
    taken = [S[f"taken{i}"] for i in range(4)]
    ada_in = [S["ada_in0"], S["ada_in1"]]

    def col(name, i=0):
        return vec[:, COLS[name] + i:COLS[name] + i + 1]

    maps = []
    for h in range(NH):
        for m in range(2):
            maps.append(("a", h, m))
    maps += [("b", h, 0) for h in range(NH)] + [("c", h, 0) for h in range(NH)]
    heads = [("a", h) for h in range(NH)] + [("b", h) for h in range(NH)] + [("c", h) for h in range(NH)]
    maps_of = {r: [i for i, m in enumerate(maps) if m[:2] == heads[r]] for r in range(12)}
    s_at = {r: 11 + 3 * r for r in range(4)} | {4: 23, 5: 26, 6: 29, 7: 32, 8: 35, 9: 37, 10: 39, 11: 41}
    t_at = {r: s_at[r] + 2 for r in range(12)}
    o_at = {r: s_at[r] + 3 for r in range(12)}
    MOD_AT = {8: 2, 16: 3, 24: 4}
    SUB_AT = {16 + 3 * h: h for h in range(NH)}

    block = ctx.enter_context(nc.Block())

    def ada_load(eng, n):
        if n >= 2:
            eng.wait_ge(S["ada_used"], 2 * n - 2)
        eng.dma_start(ada_raw[:, n % 2, :], ada[n]).then_inc(ada_in[n % 2], 16)

    @block.sync
    def _(sp):
        sp.dma_start(vec[:, :], cols).then_inc(S["small_in"], 16)
        sp.dma_start(x[:, :, :], xT).then_inc(S["x_in"], 16)

        def load(g, p):
            src = weights[p] if g is None else weights[bass.ds(g * 4 + p, 1)].rearrange("o p n -> p (o n)")
            if p >= RAW_PAIRS:
                n = 2 * p - 2 * RAW_PAIRS + 2
                sp.wait_ge(S["lo_pool"], lin(g, 8, n))
                if n % 4 == 0:
                    sp.wait_ge(S["lo_dve"], lin(g, 8, n))
            both = 2 * p + 1 < UNITS
            width = (2 if both else 1) * KC * P
            sp.dma_start(raw[:, p % RAW_PAIRS, 0:width], src[:, 0:width]).then_inc(raw_in[p % RAW_PAIRS], 16)

        for n in range(8):
            ada_load(sp, n)
        for p in range(4):
            load(None, p)
        n_loops = (UNITS // 2 - 4) // 4
        with sp.Fori(0, n_loops) as g:
            for i in range(4):
                load(g, 4 + i)
        for p in range(4 + 4 * n_loops, (UNITS + 1) // 2):
            load(None, p)
        for half in range(2):
            sp.wait_ge(S["x_final"], 4 * half + 4)
            sp.dma_start(out[:, 4 * half:4 * half + 4, :], x[:, 4 * half:4 * half + 4, :]).then_inc(S["stored"], 16)
        sp.wait_ge(S["stored"], 32)

    @block.gpsimd
    def _(pool):
        def low(g, c):
            if c % 4 == 3:
                return
            pool.wait_ge(S["hi_ready"], lin(g, 8, c + 1))
            if c >= SLOTS:
                pool.wait_ge(S["unit_done"], lin(g, 8, c - SLOTS + 1))
            r = raw[:, (c // 2) % RAW_PAIRS, (c % 2) * KC * P:(c % 2 + 1) * KC * P]
            s = c % SLOTS
            nc.gpsimd.tensor_tensor(w_lo[:, s, :], r, w_hi[:, s, :].bitcast(F32), ALU.subtract)\
                .then_inc(S["lo_pool"], 2 if c % 4 == 2 else 1)

        nc.gpsimd.memset(ones[:, :], 1.0).then_inc(S["ones_ready"], 1)
        for c in range(8):
            low(None, c)
        with pool.Fori(0, UNITS // 8 - 1) as g:
            for i in range(8):
                low(g, 8 + i)
        for c in range(UNITS // 8 * 8, UNITS):
            low(None, c)

    @block.tensor
    def _(pe):
        def unit(g, c, o, rhs_hi, rhs_lo, ready=None, parts=1, first=True, last=True, turn=(8, 2)):
            s = c % SLOTS
            per_c, per_o = turn
            pe.wait_ge(S["hi_ready"], lin(g, per_c, c + 1))
            pe.wait_ge(S["lo_dve" if c % 4 == 3 else "lo_pool"], lin(g, per_c, c + 1))
            per = KC // parts
            for q in range(parts):
                oo = o + q
                if first and oo >= 4:
                    pe.wait_ge(taken[oo % 4], lin(g, per_o, oo // 4))
                for k in range(per):
                    t = q * per + k
                    if ready is not None:
                        ready(k, t)
                    dst = mm[oo % 4][:, 0:T]
                    wh = w_hi[:, s, t * P:(t + 1) * P]
                    wl = w_lo[:, s, t * P:(t + 1) * P]
                    a, b = (first and k == 0), (last and k == per - 1)
                    nc.tensor.matmul(dst, wh, rhs_hi(k), start=a, stop=False)
                    nc.tensor.matmul(dst, wh, rhs_lo(k), start=False, stop=False)
                    i = nc.tensor.matmul(dst, wl, rhs_hi(k), start=False, stop=b)
                i.then_inc(S["unit_done"] if q == parts - 1 else S["part_done"], 1)


        def one_at_a_time(first, value):
            last = [first, value]

            def wait(name, count):
                pe.wait_ge(S[last[0]], last[1])
                last[:] = name, count
            return wait

        t_wait = one_at_a_time("tab_evac", 1)
        o_wait = one_at_a_time("var_ready", 1)

        pe.wait_ge(S["start_in"], 8 * 16)
        nc.tensor.matmul(ps_t[0:12, 0:3 * P], relb_s[:, :], hot[:, :], start=True, stop=True)\
            .then_inc(S["tab_done"], 1)
        pe.wait_ge(S["ones_ready"], 1)
        pe.wait_ge(S["x_squared"], 1)
        for k in range(KC):
            i = nc.tensor.matmul(ps_o[:, 0:T], ones[:, :], x_sq[:, k, :], start=k == 0, stop=k == KC - 1)
        i.then_inc(S["stat_done"], 1)

        def mod_columns(m, n):
            pe.wait_ge(S["ada_used"], KC * (n + 1))
            t_wait("mod_ready", n + 1)
            for j in range(KC):
                i = nc.tensor.matmul(ps_t[:, 496 + j:497 + j], ada_acc[:, j * P:(j + 1) * P], ones[:, 0:1],
                                     start=True, stop=True)
            i.then_inc(S["mod_done"], 1)

        mod_columns(0, 0)
        mod_columns(1, 1)

        def iw_transpose():
            pe.wait_ge(taken[C_IW % 4], 1)
            t_wait("iw_ready", 1)
            for t in range(QT):
                i = nc.tensor.transpose(ps_t[:, 8 * t:8 * t + 8], iwf[:, t * P:(t + 1) * P], ident[0:8, 0:8])
            i.then_inc(S["iw_tr"], 1)

        def bias_flip(n):
            if n == 0:
                pe.wait_ge(S["bias_in"], 16)
            if n >= 2:
                pe.wait_ge(S["bias_ready"], n - 1)
            nc.tensor.matmul(ps_s[n % 2][:, :], flip[:, :], bias_rev[:, 2 * n:2 * n + 2, :], start=True, stop=True)\
                .then_inc(S["flip_done"], 1)

        def index_scores(n):
            t, hh = n // 4, n % 4
            if n == 0:
                for c in (C_IQ, C_IQ + 1, C_IK):
                    pe.wait_ge(taken[c % 4], c // 4 + 1)
            if n >= 2:
                pe.wait_ge(S["relu_ready"], n - 1)
            else:
                pe.wait_ge(S["bias_ready"], 6)
            nk = P * (t + 1)
            for half in range(2):
                i = nc.tensor.matmul(ps_s[n % 2][:, half * T:half * T + nk],
                                     iqT[32 * hh:32 * hh + 32, half, t * P:(t + 1) * P],
                                     ikT[32 * hh:32 * hh + 32, 0:nk], start=True, stop=True)
            i.then_inc(S["idx_done"], 1)

        def kv_stat():
            pe.wait_ge(S["kv_squared"], 1)
            o_wait("kv_var", 1)
            nc.tensor.matmul(ps_o[:, 0:T], ones[:, :], kv_sq[:, :], start=True, stop=True)\
                .then_inc(S["kv_stat"], 1)

        def kv_transpose():
            pe.wait_ge(S["kvT_ready"], 1)
            t_wait("kv_tok_ready", 1)
            for t in range(QT):
                i = nc.tensor.transpose(ps_t[:, t * P:(t + 1) * P], kvT[:, t * P:(t + 1) * P], ident[:, :])
            i.then_inc(S["kv_tr"], 1)

        vt_users = [("kv", 0)] + [("a", h) for h in range(NH)] + [("c", j) for j in range(2)]

        def v_transpose(n):
            kind, h = vt_users[n]
            c = C_A + 3 * h + 2 if kind == "a" else C_C + 3 * h + 2
            pe.wait_ge(taken[c % 4], c // 4 + 1)
            t_wait("vt_ready", n)
            for t in range(QT):
                i = nc.tensor.transpose(ps_t[:, t * P:(t + 1) * P], vf[:, n % 2, t * P:(t + 1) * P], ident[:, :])
            i.then_inc(S["vt_done"], 1)

        def q_and_k(r, m):
            kind, h = heads[r]
            if kind == "a":
                return aqT[m * HD:(m + 1) * HD, h % 2, :], akT[m * HD:(m + 1) * HD, h % 2, :]
            if kind == "b":
                return bqT[:, h, :], kvT[:, :]
            j, e = h // 2, h % 2
            return cqT[e * HD:(e + 1) * HD, j, :], ckT[e * HD:(e + 1) * HD, j, :]

        def scores(r):
            kind, h = heads[r]
            last_c = {"a": C_A + 3 * h + 1, "b": C_BQ + h, "c": C_C + 3 * (h // 2) + 1}[kind]
            for c in (last_c - 1, last_c):
                pe.wait_ge(taken[c % 4], c // 4 + 1)
            if r == 0:
                pe.wait_ge(S["relu_ready"], 8)
            for e, m in enumerate(maps_of[r]):
                q, k = q_and_k(r, e)
                if m >= 2:
                    pe.wait_ge(S["s_taken"], m - 1)
                bank = ps_s[m % 2]
                nc.tensor.matmul(bank[:, 0:T], q[:, P:T], k, start=True, stop=True)
                nc.tensor.matmul(bank[:, T:T + P], q[:, 0:P], k[:, 0:P], start=True, stop=True)\
                    .then_inc(S["s_done"], 1)

        def prob_transpose(r):
            pe.wait_ge(S["p_ready"], r + 1)
            t_wait("pt_ready", r + 1)
            pm = prob[:, maps_of[r][-1] % 4, :]
            nc.tensor.transpose(ps_t[:, 0:P], pm[:, T:T + P], ident[:, :])
            nc.tensor.transpose(ps_t[:, P:T], pm[:, 0:P], ident[:, :])
            nc.tensor.transpose(ps_t[:, T:T + P], pm[:, P:T], ident[:, :]).then_inc(S["t_done"], 1)

        def outputs(r):
            kind, h = heads[r]
            pe.wait_ge(S["pt_ready"], r + 1)
            o_wait("o_taken", r + 1)
            pt = probT[:, r % 2, :]
            if kind == "a":
                v, dst = v_tok[:, h, :, :], ps_o[:, 0:T]
            elif kind == "b":
                v, dst = kv_tok[:, :, :], ps_o[:, 0:T]
            else:
                e = h % 2
                v, dst = cv_tok[:, h // 2, :, e * HD:(e + 1) * HD], ps_o[e * HD:(e + 1) * HD, 0:T]
            nc.tensor.matmul(dst, v[:, 0, :], pt[:, 0:T], start=True, stop=False)
            nc.tensor.matmul(dst[:, P:T], v[:, 1, :], pt[:, T:T + P], start=False, stop=True)\
                .then_inc(S["o_done"], 1)

        def up_values(h):
            pe.wait_ge(S["o_taken"], NH + h + 1)
            t_wait("uv_taken", h + 1)
            dst = ps_t[HD * (h % 2):HD * (h % 2) + HD, 0:T]
            nc.tensor.matmul(dst, wuv[:, h, :], o_mid[:, :], start=True, stop=True).then_inc(S["uv_done"], 1)

        def subln_stat(h):
            pe.wait_ge(S["osq_ready"], h + 1)
            o_wait("ovar_ready", h + 1)
            nc.tensor.matmul(ps_o[:, 0:T], ones[:, :], o_var[:, h, :], start=True, stop=True)\
                .then_inc(S["ostat_done"], 1)

        def u_ready(m):
            def wait(k, t):
                pe.wait_ge(S["ulo_ready"], KC * m + k + 1)
            return wait

        uh = lambda k: u_hi[:, k, :]
        ul = lambda k: u_lo[:, k, :]
        for c in range(N_QKV + N_GATE):
            unit(None, c, c, uh, ul, ready=u_ready(0) if c == 0 else None)
            if c == 1:
                iw_transpose()
            if 1 <= c <= 3:
                bias_flip(2 * c - 2)
                bias_flip(2 * c - 1)
            if 4 <= c <= 7:
                index_scores(2 * (c - 4))
                index_scores(2 * (c - 4) + 1)
            if c == 5:
                kv_stat()
            if c == 9:
                kv_transpose()
            for n, cn in VT_AT.items():
                if cn == c:
                    v_transpose(n)
            if c in MOD_AT:
                mod_columns(MOD_AT[c], MOD_AT[c])
            for r in range(12):
                if s_at[r] == c:
                    scores(r)
            for r in range(12):
                if o_at[r] == c:
                    outputs(r)
            for r in range(12):
                if t_at[r] == c:
                    prob_transpose(r)
            if c in UV_AT:
                up_values(UV_AT[c])
            if c in SUB_AT:
                subln_stat(SUB_AT[c])

        o = O_BR
        for n, (kind, q) in enumerate(BR_UNITS):
            src_hi, src_lo = {"a": (oa_hi, oa_lo), "b": (ob_hi, ob_lo), "c": (oc_hi, oc_lo)}[kind]
            if n == 0:
                pe.wait_ge(S["oal_ready"], NH)
            if kind == "b":
                pe.wait_ge(S["uv_taken"], NH)
            if kind == "c":
                pe.wait_ge(S["o_taken"], 12)
            parts = 2 if kind == "a" else 4
            unit(None, U_BR + n, o, lambda k: src_hi[:, k, :], lambda k: src_lo[:, k, :], parts=parts)
            o += parts
        for j in range(KC):
            unit(None, U_WO + j, O_WO + j, lambda k: m_hi[:, k, :], lambda k: m_lo[:, k, :],
                 ready=(lambda k, t: pe.wait_ge(S["ml_ready"], k + 1)) if j == 0 else None)

        def norm_stat(n, two=False):
            pe.wait_ge(S["sq_used"], SQ_BASE[n] + KC)
            o_wait("var_ready", n + 1)
            for e in range(2 if two else 1):
                i = nc.tensor.matmul(ps_o[:, e * T:(e + 1) * T], ones[:, :], acc[:, e, :], start=True, stop=True)
            i.then_inc(S["stat_done"], 1)

        norm_stat(1)
        for i in range(8):
            unit(None, U_F1 + i, O_F1 + i, uh, ul, ready=u_ready(1) if i == 0 else None)
        with pe.Fori(0, 3) as g:
            for i in range(8):
                unit(g, U_F1 + 8 + i, O_F1 + 8 + i, uh, ul)
        mod_columns(5, 5)
        pe.wait_ge(S["hl_ready"], 32)
        with pe.Fori(0, 2) as g:
            for j in range(4):
                for q in range(4):
                    unit(g, U_F2 + 4 * j + q, O_F2 + j, lambda k: h_hi[:, q * KC + k, :],
                         lambda k: h_lo[:, q * KC + k, :], first=q == 0, last=q == 3, turn=(16, 1))
        norm_stat(2, two=True)

        for l in range(LAYERS):
            uA = U_LAYER + LAYER_UNITS * l
            oA = O_LAYER + LAYER_OUTS * l

            def v_tr(g, o, H, h):
                pe.wait_ge(taken[o % 4], lin(g, 2, o // 4 + 1))
                if h + H:
                    pe.wait_ge(S["rv_ready"], lin(g, 2, H + h))
                for t in range(QT):
                    n = nc.tensor.transpose(ps_t[:, t * P:(t + 1) * P], vfr[:, h % 2, t * P:(t + 1) * P], ident[:, :])
                n.then_inc(S["rv_tr"], 1)

            def ret_scores(g, H, h):
                pe.wait_ge(S["rot_ready"], lin(g, 4, 2 * (H + h) + 2))
                if H + h >= 2:
                    pe.wait_ge(S["rs_taken"], lin(g, 2, H + h - 1))
                b = ps_s[h % 2]
                nc.tensor.matmul(b[:, 0:T], kr[:, h % 2, 0:P], qr[:, h % 2, :], start=True, stop=True)
                nc.tensor.matmul(b[:, T:T + P], kr[:, h % 2, P:T], qr[:, h % 2, P:T], start=True, stop=True)\
                    .then_inc(S["rs_done"], 1)

            def ret_out(g, H, h):
                pe.wait_ge(S["rs_taken"], lin(g, 2, H + h + 1))
                pe.wait_ge(S["rv_ready"], lin(g, 2, H + h + 1))
                if H + h:
                    pe.wait_ge(S["ret_taken"], lin(g, 2, H + h))
                nc.tensor.matmul(ps_o[:, 0:T], vtr[:, h % 2, 0, :], sdec[:, h % 2, 0:T], start=True, stop=False)
                nc.tensor.matmul(ps_o[:, P:T], vtr[:, h % 2, 1, :], sdec[:, h % 2, T:T + P], start=False, stop=True)\
                    .then_inc(S["ro_done"], 1)

            def turn(g, n0):
                c0, o0, H = uA + 8 * n0, oA + 8 * n0, RH * l + 2 * n0
                for i in range(8):
                    unit(g, c0 + i, o0 + i, uh, ul, ready=u_ready(2 + l) if n0 + i == 0 else None)
                    if i == 3:
                        v_tr(g, o0 + 2, H, 0)
                        ret_scores(g, H, 0)
                    if i == 4:
                        ret_out(g, H, 0)
                    if i == 6:
                        v_tr(g, o0 + 5, H, 1)
                        ret_scores(g, H, 1)
                    if i == 7:
                        ret_out(g, H, 1)

            turn(None, 0)
            with pe.Fori(0, 3) as g:
                turn(g, 1)
            for n in range(4):
                pe.wait_ge(S["retsq_ready"], RH * l + 2 * n + 2)
                bank = [ps_s[0], ps_s[1], ps_t, ps_o][n]
                if n == 0:
                    pe.wait_ge(S["ret_taken"], RH * l + 8)
                nc.tensor.matmul(bank[:, :], ones[:, :], ret_sq[:, 2 * n:2 * n + 2, :], start=True, stop=True)\
                    .then_inc(S["rstat_done"], 1)
            with pe.Fori(0, 4) as g:
                for i in range(8):
                    unit(g, uA + 32 + i, oA + 32 + i, uh, ul)
            for j in range(KC):
                for q in range(2):
                    off = KC if q == 0 else 0
                    rd = None
                    if j == 0:
                        rd = (lambda s: lambda k, t: pe.wait_ge(S[s], KC * l + k + 1))("mixr_ready" if q == 0 else "mixc_ready")
                    unit(None, uA + 64 + 2 * j + q, oA + 64 + j,
                         (lambda off: lambda k: mix_hi[:, off + k, :])(off),
                         (lambda off: lambda k: mix_lo[:, off + k, :])(off), ready=rd, first=q == 0, last=q == 1)
            norm_stat(3 + 2 * l)
            if l + 1 < LAYERS:
                norm_stat(4 + 2 * l)

    @block.scalar
    def _(act):
        own = Chain(act, S["act_own"])
        A = nc.scalar.activation

        def high(g, c):
            if c >= UNITS:
                return
            act.wait_ge(raw_in[(c // 2) % RAW_PAIRS], lin(g, 16, 16 * (c // 2 // RAW_PAIRS + 1)))
            if c >= SLOTS:
                act.wait_ge(S["unit_done"], lin(g, 8, c - SLOTS + 1))
            r = raw[:, (c // 2) % RAW_PAIRS, (c % 2) * KC * P:(c % 2 + 1) * KC * P]
            A(w_hi[:, c % SLOTS, :], r, ACT.Copy).then_inc(S["hi_ready"], 1)

        act.dma_start(relb_s[:, :], relb).then_inc(S["start_in"], 16)
        act.dma_start(hot[:, :], onehot).then_inc(S["start_in"], 16)
        act.dma_start(dlb[:, :], bass.AP(dl.tensor, 0, [[0, P], [1, 4 * HD]])).then_inc(S["start_in"], 16)
        act.dma_start(pos_i[:, :], bass.AP(positions.tensor, 0, [[0, P], [1, T]])).then_inc(S["start_in"], 16)
        act.dma_start(ident[:, :], ident_d).then_inc(S["start_in"], 16)
        act.dma_start(flip[:, :], flip_d).then_inc(S["start_in"], 16)
        act.dma_start(cmask[:, :], cmask_d).then_inc(S["start_in"], 16)
        act.dma_start(wuv[:, :, :], w_uv).then_inc(S["start_in"], 16)
        act.wait_ge(S["small_in"], 16)
        A(cond[:, :], vec[:, COLS["c"]:COLS["c"] + KC], ACT.Exp, scale=-1.0).then_inc(S["start_act"], 1)
        act.wait_ge(S["start_dve"], 2)
        A(lam[:, 2:4], lam[:, 0:2], ACT.Exp).then_inc(S["start_act"], 1)
        act.wait_ge(S["x_in"], 16)
        A(x_sq[:, :, :], x[:, :, :], ACT.Square).then_inc(S["x_squared"], 1)
        act.wait_ge(S["start_dve"], 3)
        A(sinT[:, :], ang[:, 1, :], ACT.Sin).then_inc(S["start_act"], 1)
        A(cosT[:, :], ang[:, 0, :], ACT.Sin, scale=0.5).then_inc(S["start_act"], 1)
        act.wait_ge(S["tab_done"], 1)
        A(tab_s[:, :], ps_t[0:12, 0:3 * P], ACT.Copy).then_inc(S["tab_evac"], 1)
        act.wait_ge(S["tab_evac"], 1)
        act.dma_start(tab_d, tab_s[:, :]).then_inc(S["tab_out"], 16)

        def root(n):
            act.wait_ge(S["var_ready"], n + 1)
            w = 2 if n == 2 else 1
            A(rstd[:, 0:w, :], var[:, 0:w, :], ACT.Sqrt).then_inc(S["rstd_ready"], 1)

        def make_u_hi(m, shift):
            for k in range(KC):
                act.wait_ge(S["t_ready"], KC * m + k + 1)
                if shift is None:
                    A(u_hi[:, k, :], t_u[:, k % 2, :], ACT.Copy).then_inc(S["uhi_ready"], 1)
                else:
                    A(u_hi[:, k, :], t_u[:, k % 2, :], ACT.Identity, bias=mod[:, shift, k:k + 1])\
                        .then_inc(S["uhi_ready"], 1)

        for c in range(SLOTS):
            high(None, c)
        root(0)
        act.wait_ge(S["tab_out"], 16)
        act.wait_ge(S["stat_done"], 1)
        act.dma_start(bias_rev[:, :, :], bass.AP(tab_d.tensor, 0, [[1, P], [3 * P, 12], [1, T]]))\
            .then_inc(S["bias_in"], 16)
        ada_load(act, 8)
        ada_load(act, 9)
        make_u_hi(0, 0)

        def take(c, dst, w=P):
            A(dst, mm[c % 4][0:w, 0:T], ACT.Copy).then_inc(taken[c % 4], 1)

        def qkv_evac(c):
            if c == C_IW:
                take(c, iwf[:, :], 8)
            elif c < C_IK:
                take(c, iqT[:, c - C_IQ, :])
            elif c == C_IK:
                take(c, ikT[:, :])
            elif c == C_KV:
                take(c, kvf[:, :])
                act.wait_ge(taken[c % 4], c // 4 + 1)
                A(kv_sq[:, :], kvf[:, :], ACT.Square).then_inc(S["kv_squared"], 1)
            elif c < C_A:
                take(c, bqT[:, c - C_BQ, :])
            elif c < C_C:
                h, e = (c - C_A) // 3, (c - C_A) % 3
                if e < 2 and h >= 2:
                    act.wait_ge(S["s_done"], 2 * (h - 2) + 2)
                if e == 2:
                    n = 1 + h
                    if n >= 3:
                        act.wait_ge(S["vt_done"], n - 2)
                    take(c, vf[:, n % 2, :])
                else:
                    take(c, (aqT, akT)[e][:, h % 2, :])
            else:
                j, e = (c - C_C) // 3, (c - C_C) % 3
                if e == 2:
                    n = 1 + NH + j
                    act.wait_ge(S["vt_done"], n - 2)
                    take(c, vf[:, n % 2, :])
                else:
                    take(c, (cqT, ckT)[e][:, j, :])

        def act_bias(n):
            act.wait_ge(S["flip_done"], n + 1)
            A(bias[:, 2 * n:2 * n + 2, :], ps_s[n % 2][:, :].rearrange("p (h k) -> p h k", h=2), ACT.Copy)\
                .then_inc(S["bias_ready"], 1)

        def act_iw():
            act.wait_ge(S["iw_tr"], 1)
            A(iw[:, :, :], ps_t[:, 0:16], ACT.Copy).then_inc(S["iw_ready"], 1)

        def act_relu(n):
            t = n // 4
            act.wait_ge(S["idx_done"], n + 1)
            if n >= 2:
                act.wait_ge(S["idx_used"], n - 1)
            nk = P * (t + 1)
            src = ps_s[n % 2][:, :].rearrange("p (e k) -> p e k", e=2)[:, :, 0:nk]
            dst = relu_s[:, n % 2, :].rearrange("p (e k) -> p e k", e=2)[:, :, 0:nk]
            A(dst, src, ACT.Relu).then_inc(S["relu_ready"], 1)

        def act_kv_tok():
            act.wait_ge(S["kv_tr"], 1)
            A(kv_tok[:, :, :], ps_t[:, 0:T], ACT.Copy).then_inc(S["kv_tok_ready"], 1)

        def act_vt(n):
            kind, h = ("a", n - 1) if n <= NH else ("c", n - 1 - NH)
            act.wait_ge(S["vt_done"], n)
            A(v_tok[:, h, :, :] if kind == "a" else cv_tok[:, h, :, :], ps_t[:, 0:T], ACT.Copy)\
                .then_inc(S["vt_ready"], 1)

        def act_exp(m):
            act.wait_ge(S["max_ready"], m + 1)
            p = prob[:, m % 4, :]
            own(A(p[:, 0:T], p[:, 0:T], ACT.Exp, bias=nmax[:, m, 0:1], accum_out=psum_[:, m, 0:1]))
            A(p[:, T:T + P], p[:, T:T + P], ACT.Exp, bias=nmax[:, m, 1:2], accum_out=psum_[:, m, 1:2])\
                .then_inc(S["exp_ready"], 1)

        def act_pt(r):
            act.wait_ge(S["t_done"], r + 1)
            if r >= 2:
                act.wait_ge(S["o_done"], r - 1)
            A(probT[:, r % 2, :], ps_t[:, 0:3 * P], ACT.Copy).then_inc(S["pt_ready"], 1)

        def act_o(r):
            kind, h = heads[r]
            act.wait_ge(S["o_done"], r + 1)
            if kind == "a":
                A(o_raw[:, h, :], ps_o[:, 0:T], ACT.Copy).then_inc(S["o_taken"], 1)
                act.wait_ge(S["o_taken"], r + 1)
                A(o_var[:, h, :], o_raw[:, h, :], ACT.Square).then_inc(S["osq_ready"], 1)
            elif kind == "b":
                if h:
                    act.wait_ge(S["uv_done"], h)
                A(o_mid[:, :], ps_o[:, 0:T], ACT.Copy).then_inc(S["o_taken"], 1)
            else:
                e = h % 2
                A(oc_hi[e * HD:(e + 1) * HD, h // 2, :], ps_o[e * HD:(e + 1) * HD, 0:T], ACT.Copy)\
                    .then_inc(S["och_ready"], 1)

        def act_uv(h):
            e = h % 2
            act.wait_ge(S["uv_done"], h + 1)
            A(ob_hi[e * HD:(e + 1) * HD, h // 2, :], ps_t[e * HD:(e + 1) * HD, 0:T], ACT.Copy)\
                .then_inc(S["obh_ready"], 1)

        def act_gate(c):
            j = c - N_QKV
            A(gates[:, j, :], mm[c % 4][:, 0:T], ACT.Tanh, scale=0.5, bias=half_gb[:, j:j + 1])\
                .then_inc(taken[c % 4], 1)

        kv_root_at = 6
        next_ada = 10
        for c in range(N_QKV + N_GATE):
            act.wait_ge(S["unit_done"], c + 1)
            (qkv_evac if c < N_QKV else act_gate)(c)
            high(None, c + SLOTS)
            if c % 2 == 0 and next_ada < 20 and c >= 2:
                ada_load(act, next_ada)
                next_ada += 1
            if c - 1 == 1:
                act_iw()
            if 1 <= c - 1 <= 3:
                act_bias(2 * c - 4)
                act_bias(2 * c - 3)
            if 4 <= c - 1 <= 7:
                act_relu(2 * (c - 5))
                act_relu(2 * (c - 5) + 1)
            if c == kv_root_at + 1:
                act.wait_ge(S["kv_var"], 1)
                A(rstd[:, 1, :], var[:, 1, :], ACT.Sqrt).then_inc(S["kv_rstd"], 1)
            if c - 1 == 9:
                act_kv_tok()
            for n, cn in VT_AT.items():
                if cn == c - 1:
                    act_vt(n)
            for r in range(12):
                if o_at[r] == c - 1:
                    act_o(r)
            for r in range(12):
                if t_at[r] == c - 1:
                    act_pt(r)
            if c - 1 in UV_AT:
                act_uv(UV_AT[c - 1])
            for r in range(12):
                if s_at[r] == c - 1:
                    for m in maps_of[r]:
                        act_exp(m)
        act.wait_ge(S["ovar_ready"], NH)
        A(o_var[:, :, :], o_var[:, :, :], ACT.Sqrt).then_inc(S["orstd_ready"], 1)
        for h in range(NH):
            act.wait_ge(S["ofin_ready"], h + 1)
            A(oa_hi[:, h, :], o_raw[:, h, :], ACT.Copy).then_inc(S["oah_ready"], 1)

        for n, (kind, q) in enumerate(BR_UNITS):
            act.wait_ge(S["unit_done"], U_BR + n + 1)
            high(None, U_BR + n + SLOTS)
            if kind == "c":
                for j in range(4 * q, 4 * q + 4):
                    act.wait_ge(S["m_ready"], j + 1)
                    A(m_hi[:, j, :], merged[:, j, :], ACT.Copy, scale=0.5).then_inc(S["mh_ready"], 1)

        def square_x(n, j, src, scale=None):
            k = SQ_BASE[n] + j
            if k >= 2:
                act.wait_ge(S["sq_used"], k - 1)
            if scale is None:
                A(sq[:, k % 2, 0, :], src, ACT.Square).then_inc(S["sq_ready"], 1)
            else:
                own(A(sq[:, k % 2, 0, :], src, ACT.Square))
                A(sq[:, k % 2, 1, :], src, ACT.Square, scale=scale).then_inc(S["sq_ready"], 1)

        for j in range(KC):
            o = O_WO + j
            act.wait_ge(S["unit_done"], U_WO + j + 1)
            high(None, U_WO + j + SLOTS)
            act.wait_ge(taken[o % 4], o // 4 + 1)
            square_x(1, j, x[:, j, :])
        root(1)
        make_u_hi(1, 3)

        def up_turn(g, base):
            for i in range(8):
                c, o, f = U_F1 + base + i, O_F1 + base + i, base + i
                act.wait_ge(S["unit_done"], lin(g, 8, c + 1))
                if f >= 2:
                    act.wait_ge(S["hl_ready"], lin(g, 8, f - 1))
                A(relu_h[:, f % 2, :], mm[o % 4][:, 0:T], ACT.Relu).then_inc(taken[o % 4], 1)
                high(g, c + SLOTS)
                act.wait_ge(taken[o % 4], lin(g, 2, o // 4 + 1))
                dst = h_hi[:, f, :] if g is None else h_hi[:, bass.ds(g * 8 + f, 1), :][:, 0, :]
                A(dst, relu_h[:, f % 2, :], ACT.Square).then_inc(S["hh_ready"], 1)
                if g is None and i in (2, 4):
                    ada_load(act, 21 + i // 2)

        ada_load(act, 20)
        ada_load(act, 21)
        up_turn(None, 0)
        with act.Fori(0, 3) as g:
            up_turn(g, 8)

        act.wait_ge(S["mod_ready"], 6)
        act.dma_start(dec[:, :, :], decay).then_inc(S["decay_in"], 16)
        for j in range(KC):
            for q in range(4):
                c = U_F2 + 4 * j + q
                act.wait_ge(S["unit_done"], c + 1)
                high(None, c + SLOTS)
            o = O_F2 + j
            act.wait_ge(taken[o % 4], o // 4 + 1)
            square_x(2, j, x[:, j, :], scale=col("norm_final", j))
        root(2)
        act.wait_ge(S["rms2_ready"], 1)
        A(rstd[:, 1, :], var[:, 1, :], ACT.Sqrt).then_inc(S["rstd2_ready"], 1)
        make_u_hi(2, None)

        for l in range(LAYERS):
            uA = U_LAYER + LAYER_UNITS * l
            oA = O_LAYER + LAYER_OUTS * l
            H = RH * l

            def a_turn(g, n0):
                c0, o0, hb = uA + 8 * n0, oA + 8 * n0, H + 2 * n0

                def step(i):
                    act.wait_ge(S["unit_done"], lin(g, 8, c0 + i + 1))

                def v_copy(i, h):
                    if hb + h >= 2:
                        act.wait_ge(S["rv_tr"], lin(g, 2, hb + h - 1))
                    A(vfr[:, h, :], mm[(o0 + i) % 4][:, 0:T], ACT.Copy).then_inc(taken[(o0 + i) % 4], 1)

                def vt_copy(h):
                    act.wait_ge(S["rv_tr"], lin(g, 2, hb + h + 1))
                    if hb + h >= 2:
                        act.wait_ge(S["ro_done"], lin(g, 2, hb + h - 1))
                    A(vtr[:, h, :, :], ps_t[:, 0:T], ACT.Copy).then_inc(S["rv_ready"], 1)

                def z_tanh(i, h):
                    act.wait_ge(taken[(o0 + i) % 4], lin(g, 2, (o0 + i) // 4 - 1))
                    A(th[:, h, :], mm[(o0 + i) % 4][:, 0:T], ACT.Tanh, scale=0.5).then_inc(S["th_ready"], 1)

                def o_copy(h):
                    act.wait_ge(S["ro_done"], lin(g, 2, hb + h + 1))
                    n = 2 * n0 + h
                    dst = ret[:, n, :] if g is None else ret[:, bass.ds(g * 2 + n, 1), :][:, 0, :]
                    ds2 = ret_sq[:, n, :] if g is None else ret_sq[:, bass.ds(g * 2 + n, 1), :][:, 0, :]
                    A(dst, ps_o[:, 0:T], ACT.Copy).then_inc(S["ret_taken"], 1)
                    act.wait_ge(S["ret_taken"], lin(g, 2, hb + h + 1))
                    A(ds2, dst, ACT.Square).then_inc(S["retsq_ready"], 1)

                for i in range(8):
                    step(i)
                    if i == 2:
                        v_copy(2, 0)
                    if i == 5:
                        v_copy(5, 1)
                    if i >= 6:
                        z_tanh(i, i - 6)
                    high(g, c0 + i + SLOTS)
                    if i == 4:
                        vt_copy(0)
                    if i == 5:
                        o_copy(0)
                    if i == 7:
                        vt_copy(1)
                        o_copy(1)

            a_turn(None, 0)
            with act.Fori(0, 3) as g:
                a_turn(g, 1)
            for n in range(4):
                act.wait_ge(S["rvar_ready"], 4 * l + n + 1)
                A(ret_sq[:, 2 * n:2 * n + 2, :], ret_sq[:, 2 * n:2 * n + 2, :], ACT.Sqrt).then_inc(S["rrstd_ready"], 1)

            def b_turn(g):
                c0, o0 = uA + 32, oA + 32
                for e in range(2):
                    for i in range(4):
                        ii = 4 * e + i
                        o = o0 + ii
                        act.wait_ge(S["unit_done"], lin(g, 8, c0 + ii + 1))
                        if i == 0:
                            act.wait_ge(taken[(o + 1) % 4], lin(g, 2, (o + 1) // 4 - 1))
                            A(cc[:, e, :], mm[o % 4][:, 0:T], ACT.Copy).then_inc(taken[o % 4], 1)
                        if i == 3:
                            act.wait_ge(taken[o % 4], lin(g, 2, o // 4 - 1))
                            A(th_c[:, e, :], mm[o % 4][:, 0:T], ACT.Tanh, scale=0.5).then_inc(S["th_ready"], 1)
                        high(g, c0 + ii + SLOTS)
                        if i == 1:
                            act.wait_ge(S["yr_ready"], lin(g, 2, 8 * l + e + 1))
                            dst = mix_hi[:, bass.ds(g * 2 + KC + e, 1), :][:, 0, :]
                            A(dst, qr[:, e, :], ACT.Copy, scale=0.5).then_inc(S["yrh_ready"], 1)
                        if i == 3:
                            act.wait_ge(S["yc_ready"], lin(g, 2, 8 * l + e + 1))
                            dst = mix_hi[:, bass.ds(g * 2 + e, 1), :][:, 0, :]
                            A(dst, cy[:, e, :], ACT.Copy, scale=0.5).then_inc(S["ych_ready"], 1)

            with act.Fori(0, 4) as g:
                b_turn(g)
            for j in range(KC):
                for q in range(2):
                    c = uA + 64 + 2 * j + q
                    act.wait_ge(S["unit_done"], c + 1)
                    if q == 1:
                        o = oA + 64 + j
                        A(o_out[:, j, :], mm[o % 4][:, 0:T], ACT.Copy).then_inc(taken[o % 4], 1)
                    high(None, c + SLOTS)
                act.wait_ge(taken[o % 4], o // 4 + 1)
                square_x(3 + 2 * l, j, o_out[:, j, :])
            root(3 + 2 * l)
            if l + 1 < LAYERS:
                for j in range(KC):
                    act.wait_ge(S["x_new"], KC * l + j + 1)
                    square_x(4 + 2 * l, j, x[:, j, :])
                root(4 + 2 * l)
                make_u_hi(3 + l, None)

    @block.vector
    def _(dve):
        own = Chain(dve, S["dve_own"])
        V = nc.vector

        def low(g, c):
            if c % 4 != 3 or c >= UNITS:
                return
            dve.wait_ge(S["hi_ready"], lin(g, 8, c + 1))
            if c >= SLOTS:
                dve.wait_ge(S["unit_done"], lin(g, 8, c - SLOTS + 1))
            r = raw[:, (c // 2) % RAW_PAIRS, (c % 2) * KC * P:(c % 2 + 1) * KC * P]
            s = c % SLOTS
            V.tensor_tensor(w_lo[:, s, :], r, w_hi[:, s, :].bitcast(F32), ALU.subtract).then_inc(S["lo_dve"], 4)

        dve.wait_ge(S["start_in"], 8 * 16)
        V.tensor_tensor(dlp[:, 0:HD], dlb[:, 0:HD], dlb[:, HD:2 * HD], ALU.mult).then_inc(S["start_dve"], 1)
        own(V.tensor_tensor(dlp[:, HD:2 * HD], dlb[:, 2 * HD:3 * HD], dlb[:, 3 * HD:4 * HD], ALU.mult))
        V.tensor_reduce(lam[:, 0:2], dlp[:, :].rearrange("p (a d) -> p a d", a=2), AX.X, ALU.add)\
            .then_inc(S["start_dve"], 1)
        dve.wait_ge(S["small_in"], 16)
        own(V.tensor_copy(pos_f[:, :], pos_i[:, :]))
        for e in range(2):
            own(V.tensor_scalar(ang[:, e, :], pos_f[:, :], col("freq", e), None, ALU.mult))
        big = 12582912.0
        own(V.tensor_scalar(turns[:, :, :], ang[:, :, :], 1.0 / (2 * math.pi), big, ALU.mult, ALU.add))
        own(V.tensor_scalar(turns[:, :, :], turns[:, :, :], big, None, ALU.subtract))
        for cst in TWO_PI_PARTS:
            own(V.scalar_tensor_tensor(ang[:, :, :], turns[:, :, :], -cst, ang[:, :, :], ALU.mult, ALU.add))
        V.tensor_scalar(ang[:, :, :], ang[:, :, :], PI_BELOW, -PI_BELOW, ALU.min, ALU.max).then_inc(S["start_dve"], 1)
        dve.wait_ge(S["start_act"], 1)
        own(V.tensor_scalar(cond[:, :], cond[:, :], 1.0, None, ALU.add))
        own(V.reciprocal(cond[:, :], cond[:, :]))
        own(V.tensor_tensor(cond[:, :], cond[:, :], vec[:, COLS["c"]:COLS["c"] + KC], ALU.mult))
        dve.wait_ge(S["start_act"], 2)
        own(V.tensor_tensor(lam[:, 4:5], lam[:, 3:4], lam[:, 2:3], ALU.subtract))
        own(V.tensor_scalar(lam[:, 5:6], lam[:, 4:5], LAM_INIT, None, ALU.subtract))
        own(V.tensor_scalar(half_gb[:, :], vec[:, COLS["gate_b"]:COLS["gate_b"] + 24], 0.5, None, ALU.mult))
        own(V.tensor_scalar(subln[:, :], col("subln"), 1.0 - LAM_INIT, None, ALU.mult))

        def ada_step(a):
            part_, k = a // KC, a % KC
            n = a // 2
            dve.wait_ge(ada_in[n % 2], 16 * (n // 2 + 1))
            src = ada_raw[:, n % 2, (a % 2) * D:(a % 2 + 1) * D]
            if k == 0:
                if part_:
                    dve.wait_ge(S["mod_done"], part_)
                ins = V.tensor_scalar(ada_acc[:, :], src, cond[:, k:k + 1], None, ALU.mult)
            else:
                ins = V.scalar_tensor_tensor(ada_acc[:, :], src, cond[:, k:k + 1], ada_acc[:, :], ALU.mult, ALU.add)
            ins.then_inc(S["ada_used"], 1)
            dve.wait_ge(S["ada_used"], a + 1)

        def mod_take(m):
            dve.wait_ge(S["mod_done"], m + 1)
            V.tensor_tensor(mod[:, m, :], ps_t[:, 496:504], vec[:, COLS["ada_b"] + KC * m:COLS["ada_b"] + KC * (m + 1)],
                            ALU.add).then_inc(S["mod_ready"], 1)

        def variance(n, bank):
            w = 2 if n == 2 else 1
            dve.wait_ge(S["stat_done"], n + 1)
            own(V.tensor_scalar(var[:, 0:w, :], bank[:, 0:w * T].rearrange("p (a t) -> p a t", a=w), 1.0 / D, EPS if w == 1 else 0.0, ALU.mult, ALU.add))
            if w == 2:
                own(V.tensor_scalar(var[:, 0, :], var[:, 0, :], EPS, None, ALU.add))
                V.reciprocal(var[:, 0, :], var[:, 0, :]).then_inc(S["var_ready"], 1)
            else:
                V.reciprocal(var[:, 0, :], var[:, 0, :]).then_inc(S["var_ready"], 1)

        def make_u(m, scale, r, shift):
            def lo(k):
                dve.wait_ge(S["uhi_ready"], KC * m + k + 1)
                hi = u_hi[:, k, :].bitcast(F32)
                if shift is None:
                    V.tensor_tensor(u_lo[:, k, :], t_u[:, k % 2, :], hi, ALU.subtract).then_inc(S["ulo_ready"], 1)
                else:
                    V.scalar_tensor_tensor(u_lo[:, k, :], t_u[:, k % 2, :], mod[:, shift, k:k + 1], hi,
                                           ALU.add, ALU.subtract).then_inc(S["ulo_ready"], 1)
            for k in range(KC):
                if k >= 2 or m:
                    dve.wait_ge(S["ulo_ready"], KC * m + k - 1)
                V.scalar_tensor_tensor(t_u[:, k % 2, :], x[:, k, :], scale(k), r, ALU.mult, ALU.mult)\
                    .then_inc(S["t_ready"], 1)
                if k:
                    lo(k - 1)
            lo(KC - 1)

        for a in range(2 * KC):
            ada_step(a)
            if a == 2:
                dve.wait_ge(S["x_in"], 16)
                variance(0, ps_o)
                dve.wait_ge(S["start_act"], 4)
                own(V.tensor_tensor(cosT[:, :], cosT[:, :], cosT[:, :], ALU.mult))
                own(V.tensor_scalar(cosT[:, :], cosT[:, :], -2.0, 1.0, ALU.mult, ALU.add))
            if a == KC:
                mod_take(0)
        mod_take(1)
        dve.wait_ge(S["mod_ready"], 2)
        own(V.scalar_tensor_tensor(a_mix[:, 0, :], mod[:, 1, :], 1.0, vec[:, COLS["norm_mix"]:COLS["norm_mix"] + KC],
                                   ALU.add, ALU.mult))
        low(None, 3)
        dve.wait_ge(S["rstd_ready"], 1)
        make_u(0, lambda k: a_mix[:, 0, k:k + 1], rstd[:, 0, :], 0)

        def score_tile(t):
            return score[:, 0:T] if t else score[:, T:T + P]

        def idx_add(n):
            t, hh = n // 4, n % 4
            dve.wait_ge(S["relu_ready"], n + 1)
            if n == 0:
                dve.wait_ge(S["iw_ready"], 1)
            nk = P * (t + 1)
            dst = score_tile(t)
            for e in range(2):
                src = relu_s[:, n % 2, e * T:e * T + nk]
                prev = dst if (hh or e) else (cmask[:, :] if t else cmask[:, P:T])
                ins = V.scalar_tensor_tensor(dst, src, iw[:, t, hh + 4 * e:hh + 4 * e + 1], prev, ALU.mult, ALU.add)
                if e == 0:
                    own(ins)
                else:
                    ins.then_inc(S["idx_used"], 1)
                    dve.wait_ge(S["idx_used"], n + 1)

        def topk_round(t):
            dst = score_tile(t)
            own(V.max(top8[:, :], dst))
            own(V.match_replace(dst, top8[:, :], dst, TAKEN))

        def kv_norm_var():
            dve.wait_ge(S["kv_stat"], 1)
            own(V.tensor_scalar(var[:, 1, :], ps_o[:, 0:T], 1.0 / P, EPS, ALU.mult, ALU.add))
            V.reciprocal(var[:, 1, :], var[:, 1, :]).then_inc(S["kv_var"], 1)

        def kv_norm():
            dve.wait_ge(S["kv_rstd"], 1)
            V.scalar_tensor_tensor(kvT[:, :], kvf[:, :], col("kv_norm"), rstd[:, 1, :], ALU.mult, ALU.mult)\
                .then_inc(S["kvT_ready"], 1)

        SCALE = {"a": HD ** -0.5, "b": P ** -0.5, "c": HD ** -0.5}
        BIAS = {"a": 0, "b": NH, "c": 2 * NH}

        def logits(m):
            kind, h, _ = maps[m]
            r = heads.index((kind, h))
            dve.wait_ge(S["s_done"], m + 1)
            if m == 0:
                dve.wait_ge(S["bias_ready"], 6)
            if m >= 4:
                dve.wait_ge(S["t_done"], heads.index(maps[m - 4][:2]) + 1)
            p, b, ps = prob[:, m % 4, :], bias[:, BIAS[kind] + h, :], ps_s[m % 2]
            own(V.scalar_tensor_tensor(p[:, 0:T], ps[:, 0:T], SCALE[kind], b, ALU.mult, ALU.add))
            V.scalar_tensor_tensor(p[:, T:T + P], ps[:, T:T + P], SCALE[kind], b[:, P:T], ALU.mult, ALU.add)\
                .then_inc(S["s_taken"], 1)
            dve.wait_ge(S["s_taken"], m + 1)
            if kind == "b":
                own(V.tensor_tensor(p, p, score[:, :], ALU.add))
            own(V.tensor_reduce(nmax[:, m, 0:1], p[:, 0:T], AX.X, ALU.max, negate=True))
            V.tensor_reduce(nmax[:, m, 1:2], p[:, T:T + P], AX.X, ALU.max, negate=True).then_inc(S["max_ready"], 1)

        def normalise(r):
            ms = maps_of[r]
            m = ms[-1]
            dve.wait_ge(S["exp_ready"], m + 1)
            for q in ms:
                own(V.reciprocal(rsum[:, q, :], psum_[:, q, :]))
            p = prob[:, m % 4, :]
            if len(ms) == 1:
                own(V.tensor_scalar(p[:, 0:T], p[:, 0:T], rsum[:, m, 0:1], None, ALU.mult))
                V.tensor_scalar(p[:, T:T + P], p[:, T:T + P], rsum[:, m, 1:2], None, ALU.mult)\
                    .then_inc(S["p_ready"], 1)
                return
            p0 = prob[:, ms[0] % 4, :]
            own(V.tensor_scalar(lnorm[:, r, :], rsum[:, m, :], lam[:, 5:6], None, ALU.mult))
            own(V.tensor_scalar(p[:, 0:T], p[:, 0:T], lnorm[:, r, 0:1], None, ALU.mult))
            own(V.tensor_scalar(p[:, T:T + P], p[:, T:T + P], lnorm[:, r, 1:2], None, ALU.mult))
            own(V.scalar_tensor_tensor(p[:, 0:T], p0[:, 0:T], rsum[:, ms[0], 0:1], p[:, 0:T], ALU.mult, ALU.add))
            V.scalar_tensor_tensor(p[:, T:T + P], p0[:, T:T + P], rsum[:, ms[0], 1:2], p[:, T:T + P],
                                   ALU.mult, ALU.add).then_inc(S["p_ready"], 1)

        def sub_var(h):
            dve.wait_ge(S["ostat_done"], h + 1)
            own(V.tensor_scalar(o_var[:, h, :], ps_o[:, 0:T], 1.0 / P, EPS, ALU.mult, ALU.add))
            V.reciprocal(o_var[:, h, :], o_var[:, h, :]).then_inc(S["ovar_ready"], 1)

        def c_low(h):
            e = h % 2
            s = slice(e * HD, (e + 1) * HD)
            dve.wait_ge(S["och_ready"], h + 1)
            V.tensor_tensor(oc_lo[s, h // 2, :], ps_o[s, 0:T], oc_hi[s, h // 2, :].bitcast(F32), ALU.subtract)\
                .then_inc(S["o_taken"], 1)

        def b_low(h):
            e = h % 2
            s = slice(e * HD, (e + 1) * HD)
            dve.wait_ge(S["obh_ready"], h + 1)
            V.tensor_tensor(ob_lo[s, h // 2, :], ps_t[s, 0:T], ob_hi[s, h // 2, :].bitcast(F32), ALU.subtract)\
                .then_inc(S["uv_taken"], 1)

        rounds = [(t, n) for n in range(TOPK // 8) for t in range(QT)]
        ada_at = 2 * KC
        for c in range(N_QKV + N_GATE):
            dve.wait_ge(S["unit_done"], c + 1)
            low(None, c + SLOTS)
            if c < 3 * KC:
                ada_step(ada_at)
                ada_at += 1
            if c in MOD_AT:
                mod_take(MOD_AT[c])
            if c - 1 == 5:
                kv_norm_var()
            if c == kv_norm_step:
                kv_norm()
            if 4 <= c - 1 <= 7:
                idx_add(2 * (c - 5))
                idx_add(2 * (c - 5) + 1)
            if c >= 9 and rounds:
                for _ in range(2):
                    topk_round(rounds.pop(0)[0])
                if not rounds:
                    own(V.tensor_scalar(score[:, :], score[:, :], TAKEN / 2, NEG, ALU.is_gt, ALU.mult))
            for r in range(12):
                if s_at[r] == c - 1:
                    for m in maps_of[r]:
                        logits(m)
            for r in range(12):
                if o_at[r] == c - 1 and heads[r][0] == "c":
                    c_low(heads[r][1])
            if c - 1 in UV_AT:
                b_low(UV_AT[c - 1])
            if c - 1 in SUB_AT:
                sub_var(SUB_AT[c - 1])
            for r in range(12):
                if s_at[r] == c - 2:
                    normalise(r)
        dve.wait_ge(S["orstd_ready"], 1)
        for h in range(NH):
            V.scalar_tensor_tensor(o_raw[:, h, :], o_raw[:, h, :], subln[:, 0:1], o_var[:, h, :], ALU.mult, ALU.mult)\
                .then_inc(S["ofin_ready"], 1)
        for h in range(NH):
            dve.wait_ge(S["oah_ready"], h + 1)
            V.tensor_tensor(oa_lo[:, h, :], o_raw[:, h, :], oa_hi[:, h, :].bitcast(F32), ALU.subtract)\
                .then_inc(S["oal_ready"], 1)
        own(V.scalar_tensor_tensor(a_mix[:, 1, :], mod[:, 4, :], 1.0, vec[:, COLS["norm_mlp"]:COLS["norm_mlp"] + KC],
                                   ALU.add, ALU.mult))

        o = O_BR
        parts_seen = 0
        for n, (kind, q) in enumerate(BR_UNITS):
            parts = 2 if kind == "a" else 4
            for e in range(parts):
                j = parts * q + e
                if e < parts - 1:
                    parts_seen += 1
                    dve.wait_ge(S["part_done"], parts_seen)
                else:
                    dve.wait_ge(S["unit_done"], U_BR + n + 1)
                g_ = gates[:, {"a": 0, "b": KC, "c": 2 * KC}[kind] + j, :]
                if kind == "a":
                    V.scalar_tensor_tensor(merged[:, j, :], g_, 1.0, mm[o % 4][:, 0:T], ALU.add, ALU.mult)\
                        .then_inc(taken[o % 4], 1)
                else:
                    V.scalar_tensor_tensor(part[:, o % 2, :], g_, 1.0, mm[o % 4][:, 0:T], ALU.add, ALU.mult)\
                        .then_inc(taken[o % 4], 1)
                    dve.wait_ge(taken[o % 4], o // 4 + 1)
                    ins = V.tensor_tensor(merged[:, j, :], merged[:, j, :], part[:, o % 2, :], ALU.add)
                    if kind == "b":
                        own(ins)
                    else:
                        ins.then_inc(S["m_ready"], 1)
                o += 1
            low(None, U_BR + n + SLOTS)
            if kind == "c":
                for j in range(4 * q, 4 * q + 4):
                    dve.wait_ge(S["mh_ready"], j + 1)
                    V.scalar_tensor_tensor(m_lo[:, j, :], merged[:, j, :], 0.5, m_hi[:, j, :].bitcast(F32),
                                           ALU.mult, ALU.subtract).then_inc(S["ml_ready"], 1)

        def add_square(n, j, two=False):
            k = SQ_BASE[n] + j
            dve.wait_ge(S["sq_ready"], k + 1)
            w = 2 if two else 1
            if j == 0:
                ins = V.tensor_copy(acc[:, 0:w, :], sq[:, k % 2, 0:w, :])
            else:
                ins = V.tensor_tensor(acc[:, 0:w, :], acc[:, 0:w, :], sq[:, k % 2, 0:w, :], ALU.add)
            ins.then_inc(S["sq_used"], 1)
            dve.wait_ge(S["sq_used"], k + 1)

        for j in range(KC):
            o = O_WO + j
            dve.wait_ge(S["unit_done"], U_WO + j + 1)
            V.scalar_tensor_tensor(x[:, j, :], mm[o % 4][:, 0:T], mod[:, 2, j:j + 1], x[:, j, :], ALU.mult, ALU.add)\
                .then_inc(taken[o % 4], 1)
            low(None, U_WO + j + SLOTS)
            if j:
                add_square(1, j - 1)
        add_square(1, KC - 1)
        variance(1, ps_o)
        dve.wait_ge(S["rstd_ready"], 2)
        make_u(1, lambda k: a_mix[:, 1, k:k + 1], rstd[:, 0, :], 3)

        def up_turn(g, base):
            for i in range(8):
                c, o, f = U_F1 + base + i, O_F1 + base + i, base + i
                dve.wait_ge(taken[o % 4], lin(g, 2, o // 4 + 1))
                own(V.tensor_tensor(h_full[:, f % 2, :], relu_h[:, f % 2, :], relu_h[:, f % 2, :], ALU.mult))
                dve.wait_ge(S["hh_ready"], lin(g, 8, f + 1))
                sl = (lambda t: t[:, f, :]) if g is None else (lambda t: t[:, bass.ds(g * 8 + f, 1), :][:, 0, :])
                V.tensor_tensor(sl(h_lo), h_full[:, f % 2, :], sl(h_hi).bitcast(F32), ALU.subtract)\
                    .then_inc(S["hl_ready"], 1)
                low(g, c + SLOTS)
                if g is None:
                    ada_step(5 * KC + i)

        up_turn(None, 0)
        with dve.Fori(0, 3) as g:
            own.enter(g, 8)
            up_turn(g, 8)
            own.leave(3)
        mod_take(5)
        dve.wait_ge(S["mod_ready"], 6)
        for j in range(KC):
            for q in range(4):
                c = U_F2 + 4 * j + q
                dve.wait_ge(S["unit_done"], c + 1)
                if q == 3:
                    o = O_F2 + j
                    V.scalar_tensor_tensor(x[:, j, :], mm[o % 4][:, 0:T], mod[:, 5, j:j + 1], x[:, j, :],
                                           ALU.mult, ALU.add).then_inc(taken[o % 4], 1)
                low(None, c + SLOTS)
                if q == 0 and j:
                    add_square(2, j - 1, two=True)
        add_square(2, KC - 1, two=True)
        variance(2, ps_o)
        dve.wait_ge(S["rstd_ready"], 3)
        own(V.tensor_tensor(rt1[:, :], rstd[:, 0, :], rstd[:, 0, :], ALU.mult))
        own(V.tensor_tensor(var[:, 1, :], var[:, 1, :], rt1[:, :], ALU.mult))
        own(V.tensor_scalar(var[:, 1, :], var[:, 1, :], EPS, None, ALU.add))
        V.reciprocal(var[:, 1, :], var[:, 1, :]).then_inc(S["rms2_ready"], 1)
        for k in range(KC):
            own(V.scalar_tensor_tensor(x[:, k, :], x[:, k, :], col("norm_final", k), rstd[:, 0, :], ALU.mult, ALU.mult))
        dve.wait_ge(S["rstd2_ready"], 1)
        make_u(2, lambda k: col("pre", k), rstd[:, 1, :], None)
        own(V.memset(cv[:, :, 0:2], 0.0))

        for l in range(LAYERS):
            uA = U_LAYER + LAYER_UNITS * l
            oA = O_LAYER + LAYER_OUTS * l
            H = RH * l

            def a_turn(g, n0):
                c0, o0, hb = uA + 8 * n0, oA + 8 * n0, H + 2 * n0

                def rotate(i, h, dst):
                    ps = mm[(o0 + i) % 4]
                    if hb + h >= 2:
                        dve.wait_ge(S["rs_done"], lin(g, 2, hb + h - 1))
                    own(V.tensor_tensor(rt1[:, :], ps[:, 0:T], cosT[:, :], ALU.mult))
                    own(V.tensor_tensor(rt2[0:HD, :], ps[HD:P, 0:T], sinT[HD:P, :], ALU.mult))
                    V.tensor_tensor(rt2[HD:P, :], ps[0:HD, 0:T], sinT[0:HD, :], ALU.mult)\
                        .then_inc(taken[(o0 + i) % 4], 1)
                    dve.wait_ge(taken[(o0 + i) % 4], lin(g, 2, (o0 + i) // 4 + 1))
                    V.tensor_tensor(dst, rt1[:, :], rt2[:, :], ALU.add).then_inc(S["rot_ready"], 1)
                    n = 2 * (hb + h) + (2 if dst_is_k[0] else 1)
                    dve.wait_ge(S["rot_ready"], lin(g, 4, n))

                def decayed(h):
                    dve.wait_ge(S["rs_done"], lin(g, 2, hb + h + 1))
                    if hb + h >= 2:
                        dve.wait_ge(S["ro_done"], lin(g, 2, hb + h - 1))
                    n = 2 * n0 + h
                    d = dec[:, n, :] if g is None else dec[:, bass.ds(g * 2 + n, 1), :][:, 0, :]
                    V.tensor_tensor(sdec[:, h, :], ps_s[h][:, 0:3 * P], d, ALU.mult).then_inc(S["rs_taken"], 1)

                def silu_z(i, h):
                    n = 2 * n0 + h
                    dst = zsil[:, n, :] if g is None else zsil[:, bass.ds(g * 2 + n, 1), :][:, 0, :]
                    dve.wait_ge(S["th_ready"], lin(g, 2, ZU[l] + 2 * n0 + h + 1))
                    V.scalar_tensor_tensor(dst, th[:, h, :], 1.0, mm[(o0 + i) % 4][:, 0:T], ALU.add, ALU.mult)\
                        .then_inc(taken[(o0 + i) % 4], 1)
                    dve.wait_ge(taken[(o0 + i) % 4], lin(g, 2, (o0 + i) // 4 + 1))

                for i in range(8):
                    dve.wait_ge(S["unit_done"], lin(g, 8, c0 + i + 1))
                    if i in (0, 1, 3, 4):
                        h = 0 if i < 3 else 1
                        dst_is_k = [i in (1, 4)]
                        rotate(i, h, (kr if dst_is_k[0] else qr)[:, h, :])
                    if i >= 6:
                        silu_z(i, i - 6)
                    low(g, c0 + i + SLOTS)
                    if i == 4:
                        decayed(0)
                    if i == 7:
                        decayed(1)

            if l == 0:
                dve.wait_ge(S["decay_in"], 16)
            a_turn(None, 0)
            with dve.Fori(0, 3) as g:
                own.enter(g, 8)
                a_turn(g, 1)
                own.leave(3)
            for n in range(4):
                bank = [ps_s[0], ps_s[1], ps_t, ps_o][n]
                dve.wait_ge(S["rstat_done"], 4 * l + n + 1)
                own(V.tensor_scalar(ret_sq[:, 2 * n:2 * n + 2, :], bank[:, :], 1.0 / P, EPS, ALU.mult, ALU.add))
                V.reciprocal(ret_sq[:, 2 * n:2 * n + 2, :], ret_sq[:, 2 * n:2 * n + 2, :]).then_inc(S["rvar_ready"], 1)
            dve.wait_ge(S["rrstd_ready"], 4 * l + 4)

            def b_turn(g):
                c0, o0 = uA + 32, oA + 32
                row = lambda t, off: t[:, bass.ds(g * 2 + off, 1), :][:, 0, :]
                for e in range(2):
                    wcol = lambda tap: vec[:, bass.ds(g * 2 + (COLS["conv"] + 24 * l + 8 * tap + e), 1)]
                    for i in range(4):
                        ii = 4 * e + i
                        o = o0 + ii
                        ps = mm[o % 4][:, 0:T]
                        tk, tv = taken[o % 4], lin(g, 2, o // 4 + 1)
                        dve.wait_ge(S["unit_done"], lin(g, 8, c0 + ii + 1))
                        if i == 0:
                            own(V.tensor_tensor(rt1[:, :], row(ret, e), row(ret_sq, e), ALU.mult))
                            V.tensor_tensor(qr[:, e, :], rt1[:, :], row(zsil, e), ALU.mult).then_inc(S["yr_ready"], 1)
                            dve.wait_ge(S["yr_ready"], lin(g, 2, 8 * l + e + 1))
                        if i == 1:
                            dve.wait_ge(taken[(o - 1) % 4], lin(g, 2, (o - 1) // 4 + 1))
                            V.tensor_tensor(cv[:, e, 2:T + 2], cc[:, e, :], ps, ALU.mult).then_inc(tk, 1)
                            dve.wait_ge(tk, tv)
                            own(V.tensor_scalar(cy[:, e, :], cv[:, e, 0:T], wcol(0), None, ALU.mult))
                            for tap in (1, 2):
                                own(V.scalar_tensor_tensor(cy[:, e, :], cv[:, e, tap:tap + T], wcol(tap), cy[:, e, :],
                                                           ALU.mult, ALU.add))
                            dve.wait_ge(S["yrh_ready"], lin(g, 2, 8 * l + e + 1))
                            V.scalar_tensor_tensor(row(mix_lo, KC + e), qr[:, e, :], 0.5,
                                                   row(mix_hi, KC + e).bitcast(F32), ALU.mult, ALU.subtract)\
                                .then_inc(S["mixr_ready"], 1)
                        if i == 2:
                            V.tensor_tensor(cy[:, e, :], cy[:, e, :], ps, ALU.mult).then_inc(tk, 1)
                            dve.wait_ge(tk, tv)
                        if i == 3:
                            dve.wait_ge(S["th_ready"], lin(g, 2, ZU[l] + 8 + e + 1))
                            V.scalar_tensor_tensor(rt2[:, :], th_c[:, e, :], 1.0, ps, ALU.add, ALU.mult).then_inc(tk, 1)
                            dve.wait_ge(tk, tv)
                            V.tensor_tensor(cy[:, e, :], cy[:, e, :], rt2[:, :], ALU.mult).then_inc(S["yc_ready"], 1)
                            dve.wait_ge(S["yc_ready"], lin(g, 2, 8 * l + e + 1))
                        low(g, c0 + ii + SLOTS)
                        if i == 3:
                            dve.wait_ge(S["ych_ready"], lin(g, 2, 8 * l + e + 1))
                            V.scalar_tensor_tensor(row(mix_lo, e), cy[:, e, :], 0.5, row(mix_hi, e).bitcast(F32),
                                                   ALU.mult, ALU.subtract).then_inc(S["mixc_ready"], 1)
                            dve.wait_ge(S["mixc_ready"], lin(g, 2, 8 * l + e + 1))

            with dve.Fori(0, 4) as g:
                own.enter(g, 8)
                b_turn(g)
                own.leave(4)
            n_out = 3 + 2 * l
            for j in range(KC):
                for q in range(2):
                    c = uA + 64 + 2 * j + q
                    dve.wait_ge(S["unit_done"], c + 1)
                    low(None, c + SLOTS)
                if j:
                    add_square(n_out, j - 1)
            add_square(n_out, KC - 1)
            variance(n_out, ps_o)
            dve.wait_ge(S["rstd_ready"], n_out + 1)
            last = l + 1 == LAYERS
            for j in range(KC):
                own(V.scalar_tensor_tensor(o_out[:, j, :], o_out[:, j, :], col("post", KC * l + j), rstd[:, 0, :],
                                           ALU.mult, ALU.mult))
                V.tensor_tensor(x[:, j, :], x[:, j, :], o_out[:, j, :], ALU.add)\
                    .then_inc(S["x_final" if last else "x_new"], 1)
                if not last and j:
                    add_square(n_out + 1, j - 1)
            if not last:
                add_square(n_out + 1, KC - 1)
                variance(n_out + 1, ps_o)
                dve.wait_ge(S["rstd_ready"], n_out + 2)
                make_u(3 + l, lambda k: col("pre", KC * (l + 1) + k), rstd[:, 0, :], None)


BR_UNITS = [("a", 0), ("a", 1), ("b", 0), ("c", 0), ("a", 2), ("a", 3), ("b", 1), ("c", 1)]
VT_AT = {1 + h: 12 + 3 * h for h in range(NH)} | {5: 26, 6: 29}
UV_AT = {27 + 3 * h: h for h in range(NH)}
kv_norm_step = 8
SQ_BASE = {1: 0, 2: KC, 3: 2 * KC, 4: 3 * KC, 5: 4 * KC}
ZU = [0, 16]
TWO_PI_PARTS = []
_rest = 2 * math.pi
for _bits in (8, 11, 24):
    _q = 2.0 ** (math.floor(math.log2(_rest)) + 1 - _bits)
    TWO_PI_PARTS.append(math.floor(_rest / _q) * _q)
    _rest -= TWO_PI_PARTS[-1]
PI_BELOW = float(np.nextafter(np.float32(math.pi), np.float32(0)))


def _units(w, order=None):
    n = w.shape[1] // P
    return w.reshape(KC, P, n, P).transpose(2, 1, 0, 3).reshape(n, P, KC * P)


def _columns(v):
    return v.reshape(-1, P).T


def _stream(w_in, w_br_a, w_br_b, w_br_c, w_o, w_ff1, w_ff2, w_in_2, w_out_2):
    at = np.cumsum([0, 512, 512, 512, 512, 128, 256, 32, 8, 256, 256, 256, 3072])
    aq, ak, av, bq, bkv, biq, bik, biw, cq, ck, cv, gate = [w_in[:, a:b] for a, b in zip(at[:-1], at[1:])]
    parts = [_units(np.pad(biw, ((0, 0), (0, P - 8)))), _units(biq), _units(np.concatenate([bik] * 4, axis=1)),
             _units(bkv), _units(bq)]
    for h in range(NH):
        parts += [_units(m[:, h * P:(h + 1) * P]) for m in (aq, ak, av)]
    for j in range(2):
        parts += [_units(m[:, j * P:(j + 1) * P]) for m in (cq, ck, cv)]
    parts.append(_units(gate))
    for kind, q in BR_UNITS:
        w = {"a": w_br_a, "b": w_br_b, "c": w_br_c}[kind]
        k = w.shape[0] // P
        n = KC // k
        w = w[:, q * n * P:(q + 1) * n * P].reshape(k, P, n, P)
        parts.append(w.transpose(1, 2, 0, 3).reshape(1, P, KC * P))
    parts += [_units(w_o), _units(w_ff1)]
    f = [_units(w_ff2[q * D:(q + 1) * D]) for q in range(4)]
    parts.append(np.stack(f, axis=1).reshape(4 * KC, P, KC * P))
    for l in range(LAYERS):
        m = _units(w_in_2[l]).reshape(8, KC, P, KC * P)
        c_b, c_c, c_x, c_z, r_q, r_k, r_v, r_z = m
        heads = [(r_q, 0), (r_k, 0), (r_v, 0), (r_q, 1), (r_k, 1), (r_v, 1), (r_z, 0), (r_z, 1)]
        for h in range(0, RH, 2):
            parts.append(np.stack([w[h + e] for w, e in heads]))
        for j in range(KC):
            parts.append(np.stack([c_c[j], c_x[j], c_b[j], c_z[j]]))
        conv, ret = _units(w_out_2[l][:D]), _units(w_out_2[l][D:])
        parts.append(np.stack([ret, conv], axis=1).reshape(2 * KC, P, KC * P))
    s = np.concatenate(parts)
    assert s.shape[0] == UNITS
    s = np.concatenate([s, np.zeros_like(s[:UNITS % 2])])
    return np.ascontiguousarray(s.reshape(-1, 2, P, KC * P).transpose(0, 2, 1, 3).reshape(-1, P, 2 * KC * P))


def _constants():
    f = np.float32
    dist = T - 1 - np.arange(3 * P)
    n = np.maximum(dist, 0)
    half = N_BUCKETS // 2
    large = half + (np.log(np.maximum(n, 1).astype(f) / f(half)) / f(math.log(MAX_DISTANCE / half))
                    * f(N_BUCKETS - half)).astype(np.int32)
    bucket = np.where(dist < 0, N_BUCKETS, np.where(n < half, n, np.minimum(large, N_BUCKETS - 1)))
    onehot = (bucket[None] == np.arange(N_BUCKETS + 1)[:, None]).astype(f)
    i = np.arange(P)
    cmask = np.concatenate([np.zeros((P, P), f), np.where(i[None] > i[:, None], f(NEG), f(0))], axis=1).astype(f)
    lg = np.log1p(-np.exp2(-5.0 - np.arange(RH)))
    diff = i[None, :] - i[:, None]
    diag = np.where(diff >= 0, np.exp(lg[:, None, None] * np.maximum(diff, 0)), 0.0)
    off = np.exp(lg[:, None, None] * (diff + P))
    dec = (np.concatenate([diag, off, diag], axis=2) * P ** -0.5).transpose(1, 0, 2).astype(f)
    freq = (f(1.0) / f(10000.0) ** (np.arange(HD, dtype=f) / f(HD))).astype(f)
    freq = np.concatenate([freq, freq])
    sign = np.where(i < HD, f(1), f(-1))
    return dict(onehot=onehot, ident=np.eye(P, dtype=f), cmask=cmask, decay=np.ascontiguousarray(dec),
                freq=np.stack([freq, freq * sign], axis=1))


def kernel(**inp):
    import concourse.bacc as bacc
    from concourse.bass_utils import run_bass_kernel_spmd

    a = {k: np.asarray(v) for k, v in inp.items()}
    k = _constants()
    vec = [_columns(a["c"][0]), _columns(a["ada_b"][0]), _columns(a["norm_mix"][0]), _columns(a["gate_b"][0]),
           _columns(a["diff_subln"][0]), _columns(a["dsa_kv_norm"][0]), _columns(a["norm_mlp"][0]),
           _columns(a["norm_final"]), _columns(a["pre_norm_2"].reshape(-1)), _columns(a["post_norm_2"].reshape(-1)),
           _columns(a["conv_w_2"].reshape(-1)), k["freq"]]
    arrays = {
        "xT": a["x"][0].T.reshape(KC, P, T).transpose(1, 0, 2),
        "weights": _stream(a["w_in"][0], a["w_br_a"][0], a["w_br_b"][0], a["w_br_c"][0], a["w_o"][0], a["w_ff1"][0],
                           a["w_ff2"][0], a["w_in_2"], a["w_out_2"]),
        "ada": a["ada_w"][0].reshape(KC // 2, 2, P, 6, D).transpose(3, 0, 2, 1, 4).reshape(24, P, 2 * D),
        "cols": np.concatenate(vec, axis=1),
        "dl": a["diff_lambda"][0].reshape(1, -1),
        "relb": np.concatenate([a["rel_bias"], np.full((1, 12), NEG, np.float32)]),
        "onehot": k["onehot"], "ident_d": k["ident"], "flip_d": k["ident"][::-1], "cmask_d": k["cmask"], "decay": k["decay"],
        "positions": a["positions_2"].astype(np.int32),
        "w_uv": a["dsa_w_uv"][0].transpose(1, 0, 2),
    }
    arrays = {n: np.ascontiguousarray(v) for n, v in arrays.items()}
    nc = bacc.Bacc("TRN2", target_bir_lowering=False, num_devices=1)
    aps = {n: nc.dram_tensor(n, v.shape, mybir.dt.from_np(v.dtype), kind="ExternalInput").ap()
           for n, v in arrays.items()}
    out = nc.dram_tensor("out", (P, KC, T), F32, kind="ExternalOutput").ap()
    build(nc, out=out, **aps)
    res = run_bass_kernel_spmd(nc, [arrays], core_ids=[0]).results[0]["out"]
    return res.transpose(1, 0, 2).reshape(D, T).T.reshape(1, T, D)
```

```python
import math
from contextlib import ExitStack

import numpy as np

import concourse.bass as bass
from concourse import mybir

F32 = mybir.dt.float32
F32R = mybir.dt.float32r
I32 = mybir.dt.int32
ALU = mybir.AluOpType
ACT = mybir.ActivationFunctionType
AX = mybir.AxisListType

P = 128
D = 1024
T = 256
KC = D // P
QT = T // P
HD = 64
NH = 4
LAYERS = 2
RH = 8
TOPK = 64
EPS = 1e-6
NEG = -1.0e30
TAKEN = -3.0e38
N_BUCKETS = 32
MAX_DISTANCE = 128
LAM_INIT = 0.8 - 0.6 * math.exp(0.0)

U_QKV = 0
N_QKV = 27
N_GATE = 24
U_BR = N_QKV + N_GATE
U_WO = U_BR + 8
U_F1 = U_WO + 8
U_F2 = U_F1 + 32
U_LAYER = U_F2 + 32
LAYER_UNITS = 80
UNITS = U_LAYER + LAYERS * LAYER_UNITS
O_BR = U_BR
O_WO = O_BR + 24
O_F1 = O_WO + 8
O_F2 = O_F1 + 32
O_LAYER = O_F2 + 8
LAYER_OUTS = 72
SLOTS = 4
RAW_PAIRS = 4

C_IW, C_IQ, C_IK, C_KV, C_BQ = 0, 1, 3, 4, 5
C_A = 9
C_C = 21

COLS = {}
_at = 0
for _name, _n in (("c", 8), ("ada_b", 48), ("norm_mix", 8), ("gate_b", 24), ("subln", 1), ("kv_norm", 1),
                  ("norm_mlp", 8), ("norm_final", 8), ("pre", 16), ("post", 16), ("conv", 48), ("freq", 2)):
    COLS[_name] = _at
    _at += _n
N_COLS = _at


def lin(g, per, const):
    return const if g is None else g * per + const


class Chain:

    def __init__(self, eng, sem):
        self.eng, self.sem, self.n, self.g, self.per, self.start = eng, sem, 0, None, 0, 0

    def __call__(self, ins):
        self.n += 1
        ins.then_inc(self.sem, 1)
        self.eng.wait_ge(self.sem, lin(self.g, self.per, self.n))

    def enter(self, g, per):
        self.g, self.per, self.start = g, per, self.n

    def leave(self, turns):
        assert self.n - self.start == self.per, (self.n - self.start, self.per)
        self.n = self.start + turns * self.per
        self.g = None


def build(nc, xT, weights, ada, cols, dl, relb, onehot, ident_d, flip_d, cmask_d, decay, positions, w_uv, out):
    with ExitStack() as ctx:
        _build(nc, ctx, xT, weights, ada, cols, dl, relb, onehot, ident_d, flip_d, cmask_d, decay, positions, w_uv, out)


def _build(nc, ctx, xT, weights, ada, cols, dl, relb, onehot, ident_d, flip_d, cmask_d, decay, positions, w_uv, out):
    def tile_in(stack, name, shape, dt=F32):
        return stack.enter_context(nc.sbuf_tensor(name, shape, dt))

    def keep(name, shape, dt=F32):
        return tile_in(ctx, name, shape, dt)

    def sem(name):
        return ctx.enter_context(nc.semaphore(name))

    x = keep("x", [P, KC, T])
    with ExitStack() as early:
        bias_rev = tile_in(early, "bias_rev", [P, 12, T])
    u_hi = keep("u_hi", [P, KC, T], F32R)
    u_lo = keep("u_lo", [P, KC, T], F32R)
    raw = keep("raw", [P, RAW_PAIRS, 2 * KC * P])
    w_hi = keep("w_hi", [P, SLOTS, KC * P], F32R)
    w_lo = keep("w_lo", [P, SLOTS, KC * P], F32R)
    vec = keep("vec", [P, N_COLS])
    mod = keep("mod", [P, 6, KC])
    ident = keep("ident", [P, P])
    ones = keep("ones", [P, P])
    flip = keep("flip", [P, P])
    cosT = keep("cosT", [P, T])
    sinT = keep("sinT", [P, T])
    a_mix = keep("a_mix", [P, 2, KC])
    half_gb = keep("half_gb", [P, 24])
    subln = keep("subln", [P, 1])
    cond = keep("cond", [P, KC])
    lam = keep("lam", [P, 8])
    t_u = keep("t_u", [P, 2, T])
    var = keep("var", [P, 2, T])
    rstd = keep("rstd", [P, 2, T])

    with ExitStack() as early:
        prob = tile_in(early, "prob", [P, 4, 3 * P])
    sq = keep("sq", [P, 2, 2, T])
    acc = keep("acc", [P, 2, T])
    ph1 = ExitStack()
    p1 = lambda name, shape, dt=F32: tile_in(ph1, name, shape, dt)
    ada_raw = p1("ada_raw", [P, 2, 2 * D])
    ada_acc = p1("ada_acc", [P, D])
    v_tok = p1("v_tok", [P, NH, QT, P])
    cv_tok = p1("cv_tok", [P, 2, QT, P])
    stA = ExitStack()
    pA = lambda name, shape, dt=F32: tile_in(stA, name, shape, dt)
    iwf = pA("iwf", [8, T])
    iw = pA("iw", [P, QT, 8])
    iqT = pA("iqT", [P, 2, T])
    ikT = pA("ikT", [P, T])
    relu_s = pA("relu_s", [P, 2, 2 * T])
    kvf = pA("kvf", [P, T])
    kv_sq = pA("kv_sq", [P, T])
    stA.close()
    gates = p1("gates", [P, 24, T])
    wuv = p1("wuv", [P, NH, HD])
    kvT = p1("kvT", [P, T])
    kv_tok = p1("kv_tok", [P, QT, P])
    o_mid = p1("o_mid", [P, T])
    bqT = p1("bqT", [P, NH, T])
    ob_hi = p1("ob_hi", [P, 2, T], F32R)
    ob_lo = p1("ob_lo", [P, 2, T], F32R)
    oc_hi = p1("oc_hi", [P, 2, T], F32R)
    oc_lo = p1("oc_lo", [P, 2, T], F32R)
    stB = ExitStack()
    pB = lambda name, shape, dt=F32: tile_in(stB, name, shape, dt)
    bias = pB("bias", [P, 12, T])
    with ExitStack() as early:
        x_sq = tile_in(early, "x_sq", [P, KC, T])
    aqT = pB("aqT", [P, 2, T])
    akT = pB("akT", [P, 2, T])
    cqT = pB("cqT", [P, 2, T])
    ckT = pB("ckT", [P, 2, T])
    vf = pB("vf", [P, 2, T])
    score = pB("score", [P, 3 * P])
    top8 = pB("top8", [P, 8])
    o_raw = pB("o_raw", [P, NH, T])
    cmask = pB("cmask", [P, T])
    probT = pB("probT", [P, 2, 3 * P])
    o_var = pB("o_var", [P, NH, T])
    nmax = pB("nmax", [P, 16, 2])
    psum_ = pB("psum_", [P, 16, 2])
    rsum = pB("rsum", [P, 16, 2])
    lnorm = pB("lnorm", [P, 4, 2])
    stB.close()
    stC = ExitStack()
    pC = lambda name, shape, dt=F32: tile_in(stC, name, shape, dt)
    oa_hi = pC("oa_hi", [P, NH, T], F32R)
    oa_lo = pC("oa_lo", [P, NH, T], F32R)
    merged = pC("merged", [P, KC, T])
    part = pC("part", [P, 2, T])
    m_hi = pC("m_hi", [P, KC, T], F32R)
    m_lo = pC("m_lo", [P, KC, T], F32R)
    stC.close()
    ph1.close()

    st0 = ExitStack()
    p0 = lambda name, shape, dt=F32: tile_in(st0, name, shape, dt)
    p0("pad_ada", [P, 5 * D])
    ada_more = p0("ada_more", [P, 2, 2 * D])
    dlb = p0("dlb", [P, 4 * HD])
    dlp = p0("dlp", [P, 2 * HD])
    relb_s = p0("relb_s", [N_BUCKETS + 1, 12])
    hot = p0("hot", [N_BUCKETS + 1, 3 * P])
    tab_s = p0("tab_s", [12, 3 * P])
    pos_i = p0("pos_i", [P, T], I32)
    pos_f = p0("pos_f", [P, T])
    ang = p0("ang", [P, 2, T])
    turns = p0("turns", [P, 2, T])
    st0.close()

    ph2 = ExitStack()
    p2 = lambda name, shape, dt=F32: tile_in(ph2, name, shape, dt)
    pad3 = p2("pad3", [P, 5, D])
    h_hi = p2("h_hi", [P, 32, T], F32R)
    h_lo = p2("h_lo", [P, 32, T], F32R)
    relu_h = p2("relu_h", [P, 2, T])
    h_full = p2("h_full", [P, 2, T])
    ph2.close()

    ph3 = ExitStack()
    p3 = lambda name, shape, dt=F32: tile_in(ph3, name, shape, dt)
    dec = p3("dec", [P, RH, 3 * P])
    mix_hi = p3("mix_hi", [P, 2 * KC, T], F32R)
    mix_lo = p3("mix_lo", [P, 2 * KC, T], F32R)
    ret = p3("ret", [P, RH, T])
    ret_sq = p3("ret_sq", [P, RH, T])
    zsil = p3("zsil", [P, RH, T])
    qr = p3("qr", [P, 2, T])
    kr = p3("kr", [P, 2, T])
    rt1 = p3("rt1", [P, T])
    rv = p3("rv", [P, 2, T])
    rt2 = p3("rt2", [P, T])
    vfr = p3("vfr", [P, 2, T])
    vtr = p3("vtr", [P, 2, QT, P])
    sdec = p3("sdec", [P, 2, 3 * P])
    th = p3("th", [P, 2, T])
    th_c = p3("th_c", [P, 2, T])
    cc = p3("cc", [P, 2, T])
    cv = p3("cv", [P, 2, T + 2])
    cy = p3("cy", [P, 2, T])
    o_out = p3("o_out", [P, KC, T])
    ph3.close()

    tab_d = nc.dram_tensor("tab_scratch", [12, 3 * P], F32, kind="Internal").ap()

    mm = [ctx.enter_context(nc.psum_tensor(f"mm{i}", [P, 512], F32)) for i in range(4)]
    ps_s = [ctx.enter_context(nc.psum_tensor(f"ps_s{i}", [P, 512], F32)) for i in range(2)]
    ps_t = ctx.enter_context(nc.psum_tensor("ps_t", [P, 512], F32))
    ps_o = ctx.enter_context(nc.psum_tensor("ps_o", [P, 512], F32))

    names = """raw_in0 raw_in1 raw_in2 raw_in3 small_in x_in tab_out bias_in flip_done bias_ready decay_in stored
        hi_ready lo_pool lo_dve unit_done part_done taken0 taken1 taken2 taken3
        ada_in0 ada_in1 ada_in2 ada_in3 mod_done mod_ready
        ones_ready act_own dve_own start_act start_dve tab_done tab_evac
        x_squared stat_done var_ready rstd_ready t_ready uhi_ready ulo_ready
        iw_tr iw_ready idx_done relu_ready idx_used kv_squared kv_stat kv_var kv_rstd kvT_ready kv_tr kv_tok_ready
        s_done s_taken max_ready exp_ready p_ready t_done pt_ready o_done o_taken vt_done vt_ready
        uv_done uv_taken osq_ready ostat_done ovar_ready orstd_ready ofin_ready oah_ready oal_ready
        obh_ready
        m_ready mh_ready ml_ready sq_ready 
        hh_ready hl_ready x_final
        rot_ready rv_tr rv_ready rs_done rs_taken ro_done ret_taken retsq_ready th_ready
        rstat_done rvar_ready rrstd_ready yr_ready yrh_ready mixr_ready yc_ready ych_ready mixc_ready
        start_in ada_used och_ready sq_used rms2_ready rstd2_ready x_new""".split()
    S = {n: sem(n) for n in names}
    raw_in = [S[f"raw_in{i}"] for i in range(RAW_PAIRS)]
    taken = [S[f"taken{i}"] for i in range(4)]
    ada_in = [S[f"ada_in{i}"] for i in range(4)]

    def col(name, i=0):
        return vec[:, COLS[name] + i:COLS[name] + i + 1]

    maps = []
    for h in range(NH):
        for m in range(2):
            maps.append(("a", h, m))
    maps += [("b", h, 0) for h in range(NH)] + [("c", h, 0) for h in range(NH)]
    heads = [("a", h) for h in range(NH)] + [("b", h) for h in range(NH)] + [("c", h) for h in range(NH)]
    maps_of = {r: [i for i, m in enumerate(maps) if m[:2] == heads[r]] for r in range(12)}
    s_at = {12 + 3 * r: r for r in range(12)}
    exp_at = {c + 1: r for c, r in s_at.items()}
    norm_at = {c + 2: r for c, r in s_at.items()}
    t_at = {c + 3: r for c, r in s_at.items()}
    o_at = {c + 4: r for c, r in s_at.items()}
    SUB_AT = {17 + 3 * h: h for h in range(NH)}
    UV_AT = {29 + 3 * h: h for h in range(NH)}
    VT_AT = {13 + 3 * h: 1 + h for h in range(NH)} | {25: 5, 28: 6}
    ADA_AT = 26
    MOD_AT = {ADA_AT + KC * (m - 1): m for m in (2, 3, 4)}
    ROOT_AT, FIN_AT, OAH_AT, OAL_AT = 30, 31, 35, 37

    block = ctx.enter_context(nc.Block())

    def ada_slot(n):
        if n < 8:
            return (ada_raw if n % 4 < 2 else ada_more)[:, n % 2, :], n % 4, n // 4 + 1
        return ada_raw[:, n % 2, :], n % 2, n // 2 - 1

    def ada_load(eng, n):
        dst, q, _ = ada_slot(n)
        if n >= 4:
            eng.wait_ge(S["ada_used"], 2 * n - (6 if n < 8 else 2))
        eng.dma_start(dst, ada[n]).then_inc(ada_in[q], 16)

    @block.sync
    def _(sp):
        sp.dma_start(vec[:, :], cols).then_inc(S["small_in"], 16)
        sp.dma_start(x[:, :, :], xT).then_inc(S["x_in"], 16)

        def load(g, p):
            src = weights[p] if g is None else weights[bass.ds(g * 4 + p, 1)].rearrange("o p n -> p (o n)")
            if p >= RAW_PAIRS:
                n = 2 * p - 2 * RAW_PAIRS + 2
                sp.wait_ge(S["lo_pool"], lin(g, 8, n))
                if n % 4 == 0:
                    sp.wait_ge(S["lo_dve"], lin(g, 8, n))
            both = 2 * p + 1 < UNITS
            width = (2 if both else 1) * KC * P
            sp.dma_start(raw[:, p % RAW_PAIRS, 0:width], src[:, 0:width]).then_inc(raw_in[p % RAW_PAIRS], 16)

        for n in range(8):
            ada_load(sp, n)
        for p in range(4):
            load(None, p)
        n_loops = (UNITS // 2 - 4) // 4
        with sp.Fori(0, n_loops) as g:
            for i in range(4):
                load(g, 4 + i)
        for p in range(4 + 4 * n_loops, (UNITS + 1) // 2):
            load(None, p)
        for half in range(2):
            sp.wait_ge(S["x_final"], 4 * half + 4)
            sp.dma_start(out[:, 4 * half:4 * half + 4, :], x[:, 4 * half:4 * half + 4, :]).then_inc(S["stored"], 16)
        sp.wait_ge(S["stored"], 32)

    @block.gpsimd
    def _(pool):
        def low(g, c):
            if c % 4 == 3:
                return
            pool.wait_ge(S["hi_ready"], lin(g, 8, c + 1))
            if c >= SLOTS:
                pool.wait_ge(S["unit_done"], lin(g, 8, c - SLOTS + 1))
            r = raw[:, (c // 2) % RAW_PAIRS, (c % 2) * KC * P:(c % 2 + 1) * KC * P]
            s = c % SLOTS
            nc.gpsimd.tensor_tensor(w_lo[:, s, :], r, w_hi[:, s, :].bitcast(F32), ALU.subtract)\
                .then_inc(S["lo_pool"], 2 if c % 4 == 2 else 1)

        nc.gpsimd.memset(ones[:, :], 1.0).then_inc(S["ones_ready"], 1)
        for c in range(8):
            low(None, c)
        with pool.Fori(0, UNITS // 8 - 1) as g:
            for i in range(8):
                low(g, 8 + i)
        for c in range(UNITS // 8 * 8, UNITS):
            low(None, c)

    @block.tensor
    def _(pe):
        def unit(g, c, o, rhs_hi, rhs_lo, ready=None, parts=1, first=True, last=True, turn=(8, 2)):
            s = c % SLOTS
            per_c, per_o = turn
            pe.wait_ge(S["hi_ready"], lin(g, per_c, c + 1))
            pe.wait_ge(S["lo_dve" if c % 4 == 3 else "lo_pool"], lin(g, per_c, c + 1))
            per = KC // parts
            for q in range(parts):
                oo = o + q
                if first and oo >= 4:
                    pe.wait_ge(taken[oo % 4], lin(g, per_o, oo // 4))
                for k in range(per):
                    t = q * per + k
                    if ready is not None:
                        ready(k, t)
                    dst = mm[oo % 4][:, 0:T]
                    wh = w_hi[:, s, t * P:(t + 1) * P]
                    wl = w_lo[:, s, t * P:(t + 1) * P]
                    a, b = (first and k == 0), (last and k == per - 1)
                    nc.tensor.matmul(dst, wh, rhs_hi(k), start=a, stop=False)
                    nc.tensor.matmul(dst, wh, rhs_lo(k), start=False, stop=False)
                    i = nc.tensor.matmul(dst, wl, rhs_hi(k), start=False, stop=b)
                i.then_inc(S["unit_done"] if q == parts - 1 else S["part_done"], 1)


        def one_at_a_time(first, value):
            last = [first, value]

            def wait(name, count):
                pe.wait_ge(S[last[0]], last[1])
                last[:] = name, count
            return wait

        t_wait = one_at_a_time("tab_evac", 1)
        o_wait = one_at_a_time("var_ready", 1)

        pe.wait_ge(S["start_in"], 8 * 16)
        nc.tensor.matmul(ps_t[0:12, 0:3 * P], relb_s[:, :], hot[:, :], start=True, stop=True)\
            .then_inc(S["tab_done"], 1)
        pe.wait_ge(S["ones_ready"], 1)
        pe.wait_ge(S["x_squared"], 1)
        for k in range(KC):
            i = nc.tensor.matmul(ps_o[:, 0:T], ones[:, :], x_sq[:, k, :], start=k == 0, stop=k == KC - 1)
        i.then_inc(S["stat_done"], 1)

        def mod_columns(m, n):
            pe.wait_ge(S["ada_used"], KC * (n + 1))
            t_wait("mod_ready", n + 1)
            for j in range(KC):
                i = nc.tensor.matmul(ps_t[:, 496 + j:497 + j], ada_acc[:, j * P:(j + 1) * P], ones[:, 0:1],
                                     start=True, stop=True)
            i.then_inc(S["mod_done"], 1)

        for n in range(6):
            if n == 0:
                pe.wait_ge(S["bias_in"], 16)
            if n >= 2:
                pe.wait_ge(S["bias_ready"], n - 1)
            nc.tensor.matmul(ps_s[n % 2][:, :], flip[:, :], bias_rev[:, 2 * n:2 * n + 2, :], start=True, stop=True)\
                .then_inc(S["flip_done"], 1)
        mod_columns(0, 0)
        mod_columns(1, 1)

        def iw_transpose():
            pe.wait_ge(taken[C_IW % 4], 1)
            t_wait("iw_ready", 1)
            for t in range(QT):
                i = nc.tensor.transpose(ps_t[:, 8 * t:8 * t + 8], iwf[:, t * P:(t + 1) * P], ident[0:8, 0:8])
            i.then_inc(S["iw_tr"], 1)

        def index_scores(n):
            t, hh = n // 4, n % 4
            if n == 0:
                for c in (C_IQ, C_IQ + 1, C_IK):
                    pe.wait_ge(taken[c % 4], c // 4 + 1)
            if n >= 2:
                pe.wait_ge(S["relu_ready"], n - 1)
            else:
                pe.wait_ge(S["bias_ready"], 6)
            nk = P * (t + 1)
            for half in range(2):
                i = nc.tensor.matmul(ps_s[n % 2][:, half * T:half * T + nk],
                                     iqT[32 * hh:32 * hh + 32, half, t * P:(t + 1) * P],
                                     ikT[32 * hh:32 * hh + 32, 0:nk], start=True, stop=True)
            i.then_inc(S["idx_done"], 1)

        def kv_stat():
            pe.wait_ge(S["kv_squared"], 1)
            o_wait("kv_var", 1)
            nc.tensor.matmul(ps_o[:, 0:T], ones[:, :], kv_sq[:, :], start=True, stop=True)\
                .then_inc(S["kv_stat"], 1)

        def kv_transpose():
            pe.wait_ge(S["kvT_ready"], 1)
            t_wait("kv_tok_ready", 1)
            for t in range(QT):
                i = nc.tensor.transpose(ps_t[:, t * P:(t + 1) * P], kvT[:, t * P:(t + 1) * P], ident[:, :])
            i.then_inc(S["kv_tr"], 1)

        vt_users = [("kv", 0)] + [("a", h) for h in range(NH)] + [("c", j) for j in range(2)]

        def v_transpose(n):
            kind, h = vt_users[n]
            c = C_A + 3 * h + 2 if kind == "a" else C_C + 3 * h + 2
            pe.wait_ge(taken[c % 4], c // 4 + 1)
            t_wait("vt_ready", n)
            for t in range(QT):
                i = nc.tensor.transpose(ps_t[:, t * P:(t + 1) * P], vf[:, n % 2, t * P:(t + 1) * P], ident[:, :])
            i.then_inc(S["vt_done"], 1)

        def q_and_k(r, m):
            kind, h = heads[r]
            if kind == "a":
                return aqT[m * HD:(m + 1) * HD, h % 2, :], akT[m * HD:(m + 1) * HD, h % 2, :]
            if kind == "b":
                return bqT[:, h, :], kvT[:, :]
            j, e = h // 2, h % 2
            return cqT[e * HD:(e + 1) * HD, j, :], ckT[e * HD:(e + 1) * HD, j, :]

        def scores(r):
            kind, h = heads[r]
            last_c = {"a": C_A + 3 * h + 1, "b": C_BQ + h, "c": C_C + 3 * (h // 2) + 1}[kind]
            for c in (last_c - 1, last_c):
                pe.wait_ge(taken[c % 4], c // 4 + 1)
            if r == 0:
                pe.wait_ge(S["relu_ready"], 8)
            for e, m in enumerate(maps_of[r]):
                q, k = q_and_k(r, e)
                if m >= 2:
                    pe.wait_ge(S["s_taken"], m - 1)
                bank = ps_s[m % 2]
                nc.tensor.matmul(bank[:, 0:T], q[:, P:T], k, start=True, stop=True)
                nc.tensor.matmul(bank[:, T:T + P], q[:, 0:P], k[:, 0:P], start=True, stop=True)\
                    .then_inc(S["s_done"], 1)

        def prob_transpose(r):
            pe.wait_ge(S["p_ready"], r + 1)
            t_wait("pt_ready", r + 1)
            pm = prob[:, maps_of[r][-1] % 4, :]
            nc.tensor.transpose(ps_t[:, 0:P], pm[:, T:T + P], ident[:, :])
            nc.tensor.transpose(ps_t[:, P:T], pm[:, 0:P], ident[:, :])
            nc.tensor.transpose(ps_t[:, T:T + P], pm[:, P:T], ident[:, :]).then_inc(S["t_done"], 1)

        def outputs(r):
            kind, h = heads[r]
            pe.wait_ge(S["pt_ready"], r + 1)
            o_wait("o_taken", r + 1)
            pt = probT[:, r % 2, :]
            if kind == "a":
                v, dst = v_tok[:, h, :, :], ps_o[:, 0:T]
            elif kind == "b":
                v, dst = kv_tok[:, :, :], ps_o[:, 0:T]
            else:
                e = h % 2
                v, dst = cv_tok[:, h // 2, :, e * HD:(e + 1) * HD], ps_o[e * HD:(e + 1) * HD, 0:T]
            nc.tensor.matmul(dst, v[:, 0, :], pt[:, 0:T], start=True, stop=False)
            nc.tensor.matmul(dst[:, P:T], v[:, 1, :], pt[:, T:T + P], start=False, stop=True)\
                .then_inc(S["o_done"], 1)

        def up_values(h):
            pe.wait_ge(S["o_taken"], NH + h + 1)
            t_wait("uv_taken", h + 1)
            dst = ps_t[HD * (h % 2):HD * (h % 2) + HD, 0:T]
            nc.tensor.matmul(dst, wuv[:, h, :], o_mid[:, :], start=True, stop=True).then_inc(S["uv_done"], 1)

        def subln_stat(h):
            pe.wait_ge(S["osq_ready"], h + 1)
            o_wait("ovar_ready", h + 1)
            nc.tensor.matmul(ps_o[:, 0:T], ones[:, :], o_var[:, h, :], start=True, stop=True)\
                .then_inc(S["ostat_done"], 1)

        def u_ready(m):
            def wait(k, t):
                pe.wait_ge(S["ulo_ready"], KC * m + k + 1)
            return wait

        uh = lambda k: u_hi[:, k, :]
        ul = lambda k: u_lo[:, k, :]
        for c in range(N_QKV + N_GATE):
            unit(None, c, c, uh, ul, ready=u_ready(0) if c == 0 else None)
            if c == 1:
                iw_transpose()
            if 4 <= c <= 11:
                index_scores(c - 4)
            if c == 5:
                kv_stat()
            if c == 9:
                kv_transpose()
            if c in VT_AT:
                v_transpose(VT_AT[c])
            if c in MOD_AT:
                mod_columns(MOD_AT[c], MOD_AT[c])
            if c in s_at:
                scores(s_at[c])
            if c in o_at:
                outputs(o_at[c])
            if c in t_at:
                prob_transpose(t_at[c])
            if c in UV_AT:
                up_values(UV_AT[c])
            if c in SUB_AT:
                subln_stat(SUB_AT[c])

        o = O_BR
        for n, (kind, q) in enumerate(BR_UNITS):
            src_hi, src_lo = {"a": (oa_hi, oa_lo), "b": (ob_hi, ob_lo), "c": (oc_hi, oc_lo)}[kind]
            if n == 0:
                pe.wait_ge(S["oal_ready"], NH)
            if kind == "b":
                pe.wait_ge(S["uv_taken"], NH)
            if kind == "c":
                pe.wait_ge(S["o_taken"], 12)
            parts = 2 if kind == "a" else 4
            unit(None, U_BR + n, o, lambda k: src_hi[:, k, :], lambda k: src_lo[:, k, :], parts=parts)
            o += parts
        for j in range(KC):
            unit(None, U_WO + j, O_WO + j, lambda k: m_hi[:, k, :], lambda k: m_lo[:, k, :],
                 ready=(lambda k, t: pe.wait_ge(S["ml_ready"], k + 1)) if j == 0 else None)

        def norm_stat(n, two=False):
            pe.wait_ge(S["sq_used"], SQ_BASE[n] + KC)
            o_wait("var_ready", n + 1)
            for e in range(2 if two else 1):
                i = nc.tensor.matmul(ps_o[:, e * T:(e + 1) * T], ones[:, :], acc[:, e, :], start=True, stop=True)
            i.then_inc(S["stat_done"], 1)

        norm_stat(1)
        for i in range(8):
            unit(None, U_F1 + i, O_F1 + i, uh, ul, ready=u_ready(1) if i == 0 else None)
        with pe.Fori(0, 3) as g:
            for i in range(8):
                unit(g, U_F1 + 8 + i, O_F1 + 8 + i, uh, ul)
        mod_columns(5, 5)
        pe.wait_ge(S["hl_ready"], 32)
        with pe.Fori(0, 2) as g:
            for j in range(4):
                for q in range(4):
                    unit(g, U_F2 + 4 * j + q, O_F2 + j, lambda k: h_hi[:, q * KC + k, :],
                         lambda k: h_lo[:, q * KC + k, :], first=q == 0, last=q == 3, turn=(16, 1))
        norm_stat(2, two=True)

        for l in range(LAYERS):
            uA = U_LAYER + LAYER_UNITS * l
            oA = O_LAYER + LAYER_OUTS * l

            def v_tr(g, o, H, h):
                pe.wait_ge(taken[o % 4], lin(g, 2, o // 4 + 1))
                if h + H:
                    pe.wait_ge(S["rv_ready"], lin(g, 2, H + h))
                for t in range(QT):
                    n = nc.tensor.transpose(ps_t[:, t * P:(t + 1) * P], vfr[:, h % 2, t * P:(t + 1) * P], ident[:, :])
                n.then_inc(S["rv_tr"], 1)

            def ret_scores(g, H, h):
                pe.wait_ge(S["rot_ready"], lin(g, 4, 2 * (H + h) + 2))
                if H + h >= 2:
                    pe.wait_ge(S["rs_taken"], lin(g, 2, H + h - 1))
                b = ps_s[h % 2]
                nc.tensor.matmul(b[:, 0:T], kr[:, h % 2, 0:P], qr[:, h % 2, :], start=True, stop=True)
                nc.tensor.matmul(b[:, T:T + P], kr[:, h % 2, P:T], qr[:, h % 2, P:T], start=True, stop=True)\
                    .then_inc(S["rs_done"], 1)

            def ret_out(g, H, h):
                if H + h:
                    if h == 0 and (H + h) >= 4:
                        pe.wait_ge(S["rvar_ready"], lin(g, 1, H // 2 - 1))
                pe.wait_ge(S["rs_taken"], lin(g, 2, H + h + 1))
                pe.wait_ge(S["rv_ready"], lin(g, 2, H + h + 1))
                if H + h:
                    pe.wait_ge(S["ret_taken"], lin(g, 2, H + h))
                nc.tensor.matmul(ps_o[:, 0:T], vtr[:, h % 2, 0, :], sdec[:, h % 2, 0:T], start=True, stop=False)
                nc.tensor.matmul(ps_o[:, P:T], vtr[:, h % 2, 1, :], sdec[:, h % 2, T:T + P], start=False, stop=True)\
                    .then_inc(S["ro_done"], 1)

            def turn(g, n0):
                c0, o0, H = uA + 8 * n0, oA + 8 * n0, RH * l + 2 * n0
                for i in range(8):
                    unit(g, c0 + i, o0 + i, uh, ul, ready=u_ready(2 + l) if n0 + i == 0 else None)
                    if i == 1:
                        v_tr(g, o0, H, 0)
                    if i == 2 and n0:
                        head_stat(g, H // 2 - 1)
                    if i == 3:
                        ret_scores(g, H, 0)
                    if i == 4:
                        v_tr(g, o0 + 3, H, 1)
                    if i == 5:
                        ret_out(g, H, 0)
                    if i == 6:
                        ret_scores(g, H, 1)
                    if i == 7:
                        ret_out(g, H, 1)

            def head_stat(g, n):
                pe.wait_ge(S["retsq_ready"], lin(g, 2, 2 * n + 2))
                if n % 4 == 3:
                    src = ret_sq[:, 6:8, :]
                elif g is None:
                    src = ret_sq[:, 2 * (n % 4):2 * (n % 4) + 2, :]
                else:
                    src = ret_sq[:, bass.ds(g * 2 + 2 * (n % 4), 2), :]
                nc.tensor.matmul(ps_o[:, :], ones[:, :], src, start=True, stop=True).then_inc(S["rstat_done"], 1)

            turn(None, 0)
            with pe.Fori(0, 3) as g:
                turn(g, 1)
            for i in range(8):
                unit(None, uA + 32 + i, oA + 32 + i, uh, ul)
                if i == 0:
                    head_stat(None, 4 * l + 3)
            with pe.Fori(0, 3) as g:
                for i in range(8):
                    unit(g, uA + 40 + i, oA + 40 + i, uh, ul)
            for j in range(KC):
                for q in range(2):
                    off = KC if q == 0 else 0
                    rd = None
                    if j == 0:
                        rd = (lambda s: lambda k, t: pe.wait_ge(S[s], KC * l + k + 1))("mixr_ready" if q == 0 else "mixc_ready")
                    unit(None, uA + 64 + 2 * j + q, oA + 64 + j,
                         (lambda off: lambda k: mix_hi[:, off + k, :])(off),
                         (lambda off: lambda k: mix_lo[:, off + k, :])(off), ready=rd, first=q == 0, last=q == 1)
            norm_stat(3 + 2 * l)
            if l + 1 < LAYERS:
                norm_stat(4 + 2 * l)

    @block.scalar
    def _(act):
        own = Chain(act, S["act_own"])
        A = nc.scalar.activation

        def high(g, c):
            if c >= UNITS:
                return
            act.wait_ge(raw_in[(c // 2) % RAW_PAIRS], lin(g, 16, 16 * (c // 2 // RAW_PAIRS + 1)))
            if c >= SLOTS:
                act.wait_ge(S["unit_done"], lin(g, 8, c - SLOTS + 1))
            r = raw[:, (c // 2) % RAW_PAIRS, (c % 2) * KC * P:(c % 2 + 1) * KC * P]
            A(w_hi[:, c % SLOTS, :], r, ACT.Copy).then_inc(S["hi_ready"], 1)

        act.dma_start(relb_s[:, :], relb).then_inc(S["start_in"], 16)
        act.dma_start(hot[:, :], onehot).then_inc(S["start_in"], 16)
        act.dma_start(dlb[:, :], bass.AP(dl.tensor, 0, [[0, P], [1, 4 * HD]])).then_inc(S["start_in"], 16)
        act.dma_start(pos_i[:, :], bass.AP(positions.tensor, 0, [[0, P], [1, T]])).then_inc(S["start_in"], 16)
        act.dma_start(ident[:, :], ident_d).then_inc(S["start_in"], 16)
        act.dma_start(flip[:, :], flip_d).then_inc(S["start_in"], 16)
        act.dma_start(cmask[:, :], cmask_d).then_inc(S["start_in"], 16)
        act.dma_start(wuv[:, :, :], w_uv).then_inc(S["start_in"], 16)
        act.wait_ge(S["small_in"], 16)
        A(cond[:, :], vec[:, COLS["c"]:COLS["c"] + KC], ACT.Exp, scale=-1.0).then_inc(S["start_act"], 1)
        act.wait_ge(S["start_dve"], 2)
        A(lam[:, 2:4], lam[:, 0:2], ACT.Exp).then_inc(S["start_act"], 1)
        act.wait_ge(S["x_in"], 16)
        A(x_sq[:, :, :], x[:, :, :], ACT.Square).then_inc(S["x_squared"], 1)
        act.wait_ge(S["start_dve"], 3)
        A(sinT[:, :], ang[:, 1, :], ACT.Sin).then_inc(S["start_act"], 1)
        A(cosT[:, :], ang[:, 0, :], ACT.Sin, scale=0.5).then_inc(S["start_act"], 1)
        act.wait_ge(S["tab_done"], 1)
        A(tab_s[:, :], ps_t[0:12, 0:3 * P], ACT.Copy).then_inc(S["tab_evac"], 1)
        act.wait_ge(S["tab_evac"], 1)
        act.dma_start(tab_d, tab_s[:, :]).then_inc(S["tab_out"], 16)

        def root(n):
            act.wait_ge(S["var_ready"], n + 1)
            w = 2 if n == 2 else 1
            A(rstd[:, 0:w, :], var[:, 0:w, :], ACT.Sqrt).then_inc(S["rstd_ready"], 1)

        def make_u_hi(m, shift):
            for k in range(KC):
                act.wait_ge(S["t_ready"], KC * m + k + 1)
                if shift is None:
                    A(u_hi[:, k, :], t_u[:, k % 2, :], ACT.Copy).then_inc(S["uhi_ready"], 1)
                else:
                    A(u_hi[:, k, :], t_u[:, k % 2, :], ACT.Identity, bias=mod[:, shift, k:k + 1])\
                        .then_inc(S["uhi_ready"], 1)

        act.wait_ge(S["tab_out"], 16)
        act.dma_start(bias_rev[:, :, :], bass.AP(tab_d.tensor, 0, [[1, P], [3 * P, 12], [1, T]]))\
            .then_inc(S["bias_in"], 16)
        root(0)
        for n in range(6):
            act.wait_ge(S["flip_done"], n + 1)
            A(bias[:, 2 * n:2 * n + 2, :], ps_s[n % 2][:, :].rearrange("p (h k) -> p h k", h=2), ACT.Copy)\
                .then_inc(S["bias_ready"], 1)
        for c in range(SLOTS):
            high(None, c)
        ada_load(act, 8)
        ada_load(act, 9)
        make_u_hi(0, 0)

        def take(c, dst, w=P):
            A(dst, mm[c % 4][0:w, 0:T], ACT.Copy).then_inc(taken[c % 4], 1)

        def qkv_evac(c):
            if c == C_IW:
                take(c, iwf[:, :], 8)
            elif c < C_IK:
                take(c, iqT[:, c - C_IQ, :])
            elif c == C_IK:
                take(c, ikT[:, :])
            elif c == C_KV:
                take(c, kvf[:, :])
                act.wait_ge(taken[c % 4], c // 4 + 1)
                A(kv_sq[:, :], kvf[:, :], ACT.Square).then_inc(S["kv_squared"], 1)
            elif c < C_A:
                take(c, bqT[:, c - C_BQ, :])
            elif c < C_C:
                h, e = (c - C_A) // 3, (c - C_A) % 3
                if e < 2 and h >= 2:
                    act.wait_ge(S["s_done"], 2 * (h - 2) + 2)
                if e == 2:
                    n = 1 + h
                    if n >= 3:
                        act.wait_ge(S["vt_done"], n - 2)
                    take(c, vf[:, n % 2, :])
                else:
                    take(c, (aqT, akT)[e][:, h % 2, :])
            else:
                j, e = (c - C_C) // 3, (c - C_C) % 3
                if e == 2:
                    n = 1 + NH + j
                    act.wait_ge(S["vt_done"], n - 2)
                    take(c, vf[:, n % 2, :])
                else:
                    take(c, (cqT, ckT)[e][:, j, :])

        def act_iw():
            act.wait_ge(S["iw_tr"], 1)
            A(iw[:, :, :], ps_t[:, 0:16], ACT.Copy).then_inc(S["iw_ready"], 1)

        def act_relu(n):
            t = n // 4
            act.wait_ge(S["idx_done"], n + 1)
            if n >= 2:
                act.wait_ge(S["idx_used"], n - 1)
            nk = P * (t + 1)
            src = ps_s[n % 2][:, :].rearrange("p (e k) -> p e k", e=2)[:, :, 0:nk]
            dst = relu_s[:, n % 2, :].rearrange("p (e k) -> p e k", e=2)[:, :, 0:nk]
            A(dst, src, ACT.Relu).then_inc(S["relu_ready"], 1)

        def act_kv_tok():
            act.wait_ge(S["kv_tr"], 1)
            A(kv_tok[:, :, :], ps_t[:, 0:T], ACT.Copy).then_inc(S["kv_tok_ready"], 1)

        def act_vt(n):
            kind, h = ("a", n - 1) if n <= NH else ("c", n - 1 - NH)
            act.wait_ge(S["vt_done"], n)
            A(v_tok[:, h, :, :] if kind == "a" else cv_tok[:, h, :, :], ps_t[:, 0:T], ACT.Copy)\
                .then_inc(S["vt_ready"], 1)

        def act_exp(m):
            act.wait_ge(S["max_ready"], m + 1)
            p = prob[:, m % 4, :]
            own(A(p[:, 0:T], p[:, 0:T], ACT.Exp, bias=nmax[:, m, 0:1], accum_out=psum_[:, m, 0:1]))
            A(p[:, T:T + P], p[:, T:T + P], ACT.Exp, bias=nmax[:, m, 1:2], accum_out=psum_[:, m, 1:2])\
                .then_inc(S["exp_ready"], 1)

        def act_pt(r):
            act.wait_ge(S["t_done"], r + 1)
            if r >= 2:
                act.wait_ge(S["o_done"], r - 1)
            A(probT[:, r % 2, :], ps_t[:, 0:3 * P], ACT.Copy).then_inc(S["pt_ready"], 1)

        def act_o(r):
            kind, h = heads[r]
            act.wait_ge(S["o_done"], r + 1)
            if kind == "a":
                A(o_raw[:, h, :], ps_o[:, 0:T], ACT.Copy).then_inc(S["o_taken"], 1)
                act.wait_ge(S["o_taken"], r + 1)
                A(o_var[:, h, :], o_raw[:, h, :], ACT.Square).then_inc(S["osq_ready"], 1)
            elif kind == "b":
                if h:
                    act.wait_ge(S["uv_done"], h)
                A(o_mid[:, :], ps_o[:, 0:T], ACT.Copy).then_inc(S["o_taken"], 1)
            else:
                e = h % 2
                A(oc_hi[e * HD:(e + 1) * HD, h // 2, :], ps_o[e * HD:(e + 1) * HD, 0:T], ACT.Copy)\
                    .then_inc(S["och_ready"], 1)

        def act_uv(h):
            e = h % 2
            act.wait_ge(S["uv_done"], h + 1)
            A(ob_hi[e * HD:(e + 1) * HD, h // 2, :], ps_t[e * HD:(e + 1) * HD, 0:T], ACT.Copy)\
                .then_inc(S["obh_ready"], 1)

        def act_gate(c):
            j = c - N_QKV
            A(gates[:, j, :], mm[c % 4][:, 0:T], ACT.Tanh, scale=0.5, bias=half_gb[:, j:j + 1])\
                .then_inc(taken[c % 4], 1)

        for c in range(N_QKV + N_GATE):
            act.wait_ge(S["unit_done"], c + 1)
            (qkv_evac if c < N_QKV else act_gate)(c)
            high(None, c + SLOTS)
            if c % 2 == 0 and 10 <= (c - 8) // 2 < 20:
                ada_load(act, (c - 8) // 2)
            if c == 1:
                act_iw()
            if 4 <= c <= 11:
                act_relu(c - 4)
            if c == 6:
                act.wait_ge(S["kv_var"], 1)
                A(rstd[:, 1, :], var[:, 1, :], ACT.Sqrt).then_inc(S["kv_rstd"], 1)
            if c == 9:
                act_kv_tok()
            if c in exp_at:
                for m in maps_of[exp_at[c]]:
                    act_exp(m)
            if c in VT_AT:
                act_vt(VT_AT[c])
            if c in o_at:
                act_o(o_at[c])
            if c in t_at:
                act_pt(t_at[c])
            if c in UV_AT:
                act_uv(UV_AT[c])
            if c == ROOT_AT:
                act.wait_ge(S["ovar_ready"], NH)
                A(o_var[:, :, :], o_var[:, :, :], ACT.Sqrt).then_inc(S["orstd_ready"], 1)
            if OAH_AT <= c < OAH_AT + NH:
                h = c - OAH_AT
                act.wait_ge(S["ofin_ready"], h + 1)
                A(oa_hi[:, h, :], o_raw[:, h, :], ACT.Copy).then_inc(S["oah_ready"], 1)

        for n, (kind, q) in enumerate(BR_UNITS):
            act.wait_ge(S["unit_done"], U_BR + n + 1)
            high(None, U_BR + n + SLOTS)
            if kind == "c":
                for j in range(4 * q, 4 * q + 4):
                    act.wait_ge(S["m_ready"], j + 1)
                    A(m_hi[:, j, :], merged[:, j, :], ACT.Copy, scale=0.5).then_inc(S["mh_ready"], 1)

        def square_x(n, j, src, scale=None):
            k = SQ_BASE[n] + j
            if k >= 2:
                act.wait_ge(S["sq_used"], k - 1)
            if scale is None:
                A(sq[:, k % 2, 0, :], src, ACT.Square).then_inc(S["sq_ready"], 1)
            else:
                own(A(sq[:, k % 2, 0, :], src, ACT.Square))
                A(sq[:, k % 2, 1, :], src, ACT.Square, scale=scale).then_inc(S["sq_ready"], 1)

        for j in range(KC):
            o = O_WO + j
            act.wait_ge(S["unit_done"], U_WO + j + 1)
            high(None, U_WO + j + SLOTS)
            act.wait_ge(taken[o % 4], o // 4 + 1)
            square_x(1, j, x[:, j, :])
        root(1)
        make_u_hi(1, 3)

        def up_turn(g, base):
            for i in range(8):
                c, o, f = U_F1 + base + i, O_F1 + base + i, base + i
                act.wait_ge(S["unit_done"], lin(g, 8, c + 1))
                if f >= 2:
                    act.wait_ge(S["hl_ready"], lin(g, 8, f - 1))
                A(relu_h[:, f % 2, :], mm[o % 4][:, 0:T], ACT.Relu).then_inc(taken[o % 4], 1)
                high(g, c + SLOTS)
                act.wait_ge(taken[o % 4], lin(g, 2, o // 4 + 1))
                dst = h_hi[:, f, :] if g is None else h_hi[:, bass.ds(g * 8 + f, 1), :][:, 0, :]
                A(dst, relu_h[:, f % 2, :], ACT.Square).then_inc(S["hh_ready"], 1)
                if g is None and i in (2, 4):
                    ada_load(act, 21 + i // 2)

        ada_load(act, 20)
        ada_load(act, 21)
        up_turn(None, 0)
        with act.Fori(0, 3) as g:
            up_turn(g, 8)

        act.wait_ge(S["mod_ready"], 6)
        act.dma_start(dec[:, :, :], decay).then_inc(S["decay_in"], 16)
        for j in range(KC):
            for q in range(4):
                c = U_F2 + 4 * j + q
                act.wait_ge(S["unit_done"], c + 1)
                high(None, c + SLOTS)
            o = O_F2 + j
            act.wait_ge(taken[o % 4], o // 4 + 1)
            square_x(2, j, x[:, j, :], scale=col("norm_final", j))
        root(2)
        act.wait_ge(S["rms2_ready"], 1)
        A(rstd[:, 1, :], var[:, 1, :], ACT.Sqrt).then_inc(S["rstd2_ready"], 1)
        make_u_hi(2, None)

        for l in range(LAYERS):
            uA = U_LAYER + LAYER_UNITS * l
            oA = O_LAYER + LAYER_OUTS * l
            H = RH * l

            def a_turn(g, n0):
                c0, o0, hb = uA + 8 * n0, oA + 8 * n0, H + 2 * n0

                def step(i):
                    act.wait_ge(S["unit_done"], lin(g, 8, c0 + i + 1))

                def v_copy(i, h):
                    if hb + h >= 2:
                        act.wait_ge(S["rv_tr"], lin(g, 2, hb + h - 1))
                    A(vfr[:, h, :], mm[(o0 + i) % 4][:, 0:T], ACT.Copy).then_inc(taken[(o0 + i) % 4], 1)

                def vt_copy(h):
                    act.wait_ge(S["rv_tr"], lin(g, 2, hb + h + 1))
                    if hb + h >= 2:
                        act.wait_ge(S["ro_done"], lin(g, 2, hb + h - 1))
                    A(vtr[:, h, :, :], ps_t[:, 0:T], ACT.Copy).then_inc(S["rv_ready"], 1)

                def z_tanh(i, h):
                    act.wait_ge(taken[(o0 + i) % 4], lin(g, 2, (o0 + i) // 4 - 1))
                    A(th[:, h, :], mm[(o0 + i) % 4][:, 0:T], ACT.Tanh, scale=0.5).then_inc(S["th_ready"], 1)

                def o_copy(h):
                    act.wait_ge(S["ro_done"], lin(g, 2, hb + h + 1))
                    n = 2 * n0 + h
                    dst = ret[:, n, :] if g is None else ret[:, bass.ds(g * 2 + n, 1), :][:, 0, :]
                    ds2 = ret_sq[:, n, :] if g is None else ret_sq[:, bass.ds(g * 2 + n, 1), :][:, 0, :]
                    A(dst, ps_o[:, 0:T], ACT.Copy).then_inc(S["ret_taken"], 1)
                    act.wait_ge(S["ret_taken"], lin(g, 2, hb + h + 1))
                    A(ds2, dst, ACT.Square).then_inc(S["retsq_ready"], 1)

                for i in range(8):
                    step(i)
                    if i in (0, 3):
                        v_copy(i, i // 3)
                    if i >= 6:
                        z_tanh(i, i - 6)
                    if i in (1, 4):
                        vt_copy(i // 4)
                    high(g, c0 + i + SLOTS)
                    if i in (5, 7):
                        o_copy(i // 7)

            a_turn(None, 0)
            with act.Fori(0, 3) as g:
                a_turn(g, 1)

            def conv_high(g, n):
                act.wait_ge(S["yc_ready"], lin(g, 2, 8 * l + n + 1))
                dst = mix_hi[:, n, :] if g is None else mix_hi[:, bass.ds(g * 2 + n, 1), :][:, 0, :]
                A(dst, cy[:, n % 2, :], ACT.Copy, scale=0.5).then_inc(S["ych_ready"], 1)

            def b_turn(g, n0):
                c0, o0 = uA + 32 + 8 * n0, oA + 32 + 8 * n0
                for e in range(2):
                    n = 2 * n0 + e
                    for i in range(4):
                        ii = 4 * e + i
                        o = o0 + ii
                        act.wait_ge(S["unit_done"], lin(g, 8, c0 + ii + 1))
                        if i == 0:
                            act.wait_ge(taken[(o + 1) % 4], lin(g, 2, (o + 1) // 4 - 1))
                            A(cc[:, e, :], mm[o % 4][:, 0:T], ACT.Copy).then_inc(taken[o % 4], 1)
                        if i == 3:
                            act.wait_ge(taken[o % 4], lin(g, 2, o // 4 - 1))
                            A(th_c[:, e, :], mm[o % 4][:, 0:T], ACT.Tanh, scale=0.5).then_inc(S["th_ready"], 1)
                        high(g, c0 + ii + SLOTS)
                        if i == 0 and n:
                            conv_high(g, n - 1)
                        if ii == 1 and n0 == 0:
                            act.wait_ge(S["rvar_ready"], 4 * l + 4)
                            A(ret_sq[:, :, :], ret_sq[:, :, :], ACT.Sqrt).then_inc(S["rrstd_ready"], 1)
                        if i == 2:
                            act.wait_ge(S["yr_ready"], lin(g, 2, 8 * l + n + 1))
                            dst = mix_hi[:, KC + n, :] if g is None else mix_hi[:, bass.ds(g * 2 + KC + n, 1), :][:, 0, :]
                            A(dst, qr[:, e, :], ACT.Copy, scale=0.5).then_inc(S["yrh_ready"], 1)

            b_turn(None, 0)
            with act.Fori(0, 3) as g:
                b_turn(g, 1)
            conv_high(None, KC - 1)
            for j in range(KC):
                for q in range(2):
                    c = uA + 64 + 2 * j + q
                    act.wait_ge(S["unit_done"], c + 1)
                    if q == 1:
                        o = oA + 64 + j
                        A(o_out[:, j, :], mm[o % 4][:, 0:T], ACT.Copy).then_inc(taken[o % 4], 1)
                    high(None, c + SLOTS)
                act.wait_ge(taken[o % 4], o // 4 + 1)
                square_x(3 + 2 * l, j, o_out[:, j, :])
            root(3 + 2 * l)
            if l + 1 < LAYERS:
                for j in range(KC):
                    act.wait_ge(S["x_new"], KC * l + j + 1)
                    square_x(4 + 2 * l, j, x[:, j, :])
                root(4 + 2 * l)
                make_u_hi(3 + l, None)

    @block.vector
    def _(dve):
        own = Chain(dve, S["dve_own"])
        V = nc.vector

        def low(g, c):
            if c % 4 != 3 or c >= UNITS:
                return
            dve.wait_ge(S["hi_ready"], lin(g, 8, c + 1))
            if c >= SLOTS:
                dve.wait_ge(S["unit_done"], lin(g, 8, c - SLOTS + 1))
            r = raw[:, (c // 2) % RAW_PAIRS, (c % 2) * KC * P:(c % 2 + 1) * KC * P]
            s = c % SLOTS
            V.tensor_tensor(w_lo[:, s, :], r, w_hi[:, s, :].bitcast(F32), ALU.subtract).then_inc(S["lo_dve"], 4)

        dve.wait_ge(S["start_in"], 8 * 16)
        V.tensor_tensor(dlp[:, 0:HD], dlb[:, 0:HD], dlb[:, HD:2 * HD], ALU.mult).then_inc(S["start_dve"], 1)
        own(V.tensor_tensor(dlp[:, HD:2 * HD], dlb[:, 2 * HD:3 * HD], dlb[:, 3 * HD:4 * HD], ALU.mult))
        V.tensor_reduce(lam[:, 0:2], dlp[:, :].rearrange("p (a d) -> p a d", a=2), AX.X, ALU.add)\
            .then_inc(S["start_dve"], 1)
        dve.wait_ge(S["small_in"], 16)
        own(V.tensor_copy(pos_f[:, :], pos_i[:, :]))
        for e in range(2):
            own(V.tensor_scalar(ang[:, e, :], pos_f[:, :], col("freq", e), None, ALU.mult))
        big = 12582912.0
        own(V.tensor_scalar(turns[:, :, :], ang[:, :, :], 1.0 / (2 * math.pi), big, ALU.mult, ALU.add))
        own(V.tensor_scalar(turns[:, :, :], turns[:, :, :], big, None, ALU.subtract))
        for cst in TWO_PI_PARTS:
            own(V.scalar_tensor_tensor(ang[:, :, :], turns[:, :, :], -cst, ang[:, :, :], ALU.mult, ALU.add))
        V.tensor_scalar(ang[:, :, :], ang[:, :, :], PI_BELOW, -PI_BELOW, ALU.min, ALU.max).then_inc(S["start_dve"], 1)
        dve.wait_ge(S["start_act"], 1)
        own(V.tensor_scalar(cond[:, :], cond[:, :], 1.0, None, ALU.add))
        own(V.reciprocal(cond[:, :], cond[:, :]))
        own(V.tensor_tensor(cond[:, :], cond[:, :], vec[:, COLS["c"]:COLS["c"] + KC], ALU.mult))
        dve.wait_ge(S["start_act"], 2)
        own(V.tensor_tensor(lam[:, 4:5], lam[:, 3:4], lam[:, 2:3], ALU.subtract))
        own(V.tensor_scalar(lam[:, 5:6], lam[:, 4:5], LAM_INIT, None, ALU.subtract))
        own(V.tensor_scalar(half_gb[:, :], vec[:, COLS["gate_b"]:COLS["gate_b"] + 24], 0.5, None, ALU.mult))
        own(V.tensor_scalar(subln[:, :], col("subln"), 1.0 - LAM_INIT, None, ALU.mult))

        def ada_step(a):
            part_, k = a // KC, a % KC
            n = a // 2
            slot, q, seen = ada_slot(n)
            dve.wait_ge(ada_in[q], 16 * seen)
            src = slot[:, (a % 2) * D:(a % 2 + 1) * D]
            if k == 0:
                if part_:
                    dve.wait_ge(S["mod_done"], part_)
                ins = V.tensor_scalar(ada_acc[:, :], src, cond[:, k:k + 1], None, ALU.mult)
            else:
                ins = V.scalar_tensor_tensor(ada_acc[:, :], src, cond[:, k:k + 1], ada_acc[:, :], ALU.mult, ALU.add)
            ins.then_inc(S["ada_used"], 1)
            dve.wait_ge(S["ada_used"], a + 1)

        def mod_take(m):
            dve.wait_ge(S["mod_done"], m + 1)
            V.tensor_tensor(mod[:, m, :], ps_t[:, 496:504], vec[:, COLS["ada_b"] + KC * m:COLS["ada_b"] + KC * (m + 1)],
                            ALU.add).then_inc(S["mod_ready"], 1)

        def variance(n, bank):
            w = 2 if n == 2 else 1
            dve.wait_ge(S["stat_done"], n + 1)
            own(V.tensor_scalar(var[:, 0:w, :], bank[:, 0:w * T].rearrange("p (a t) -> p a t", a=w), 1.0 / D, EPS if w == 1 else 0.0, ALU.mult, ALU.add))
            if w == 2:
                own(V.tensor_scalar(var[:, 0, :], var[:, 0, :], EPS, None, ALU.add))
                V.reciprocal(var[:, 0, :], var[:, 0, :]).then_inc(S["var_ready"], 1)
            else:
                V.reciprocal(var[:, 0, :], var[:, 0, :]).then_inc(S["var_ready"], 1)

        def make_u(m, scale, r, shift):
            def lo(k):
                dve.wait_ge(S["uhi_ready"], KC * m + k + 1)
                hi = u_hi[:, k, :].bitcast(F32)
                if shift is None:
                    V.tensor_tensor(u_lo[:, k, :], t_u[:, k % 2, :], hi, ALU.subtract).then_inc(S["ulo_ready"], 1)
                else:
                    V.scalar_tensor_tensor(u_lo[:, k, :], t_u[:, k % 2, :], mod[:, shift, k:k + 1], hi,
                                           ALU.add, ALU.subtract).then_inc(S["ulo_ready"], 1)
            for k in range(KC):
                if k >= 2 or m:
                    dve.wait_ge(S["ulo_ready"], KC * m + k - 1)
                V.scalar_tensor_tensor(t_u[:, k % 2, :], x[:, k, :], scale(k), r, ALU.mult, ALU.mult)\
                    .then_inc(S["t_ready"], 1)
                if k:
                    lo(k - 1)
            lo(KC - 1)

        for a in range(2 * KC):
            ada_step(a)
            if a == 2:
                dve.wait_ge(S["x_in"], 16)
                variance(0, ps_o)
                dve.wait_ge(S["start_act"], 4)
                own(V.tensor_tensor(cosT[:, :], cosT[:, :], cosT[:, :], ALU.mult))
                own(V.tensor_scalar(cosT[:, :], cosT[:, :], -2.0, 1.0, ALU.mult, ALU.add))
            if a == KC:
                mod_take(0)
        mod_take(1)
        dve.wait_ge(S["mod_ready"], 2)
        own(V.scalar_tensor_tensor(a_mix[:, 0, :], mod[:, 1, :], 1.0, vec[:, COLS["norm_mix"]:COLS["norm_mix"] + KC],
                                   ALU.add, ALU.mult))
        low(None, 3)
        dve.wait_ge(S["rstd_ready"], 1)
        make_u(0, lambda k: a_mix[:, 0, k:k + 1], rstd[:, 0, :], 0)

        def score_tile(t):
            return score[:, 0:T] if t else score[:, T:T + P]

        def idx_add(n):
            t, hh = n // 4, n % 4
            dve.wait_ge(S["relu_ready"], n + 1)
            if n == 0:
                dve.wait_ge(S["iw_ready"], 1)
            nk = P * (t + 1)
            dst = score_tile(t)
            for e in range(2):
                src = relu_s[:, n % 2, e * T:e * T + nk]
                prev = dst if (hh or e) else (cmask[:, :] if t else cmask[:, P:T])
                ins = V.scalar_tensor_tensor(dst, src, iw[:, t, hh + 4 * e:hh + 4 * e + 1], prev, ALU.mult, ALU.add)
                if e == 0:
                    own(ins)
                else:
                    ins.then_inc(S["idx_used"], 1)
                    dve.wait_ge(S["idx_used"], n + 1)

        def topk_round(t):
            dst = score_tile(t)
            own(V.max(top8[:, :], dst))
            own(V.match_replace(dst, top8[:, :], dst, TAKEN))

        def kv_norm_var():
            dve.wait_ge(S["kv_stat"], 1)
            own(V.tensor_scalar(var[:, 1, :], ps_o[:, 0:T], 1.0 / P, EPS, ALU.mult, ALU.add))
            V.reciprocal(var[:, 1, :], var[:, 1, :]).then_inc(S["kv_var"], 1)

        def kv_norm():
            dve.wait_ge(S["kv_rstd"], 1)
            V.scalar_tensor_tensor(kvT[:, :], kvf[:, :], col("kv_norm"), rstd[:, 1, :], ALU.mult, ALU.mult)\
                .then_inc(S["kvT_ready"], 1)

        SCALE = {"a": HD ** -0.5, "b": P ** -0.5, "c": HD ** -0.5}
        BIAS = {"a": 0, "b": NH, "c": 2 * NH}

        def logits(m):
            kind, h, _ = maps[m]
            r = heads.index((kind, h))
            dve.wait_ge(S["s_done"], m + 1)
            if m == 0:
                dve.wait_ge(S["bias_ready"], 6)
            if m >= 4:
                dve.wait_ge(S["t_done"], heads.index(maps[m - 4][:2]) + 1)
            p, b, ps = prob[:, m % 4, :], bias[:, BIAS[kind] + h, :], ps_s[m % 2]
            own(V.scalar_tensor_tensor(p[:, 0:T], ps[:, 0:T], SCALE[kind], b, ALU.mult, ALU.add))
            V.scalar_tensor_tensor(p[:, T:T + P], ps[:, T:T + P], SCALE[kind], b[:, P:T], ALU.mult, ALU.add)\
                .then_inc(S["s_taken"], 1)
            dve.wait_ge(S["s_taken"], m + 1)
            if kind == "b":
                own(V.tensor_tensor(p, p, score[:, :], ALU.add))
            own(V.tensor_reduce(nmax[:, m, 0:1], p[:, 0:T], AX.X, ALU.max, negate=True))
            V.tensor_reduce(nmax[:, m, 1:2], p[:, T:T + P], AX.X, ALU.max, negate=True).then_inc(S["max_ready"], 1)

        def normalise(r):
            ms = maps_of[r]
            m = ms[-1]
            dve.wait_ge(S["exp_ready"], m + 1)
            for q in ms:
                own(V.reciprocal(rsum[:, q, :], psum_[:, q, :]))
            p = prob[:, m % 4, :]
            if len(ms) == 1:
                own(V.tensor_scalar(p[:, 0:T], p[:, 0:T], rsum[:, m, 0:1], None, ALU.mult))
                V.tensor_scalar(p[:, T:T + P], p[:, T:T + P], rsum[:, m, 1:2], None, ALU.mult)\
                    .then_inc(S["p_ready"], 1)
                return
            p0 = prob[:, ms[0] % 4, :]
            own(V.tensor_scalar(lnorm[:, r, :], rsum[:, m, :], lam[:, 5:6], None, ALU.mult))
            own(V.tensor_scalar(p[:, 0:T], p[:, 0:T], lnorm[:, r, 0:1], None, ALU.mult))
            own(V.tensor_scalar(p[:, T:T + P], p[:, T:T + P], lnorm[:, r, 1:2], None, ALU.mult))
            own(V.scalar_tensor_tensor(p[:, 0:T], p0[:, 0:T], rsum[:, ms[0], 0:1], p[:, 0:T], ALU.mult, ALU.add))
            V.scalar_tensor_tensor(p[:, T:T + P], p0[:, T:T + P], rsum[:, ms[0], 1:2], p[:, T:T + P],
                                   ALU.mult, ALU.add).then_inc(S["p_ready"], 1)

        def sub_var(h):
            dve.wait_ge(S["ostat_done"], h + 1)
            own(V.tensor_scalar(o_var[:, h, :], ps_o[:, 0:T], 1.0 / P, EPS, ALU.mult, ALU.add))
            V.reciprocal(o_var[:, h, :], o_var[:, h, :]).then_inc(S["ovar_ready"], 1)

        def c_low(h):
            e = h % 2
            s = slice(e * HD, (e + 1) * HD)
            dve.wait_ge(S["och_ready"], h + 1)
            V.tensor_tensor(oc_lo[s, h // 2, :], ps_o[s, 0:T], oc_hi[s, h // 2, :].bitcast(F32), ALU.subtract)\
                .then_inc(S["o_taken"], 1)

        def b_low(h):
            e = h % 2
            s = slice(e * HD, (e + 1) * HD)
            dve.wait_ge(S["obh_ready"], h + 1)
            V.tensor_tensor(ob_lo[s, h // 2, :], ps_t[s, 0:T], ob_hi[s, h // 2, :].bitcast(F32), ALU.subtract)\
                .then_inc(S["uv_taken"], 1)

        for c in range(N_QKV + N_GATE):
            dve.wait_ge(S["unit_done"], c + 1)
            if c == 5:
                kv_norm_var()
            if c == 7:
                kv_norm()
            if 5 <= c <= 12:
                idx_add(c - 5)
            if 9 <= c < 13:
                topk_round(0)
                topk_round(0)
            if 13 <= c < 21:
                topk_round(1)
            if c == 21:
                own(V.tensor_scalar(score[:, :], score[:, :], TAKEN / 2, NEG, ALU.is_gt, ALU.mult))
            if c in norm_at:
                normalise(norm_at[c])
            if c in s_at:
                for m in maps_of[s_at[c]]:
                    logits(m)
            if c in o_at and heads[o_at[c]][0] == "c":
                c_low(heads[o_at[c]][1])
            if c in UV_AT:
                b_low(UV_AT[c])
            if c in SUB_AT:
                sub_var(SUB_AT[c])
            low(None, c + SLOTS)
            if 0 <= c - ADA_AT < 3 * KC:
                ada_step(2 * KC + c - ADA_AT)
            if c in MOD_AT:
                mod_take(MOD_AT[c])
            if FIN_AT <= c < FIN_AT + NH:
                h = c - FIN_AT
                dve.wait_ge(S["orstd_ready"], 1)
                V.scalar_tensor_tensor(o_raw[:, h, :], o_raw[:, h, :], subln[:, 0:1], o_var[:, h, :], ALU.mult, ALU.mult)\
                    .then_inc(S["ofin_ready"], 1)
            if OAL_AT <= c < OAL_AT + NH:
                h = c - OAL_AT
                dve.wait_ge(S["oah_ready"], h + 1)
                V.tensor_tensor(oa_lo[:, h, :], o_raw[:, h, :], oa_hi[:, h, :].bitcast(F32), ALU.subtract)\
                    .then_inc(S["oal_ready"], 1)
        dve.wait_ge(S["mod_ready"], 5)
        own(V.scalar_tensor_tensor(a_mix[:, 1, :], mod[:, 4, :], 1.0, vec[:, COLS["norm_mlp"]:COLS["norm_mlp"] + KC],
                                   ALU.add, ALU.mult))

        o = O_BR
        parts_seen = 0
        for n, (kind, q) in enumerate(BR_UNITS):
            parts = 2 if kind == "a" else 4
            for e in range(parts):
                j = parts * q + e
                if e < parts - 1:
                    parts_seen += 1
                    dve.wait_ge(S["part_done"], parts_seen)
                else:
                    dve.wait_ge(S["unit_done"], U_BR + n + 1)
                g_ = gates[:, {"a": 0, "b": KC, "c": 2 * KC}[kind] + j, :]
                if kind == "a":
                    V.scalar_tensor_tensor(merged[:, j, :], g_, 1.0, mm[o % 4][:, 0:T], ALU.add, ALU.mult)\
                        .then_inc(taken[o % 4], 1)
                else:
                    V.scalar_tensor_tensor(part[:, o % 2, :], g_, 1.0, mm[o % 4][:, 0:T], ALU.add, ALU.mult)\
                        .then_inc(taken[o % 4], 1)
                    dve.wait_ge(taken[o % 4], o // 4 + 1)
                    ins = V.tensor_tensor(merged[:, j, :], merged[:, j, :], part[:, o % 2, :], ALU.add)
                    if kind == "b":
                        own(ins)
                    else:
                        ins.then_inc(S["m_ready"], 1)
                o += 1
            low(None, U_BR + n + SLOTS)
            if kind == "c":
                for j in range(4 * q, 4 * q + 4):
                    dve.wait_ge(S["mh_ready"], j + 1)
                    V.scalar_tensor_tensor(m_lo[:, j, :], merged[:, j, :], 0.5, m_hi[:, j, :].bitcast(F32),
                                           ALU.mult, ALU.subtract).then_inc(S["ml_ready"], 1)

        def add_square(n, j, two=False):
            k = SQ_BASE[n] + j
            dve.wait_ge(S["sq_ready"], k + 1)
            w = 2 if two else 1
            if j == 0:
                ins = V.tensor_copy(acc[:, 0:w, :], sq[:, k % 2, 0:w, :])
            else:
                ins = V.tensor_tensor(acc[:, 0:w, :], acc[:, 0:w, :], sq[:, k % 2, 0:w, :], ALU.add)
            ins.then_inc(S["sq_used"], 1)
            dve.wait_ge(S["sq_used"], k + 1)

        for j in range(KC):
            o = O_WO + j
            dve.wait_ge(S["unit_done"], U_WO + j + 1)
            V.scalar_tensor_tensor(x[:, j, :], mm[o % 4][:, 0:T], mod[:, 2, j:j + 1], x[:, j, :], ALU.mult, ALU.add)\
                .then_inc(taken[o % 4], 1)
            low(None, U_WO + j + SLOTS)
            if j:
                add_square(1, j - 1)
        add_square(1, KC - 1)
        variance(1, ps_o)
        dve.wait_ge(S["rstd_ready"], 2)
        make_u(1, lambda k: a_mix[:, 1, k:k + 1], rstd[:, 0, :], 3)

        def up_turn(g, base):
            for i in range(8):
                c, o, f = U_F1 + base + i, O_F1 + base + i, base + i
                dve.wait_ge(taken[o % 4], lin(g, 2, o // 4 + 1))
                own(V.tensor_tensor(h_full[:, f % 2, :], relu_h[:, f % 2, :], relu_h[:, f % 2, :], ALU.mult))
                dve.wait_ge(S["hh_ready"], lin(g, 8, f + 1))
                sl = (lambda t: t[:, f, :]) if g is None else (lambda t: t[:, bass.ds(g * 8 + f, 1), :][:, 0, :])
                V.tensor_tensor(sl(h_lo), h_full[:, f % 2, :], sl(h_hi).bitcast(F32), ALU.subtract)\
                    .then_inc(S["hl_ready"], 1)
                low(g, c + SLOTS)
                if g is None:
                    ada_step(5 * KC + i)

        up_turn(None, 0)
        with dve.Fori(0, 3) as g:
            own.enter(g, 8)
            up_turn(g, 8)
            own.leave(3)
        mod_take(5)
        dve.wait_ge(S["mod_ready"], 6)
        for j in range(KC):
            for q in range(4):
                c = U_F2 + 4 * j + q
                dve.wait_ge(S["unit_done"], c + 1)
                if q == 3:
                    o = O_F2 + j
                    V.scalar_tensor_tensor(x[:, j, :], mm[o % 4][:, 0:T], mod[:, 5, j:j + 1], x[:, j, :],
                                           ALU.mult, ALU.add).then_inc(taken[o % 4], 1)
                low(None, c + SLOTS)
                if q == 0 and j:
                    add_square(2, j - 1, two=True)
        add_square(2, KC - 1, two=True)
        variance(2, ps_o)
        dve.wait_ge(S["rstd_ready"], 3)
        own(V.tensor_tensor(rt1[:, :], rstd[:, 0, :], rstd[:, 0, :], ALU.mult))
        own(V.tensor_tensor(var[:, 1, :], var[:, 1, :], rt1[:, :], ALU.mult))
        own(V.tensor_scalar(var[:, 1, :], var[:, 1, :], EPS, None, ALU.add))
        V.reciprocal(var[:, 1, :], var[:, 1, :]).then_inc(S["rms2_ready"], 1)
        for k in range(KC):
            own(V.scalar_tensor_tensor(x[:, k, :], x[:, k, :], col("norm_final", k), rstd[:, 0, :], ALU.mult, ALU.mult))
        dve.wait_ge(S["rstd2_ready"], 1)
        make_u(2, lambda k: col("pre", k), rstd[:, 1, :], None)
        own(V.memset(cv[:, :, 0:2], 0.0))

        for l in range(LAYERS):
            uA = U_LAYER + LAYER_UNITS * l
            oA = O_LAYER + LAYER_OUTS * l
            H = RH * l

            def a_turn(g, n0):
                c0, o0, hb = uA + 8 * n0, oA + 8 * n0, H + 2 * n0

                def rotate(i, h, is_k):
                    ps, dst = mm[(o0 + i) % 4], (kr if is_k else qr)[:, h, :]
                    if hb + h >= 2:
                        dve.wait_ge(S["rs_done"], lin(g, 2, hb + h - 1))
                    own(V.tensor_tensor(rt1[:, :], ps[:, 0:T], cosT[:, :], ALU.mult))
                    own(V.tensor_tensor(rt2[0:HD, :], ps[HD:P, 0:T], sinT[HD:P, :], ALU.mult))
                    V.tensor_tensor(rt2[HD:P, :], ps[0:HD, 0:T], sinT[0:HD, :], ALU.mult)\
                        .then_inc(taken[(o0 + i) % 4], 1)
                    dve.wait_ge(taken[(o0 + i) % 4], lin(g, 2, (o0 + i) // 4 + 1))
                    V.tensor_tensor(dst, rt1[:, :], rt2[:, :], ALU.add).then_inc(S["rot_ready"], 1)
                    n = 2 * (hb + h) + (2 if is_k else 1)
                    dve.wait_ge(S["rot_ready"], lin(g, 4, n))

                def decayed(h):
                    dve.wait_ge(S["rs_done"], lin(g, 2, hb + h + 1))
                    if hb + h >= 2:
                        dve.wait_ge(S["ro_done"], lin(g, 2, hb + h - 1))
                    n = 2 * n0 + h
                    d = dec[:, n, :] if g is None else dec[:, bass.ds(g * 2 + n, 1), :][:, 0, :]
                    V.tensor_tensor(sdec[:, h, :], ps_s[h][:, 0:3 * P], d, ALU.mult).then_inc(S["rs_taken"], 1)

                def silu_z(i, h):
                    n = 2 * n0 + h
                    dst = zsil[:, n, :] if g is None else zsil[:, bass.ds(g * 2 + n, 1), :][:, 0, :]
                    dve.wait_ge(S["th_ready"], lin(g, 2, ZU[l] + 2 * n0 + h + 1))
                    V.scalar_tensor_tensor(dst, th[:, h, :], 1.0, mm[(o0 + i) % 4][:, 0:T], ALU.add, ALU.mult)\
                        .then_inc(taken[(o0 + i) % 4], 1)
                    dve.wait_ge(taken[(o0 + i) % 4], lin(g, 2, (o0 + i) // 4 + 1))

                for i in range(8):
                    dve.wait_ge(S["unit_done"], lin(g, 8, c0 + i + 1))
                    if i in (1, 2, 4, 5):
                        rotate(i, i // 3, i in (2, 5))
                    if i >= 6:
                        silu_z(i, i - 6)
                    if i == 3:
                        decayed(0)
                    if i == 6:
                        decayed(1)
                    low(g, c0 + i + SLOTS)
                    if i == 2 and n0:
                        head_var(g, hb // 2 - 1)

            def head_var(g, n):
                dve.wait_ge(S["rstat_done"], lin(g, 1, n + 1))
                q = 2 * (n % 4)
                dst = ret_sq[:, q:q + 2, :] if g is None else ret_sq[:, bass.ds(g * 2 + q, 2), :]
                own(V.tensor_scalar(rv[:, :, :], ps_o[:, :].rearrange("p (a t) -> p a t", a=2), 1.0 / P, EPS, ALU.mult, ALU.add))
                V.reciprocal(dst, rv[:, :, :]).then_inc(S["rvar_ready"], 1)
                dve.wait_ge(S["rvar_ready"], lin(g, 1, n + 1))

            if l == 0:
                dve.wait_ge(S["decay_in"], 16)
            a_turn(None, 0)
            with dve.Fori(0, 3) as g:
                own.enter(g, 9)
                a_turn(g, 1)
                own.leave(3)

            def conv_low(g, n):
                dve.wait_ge(S["ych_ready"], lin(g, 2, 8 * l + n + 1))
                row = (lambda t: t[:, n, :]) if g is None else (lambda t: t[:, bass.ds(g * 2 + n, 1), :][:, 0, :])
                V.scalar_tensor_tensor(row(mix_lo), cy[:, n % 2, :], 0.5, row(mix_hi).bitcast(F32),
                                       ALU.mult, ALU.subtract).then_inc(S["mixc_ready"], 1)
                dve.wait_ge(S["mixc_ready"], lin(g, 2, 8 * l + n + 1))

            def b_turn(g, n0):
                c0, o0 = uA + 32 + 8 * n0, oA + 32 + 8 * n0

                def row(t, n):
                    return t[:, n, :] if g is None else t[:, bass.ds(g * 2 + n, 1), :][:, 0, :]

                for e in range(2):
                    n = 2 * n0 + e

                    def wcol(tap):
                        at = COLS["conv"] + 24 * l + 8 * tap + n
                        return vec[:, at:at + 1] if g is None else vec[:, bass.ds(g * 2 + at, 1)]

                    for i in range(4):
                        ii = 4 * e + i
                        o = o0 + ii
                        ps = mm[o % 4][:, 0:T]
                        tk, tv = taken[o % 4], lin(g, 2, o // 4 + 1)
                        dve.wait_ge(S["unit_done"], lin(g, 8, c0 + ii + 1))
                        if i == 1:
                            dve.wait_ge(taken[(o - 1) % 4], lin(g, 2, (o - 1) // 4 + 1))
                            V.tensor_tensor(cv[:, e, 2:T + 2], cc[:, e, :], ps, ALU.mult).then_inc(tk, 1)
                            dve.wait_ge(tk, tv)
                            own(V.tensor_scalar(cy[:, e, :], cv[:, e, 0:T], wcol(0), None, ALU.mult))
                            for tap in (1, 2):
                                own(V.scalar_tensor_tensor(cy[:, e, :], cv[:, e, tap:tap + T], wcol(tap), cy[:, e, :],
                                                           ALU.mult, ALU.add))
                        if i == 2:
                            V.tensor_tensor(cy[:, e, :], cy[:, e, :], ps, ALU.mult).then_inc(tk, 1)
                            dve.wait_ge(tk, tv)
                        if i == 3:
                            dve.wait_ge(S["th_ready"], lin(g, 2, ZU[l] + 8 + n + 1))
                            V.scalar_tensor_tensor(rt2[:, :], th_c[:, e, :], 1.0, ps, ALU.add, ALU.mult).then_inc(tk, 1)
                            dve.wait_ge(tk, tv)
                            V.tensor_tensor(cy[:, e, :], cy[:, e, :], rt2[:, :], ALU.mult).then_inc(S["yc_ready"], 1)
                            dve.wait_ge(S["yc_ready"], lin(g, 2, 8 * l + n + 1))
                        low(g, c0 + ii + SLOTS)
                        if ii == 0 and n0 == 0:
                            head_var(None, 4 * l + 3)
                        if i == 1:
                            if n == 0:
                                dve.wait_ge(S["rrstd_ready"], l + 1)
                            own(V.tensor_tensor(rt1[:, :], row(ret, n), row(ret_sq, n), ALU.mult))
                            V.tensor_tensor(qr[:, e, :], rt1[:, :], row(zsil, n), ALU.mult).then_inc(S["yr_ready"], 1)
                            dve.wait_ge(S["yr_ready"], lin(g, 2, 8 * l + n + 1))
                            if n:
                                conv_low(g, n - 1)
                        if i == 3:
                            dve.wait_ge(S["yrh_ready"], lin(g, 2, 8 * l + n + 1))
                            V.scalar_tensor_tensor(row(mix_lo, KC + n), qr[:, e, :], 0.5,
                                                   row(mix_hi, KC + n).bitcast(F32), ALU.mult, ALU.subtract)\
                                .then_inc(S["mixr_ready"], 1)

            b_turn(None, 0)
            with dve.Fori(0, 3) as g:
                own.enter(g, 8)
                b_turn(g, 1)
                own.leave(3)
            conv_low(None, KC - 1)
            n_out = 3 + 2 * l
            for j in range(KC):
                for q in range(2):
                    c = uA + 64 + 2 * j + q
                    dve.wait_ge(S["unit_done"], c + 1)
                    low(None, c + SLOTS)
                if j:
                    add_square(n_out, j - 1)
            add_square(n_out, KC - 1)
            variance(n_out, ps_o)
            dve.wait_ge(S["rstd_ready"], n_out + 1)
            last = l + 1 == LAYERS
            for j in range(KC):
                own(V.scalar_tensor_tensor(o_out[:, j, :], o_out[:, j, :], col("post", KC * l + j), rstd[:, 0, :],
                                           ALU.mult, ALU.mult))
                V.tensor_tensor(x[:, j, :], x[:, j, :], o_out[:, j, :], ALU.add)\
                    .then_inc(S["x_final" if last else "x_new"], 1)
                if not last and j:
                    add_square(n_out + 1, j - 1)
            if not last:
                add_square(n_out + 1, KC - 1)
                variance(n_out + 1, ps_o)
                dve.wait_ge(S["rstd_ready"], n_out + 2)
                make_u(3 + l, lambda k: col("pre", KC * (l + 1) + k), rstd[:, 0, :], None)


BR_UNITS = [("a", 0), ("a", 1), ("b", 0), ("a", 2), ("c", 0), ("a", 3), ("b", 1), ("c", 1)]
SQ_BASE = {1: 0, 2: KC, 3: 2 * KC, 4: 3 * KC, 5: 4 * KC}
ZU = [0, 16]
TWO_PI_PARTS = []
_rest = 2 * math.pi
for _bits in (8, 11, 24):
    _q = 2.0 ** (math.floor(math.log2(_rest)) + 1 - _bits)
    TWO_PI_PARTS.append(math.floor(_rest / _q) * _q)
    _rest -= TWO_PI_PARTS[-1]
PI_BELOW = float(np.nextafter(np.float32(math.pi), np.float32(0)))


def _units(w, order=None):
    n = w.shape[1] // P
    return w.reshape(KC, P, n, P).transpose(2, 1, 0, 3).reshape(n, P, KC * P)


def _columns(v):
    return v.reshape(-1, P).T


def _stream(w_in, w_br_a, w_br_b, w_br_c, w_o, w_ff1, w_ff2, w_in_2, w_out_2):
    at = np.cumsum([0, 512, 512, 512, 512, 128, 256, 32, 8, 256, 256, 256, 3072])
    aq, ak, av, bq, bkv, biq, bik, biw, cq, ck, cv, gate = [w_in[:, a:b] for a, b in zip(at[:-1], at[1:])]
    parts = [_units(np.pad(biw, ((0, 0), (0, P - 8)))), _units(biq), _units(np.concatenate([bik] * 4, axis=1)),
             _units(bkv), _units(bq)]
    for h in range(NH):
        parts += [_units(m[:, h * P:(h + 1) * P]) for m in (aq, ak, av)]
    for j in range(2):
        parts += [_units(m[:, j * P:(j + 1) * P]) for m in (cq, ck, cv)]
    parts.append(_units(gate))
    for kind, q in BR_UNITS:
        w = {"a": w_br_a, "b": w_br_b, "c": w_br_c}[kind]
        k = w.shape[0] // P
        n = KC // k
        w = w[:, q * n * P:(q + 1) * n * P].reshape(k, P, n, P)
        parts.append(w.transpose(1, 2, 0, 3).reshape(1, P, KC * P))
    parts += [_units(w_o), _units(w_ff1)]
    f = [_units(w_ff2[q * D:(q + 1) * D]) for q in range(4)]
    parts.append(np.stack(f, axis=1).reshape(4 * KC, P, KC * P))
    for l in range(LAYERS):
        m = _units(w_in_2[l]).reshape(8, KC, P, KC * P)
        c_b, c_c, c_x, c_z, r_q, r_k, r_v, r_z = m
        heads = [(r_v, 0), (r_q, 0), (r_k, 0), (r_v, 1), (r_q, 1), (r_k, 1), (r_z, 0), (r_z, 1)]
        for h in range(0, RH, 2):
            parts.append(np.stack([w[h + e] for w, e in heads]))
        for j in range(KC):
            parts.append(np.stack([c_c[j], c_x[j], c_b[j], c_z[j]]))
        conv, ret = _units(w_out_2[l][:D]), _units(w_out_2[l][D:])
        parts.append(np.stack([ret, conv], axis=1).reshape(2 * KC, P, KC * P))
    s = np.concatenate(parts)
    assert s.shape[0] == UNITS
    s = np.concatenate([s, np.zeros_like(s[:UNITS % 2])])
    return np.ascontiguousarray(s.reshape(-1, 2, P, KC * P).transpose(0, 2, 1, 3).reshape(-1, P, 2 * KC * P))


def _constants():
    f = np.float32
    dist = T - 1 - np.arange(3 * P)
    n = np.maximum(dist, 0)
    half = N_BUCKETS // 2
    large = half + (np.log(np.maximum(n, 1).astype(f) / f(half)) / f(math.log(MAX_DISTANCE / half))
                    * f(N_BUCKETS - half)).astype(np.int32)
    bucket = np.where(dist < 0, N_BUCKETS, np.where(n < half, n, np.minimum(large, N_BUCKETS - 1)))
    onehot = (bucket[None] == np.arange(N_BUCKETS + 1)[:, None]).astype(f)
    i = np.arange(P)
    cmask = np.concatenate([np.zeros((P, P), f), np.where(i[None] > i[:, None], f(NEG), f(0))], axis=1).astype(f)
    lg = np.log1p(-np.exp2(-5.0 - np.arange(RH)))
    diff = i[None, :] - i[:, None]
    diag = np.where(diff >= 0, np.exp(lg[:, None, None] * np.maximum(diff, 0)), 0.0)
    off = np.exp(lg[:, None, None] * (diff + P))
    dec = (np.concatenate([diag, off, diag], axis=2) * P ** -0.5).transpose(1, 0, 2).astype(f)
    freq = (f(1.0) / f(10000.0) ** (np.arange(HD, dtype=f) / f(HD))).astype(f)
    freq = np.concatenate([freq, freq])
    sign = np.where(i < HD, f(1), f(-1))
    return dict(onehot=onehot, ident=np.eye(P, dtype=f), cmask=cmask, decay=np.ascontiguousarray(dec),
                freq=np.stack([freq, freq * sign], axis=1))


def kernel(**inp):
    import concourse.bacc as bacc
    from concourse.bass_utils import run_bass_kernel_spmd

    a = {k: np.asarray(v) for k, v in inp.items()}
    k = _constants()
    vec = [_columns(a["c"][0]), _columns(a["ada_b"][0]), _columns(a["norm_mix"][0]), _columns(a["gate_b"][0]),
           _columns(a["diff_subln"][0]), _columns(a["dsa_kv_norm"][0]), _columns(a["norm_mlp"][0]),
           _columns(a["norm_final"]), _columns(a["pre_norm_2"].reshape(-1)), _columns(a["post_norm_2"].reshape(-1)),
           _columns(a["conv_w_2"].reshape(-1)), k["freq"]]
    arrays = {
        "xT": a["x"][0].T.reshape(KC, P, T).transpose(1, 0, 2),
        "weights": _stream(a["w_in"][0], a["w_br_a"][0], a["w_br_b"][0], a["w_br_c"][0], a["w_o"][0], a["w_ff1"][0],
                           a["w_ff2"][0], a["w_in_2"], a["w_out_2"]),
        "ada": a["ada_w"][0].reshape(KC // 2, 2, P, 6, D).transpose(3, 0, 2, 1, 4).reshape(24, P, 2 * D),
        "cols": np.concatenate(vec, axis=1),
        "dl": a["diff_lambda"][0].reshape(1, -1),
        "relb": np.concatenate([a["rel_bias"], np.full((1, 12), NEG, np.float32)]),
        "onehot": k["onehot"], "ident_d": k["ident"], "flip_d": k["ident"][::-1], "cmask_d": k["cmask"], "decay": k["decay"],
        "positions": a["positions_2"].astype(np.int32),
        "w_uv": a["dsa_w_uv"][0].transpose(1, 0, 2),
    }
    arrays = {n: np.ascontiguousarray(v) for n, v in arrays.items()}
    nc = bacc.Bacc("TRN2", target_bir_lowering=False, num_devices=1)
    aps = {n: nc.dram_tensor(n, v.shape, mybir.dt.from_np(v.dtype), kind="ExternalInput").ap()
           for n, v in arrays.items()}
    out = nc.dram_tensor("out", (P, KC, T), F32, kind="ExternalOutput").ap()
    build(nc, out=out, **aps)
    res = run_bass_kernel_spmd(nc, [arrays], core_ids=[0]).results[0]["out"]
    return res.transpose(1, 0, 2).reshape(D, T).T.reshape(1, T, D)
```

```python
import math
from contextlib import ExitStack

import numpy as np

import concourse.bass as bass
from concourse import mybir

F32 = mybir.dt.float32
F32R = mybir.dt.float32r
I32 = mybir.dt.int32
ALU = mybir.AluOpType
ACT = mybir.ActivationFunctionType
AX = mybir.AxisListType

P = 128
D = 1024
T = 256
KC = D // P
QT = T // P
HD = 64
NH = 4
LAYERS = 2
RH = 8
TOPK = 64
EPS = 1e-6
NEG = -1.0e30
TAKEN = -3.0e38
N_BUCKETS = 32
MAX_DISTANCE = 128
LAM_INIT = 0.8 - 0.6 * math.exp(0.0)

U_QKV = 0
N_QKV = 27
N_GATE = 24
U_BR = N_QKV + N_GATE
U_WO = U_BR + 8
U_F1 = U_WO + 8
U_F2 = U_F1 + 32
U_LAYER = U_F2 + 32
LAYER_UNITS = 80
UNITS = U_LAYER + LAYERS * LAYER_UNITS
O_BR = U_BR
O_WO = O_BR + 24
O_F1 = O_WO + 8
O_F2 = O_F1 + 32
O_LAYER = O_F2 + 8
LAYER_OUTS = 72
SLOTS = 4
FIRST = 3
MOD_LAG = 6, 3, 3
WARM = (6, 5, 7, 2, 10)
RAW_PAIRS = 4

C_IW, C_IQ, C_IK, C_KV, C_BQ = 0, 1, 3, 4, 5
C_A = 9
C_C = 21

SCALE1, SHIFT1, GATE1, SHIFT2, SCALE2, GATE2 = range(6)

COLS = {}
_at = 0
for _name, _n in (("c", 8), ("ada_b", 48), ("norm_mix", 8), ("gate_b", 24), ("subln", 1), ("kv_norm", 1),
                  ("norm_mlp", 8), ("norm_final", 8), ("pre", 16), ("post", 16), ("conv", 48), ("freq", 2)):
    COLS[_name] = _at
    _at += _n
N_COLS = _at


def lin(g, per, const):
    return const if g is None else g * per + const


class Chain:

    def __init__(self, eng, sem):
        self.eng, self.sem, self.n, self.g, self.per, self.start = eng, sem, 0, None, 0, 0

    def __call__(self, ins):
        self.n += 1
        ins.then_inc(self.sem, 1)
        self.eng.wait_ge(self.sem, lin(self.g, self.per, self.n))

    def enter(self, g, per):
        self.g, self.per, self.start = g, per, self.n

    def leave(self, turns):
        assert self.n - self.start == self.per, (self.n - self.start, self.per)
        self.n = self.start + turns * self.per
        self.g = None


def build(nc, xT, weights, ada, cols, dl, relb, onehot, ident_d, flip_d, cmask_d, decay, positions, w_uv, out):
    with ExitStack() as ctx:
        _build(nc, ctx, xT, weights, ada, cols, dl, relb, onehot, ident_d, flip_d, cmask_d, decay, positions, w_uv, out)


def _build(nc, ctx, xT, weights, ada, cols, dl, relb, onehot, ident_d, flip_d, cmask_d, decay, positions, w_uv, out):
    def tile_in(stack, name, shape, dt=F32):
        return stack.enter_context(nc.sbuf_tensor(name, shape, dt))

    def keep(name, shape, dt=F32):
        return tile_in(ctx, name, shape, dt)

    def sem(name):
        return ctx.enter_context(nc.semaphore(name))

    x = keep("x", [P, KC, T])
    u_hi = keep("u_hi", [P, KC, T], F32R)
    u_lo = keep("u_lo", [P, KC, T], F32R)
    raw = keep("raw", [P, RAW_PAIRS, 2 * KC * P])
    w_hi = keep("w_hi", [P, SLOTS, KC * P], F32R)
    w_lo = keep("w_lo", [P, SLOTS, KC * P], F32R)
    vec = keep("vec", [P, N_COLS])
    mod = keep("mod", [P, 6, KC])
    ident = keep("ident", [P, P])
    ones = keep("ones", [P, P])
    flip = keep("flip", [P, P])
    cosT = keep("cosT", [P, T])
    sinT = keep("sinT", [P, T])
    a_mix = keep("a_mix", [P, 2, KC])
    half_gb = keep("half_gb", [P, 24])
    subln = keep("subln", [P, 1])
    cond = keep("cond", [P, KC])
    nf_pre = keep("nf_pre", [P, KC])
    lam = keep("lam", [P, 8])
    tok_v = keep("tok_v", [P, 4])
    tok_r = keep("tok_r", [P, 4])
    diag = keep("diag", [P, 4, P])

    with ExitStack() as early:
        prob = tile_in(early, "prob", [P, 4, 3 * P])
        vf = tile_in(early, "vf", [P, 2, T])
    t_u = keep("t_u", [P, 2, T])
    sq = keep("sq", [P, 2, 2, T])
    acc = keep("acc", [P, 2, T])
    ph1 = ExitStack()
    p1 = lambda name, shape, dt=F32: tile_in(ph1, name, shape, dt)
    ada_raw = p1("ada_raw", [P, 2, 2 * D])
    ada_acc = p1("ada_acc", [P, 2, D])
    v_tok = p1("v_tok", [P, NH, QT, P])
    cv_tok = p1("cv_tok", [P, 2, QT, P])
    stA = ExitStack()
    pA = lambda name, shape, dt=F32: tile_in(stA, name, shape, dt)
    iwf = pA("iwf", [8, T])
    iw = pA("iw", [P, QT, 8])
    iqT = pA("iqT", [P, 2, T])
    ikT = pA("ikT", [P, T])
    relu_s = pA("relu_s", [P, 2, 2 * T])
    kvf = pA("kvf", [P, T])
    kv_sq = pA("kv_sq", [P, T])
    kv_v = pA("kv_v", [P, T])
    kv_r = pA("kv_r", [P, T])
    stA.close()
    gates = p1("gates", [P, 24, T])
    wuv = p1("wuv", [P, NH, HD])
    kvT = p1("kvT", [P, T])
    kv_tok = p1("kv_tok", [P, QT, P])
    o_mid = p1("o_mid", [P, T])
    bqT = p1("bqT", [P, NH, T])
    ob_hi = p1("ob_hi", [P, 2, T], F32R)
    ob_lo = p1("ob_lo", [P, 2, T], F32R)
    oc_hi = p1("oc_hi", [P, 2, T], F32R)
    oc_lo = p1("oc_lo", [P, 2, T], F32R)
    stB = ExitStack()
    pB = lambda name, shape, dt=F32: tile_in(stB, name, shape, dt)
    bias = pB("bias", [P, 12, T])
    with ExitStack() as early:
        x_sq = tile_in(early, "x_sq", [P, KC, T])
        x_sum = tile_in(early, "x_sum", [P, T])
    aqT = pB("aqT", [P, 2, T])
    akT = pB("akT", [P, 2, T])
    cqT = pB("cqT", [P, 2, T])
    ckT = pB("ckT", [P, 2, T])
    score = pB("score", [P, 3 * P])
    top8 = pB("top8", [P, 8])
    cmask = pB("cmask", [P, T])
    o_raw = pB("o_raw", [P, NH, T])
    probT = pB("probT", [P, 2, 3 * P])
    o_var = pB("o_var", [P, NH, T])
    nmax = pB("nmax", [P, 16, 2])
    psum_ = pB("psum_", [P, 16, 2])
    rsum = pB("rsum", [P, 16, 2])
    lnorm = pB("lnorm", [P, 4, 2])
    stB.close()
    stC = ExitStack()
    pC = lambda name, shape, dt=F32: tile_in(stC, name, shape, dt)
    oa_hi = pC("oa_hi", [P, NH, T], F32R)
    oa_lo = pC("oa_lo", [P, NH, T], F32R)
    merged = pC("merged", [P, KC, T])
    part = pC("part", [P, 2, T])
    m_hi = pC("m_hi", [P, KC, T], F32R)
    m_lo = pC("m_lo", [P, KC, T], F32R)
    stC.close()
    ph1.close()

    st0 = ExitStack()
    p0 = lambda name, shape, dt=F32: tile_in(st0, name, shape, dt)
    p0("pad_ada", [P, 6 * D])
    ada_more = p0("ada_more", [P, 2, 2 * D])
    dlb = p0("dlb", [P, 4 * HD])
    dlp = p0("dlp", [P, 2 * HD])
    relb_s = p0("relb_s", [N_BUCKETS + 1, 12])
    hot = p0("hot", [N_BUCKETS + 1, 3 * P])
    tab_s = p0("tab_s", [12, 3 * P])
    pos_i = p0("pos_i", [P, T], I32)
    pos_f = p0("pos_f", [P, T])
    ang = p0("ang", [P, 2, T])
    turns = p0("turns", [P, 2, T])
    part_turn = p0("part_turn", [P, 2, T])
    st0.close()

    ph2 = ExitStack()
    p2 = lambda name, shape, dt=F32: tile_in(ph2, name, shape, dt)
    pad3 = p2("pad3", [P, 6, D])
    h_hi = p2("h_hi", [P, 32, T], F32R)
    h_lo = p2("h_lo", [P, 32, T], F32R)
    relu_h = p2("relu_h", [P, 2, T])
    h_full = p2("h_full", [P, 2, T])
    ph2.close()

    ph3 = ExitStack()
    p3 = lambda name, shape, dt=F32: tile_in(ph3, name, shape, dt)
    dec = p3("dec", [P, RH, 3 * P])
    mix_hi = p3("mix_hi", [P, 2 * KC, T], F32R)
    mix_lo = p3("mix_lo", [P, 2 * KC, T], F32R)
    ret = p3("ret", [P, RH, T])
    ret_sq = p3("ret_sq", [P, RH, T])
    zsil = p3("zsil", [P, RH, T])
    qr = p3("qr", [P, 2, T])
    kr = p3("kr", [P, 2, T])
    rt1 = p3("rt1", [P, T])
    rv = p3("rv", [P, 2, T])
    rt2 = p3("rt2", [P, T])
    vfr = p3("vfr", [P, 2, T])
    vtr = p3("vtr", [P, 2, QT, P])
    sdec = p3("sdec", [P, 2, 3 * P])
    th = p3("th", [P, 2, T])
    th_c = p3("th_c", [P, 2, T])
    cc = p3("cc", [P, 2, T])
    cv = p3("cv", [P, 2, T + 2])
    cy = p3("cy", [P, 2, T])
    o_out = p3("o_out", [P, KC, T])
    ph3.close()

    tab_d = nc.dram_tensor("tab_scratch", [12, 3 * P], F32, kind="Internal").ap()

    mm = [ctx.enter_context(nc.psum_tensor(f"mm{i}", [P, 512], F32)) for i in range(4)]
    ps_s = [ctx.enter_context(nc.psum_tensor(f"ps_s{i}", [P, 512], F32)) for i in range(2)]
    ps_t = ctx.enter_context(nc.psum_tensor("ps_t", [P, 512], F32))
    ps_o = ctx.enter_context(nc.psum_tensor("ps_o", [P, 512], F32))

    names = """ident_in tab_in dl_in pos_in start_pool pool_own raw_in0 raw_in1 raw_in2 raw_in3 small_in x_in tab_out bias_in decay_in stored
        hi_ready lo_pool lo_dve lo_first unit_done part_done taken0 taken1 taken2 taken3
        ada_in0 ada_in1 ada_in2 ada_in3 mod_done mod_ready
        ones_ready act_own dve_own start_act start_dve tab_done tab_evac
        x_squared x_summed stat_done var_ready rstd_ready t_ready uhi_ready ulo_ready
        iw_tr iw_ready idx_done relu_ready idx_used kv_squared kv_stat kv_var kv_rstd kvT_ready kv_tr kv_tok_ready
        s_done s_taken max_ready exp_ready p_ready t_done pt_ready o_done o_taken vt_done vt_ready
        uv_done uv_taken osq_ready ostat_done ovar_ready orstd_ready ofin_ready oah_ready oal_ready
        obh_ready
        m_ready mh_ready ml_ready sq_ready 
        hh_ready hl_ready
        rot_ready rv_tr rv_ready rs_done rs_taken ro_done ret_taken retsq_ready th_ready
        rstat_done rvar_ready rrstd_ready yr_ready yrh_ready mixr_ready yc_ready ych_ready mixc_ready
        start_in ada_used och_ready sq_used root_ready diag_ready r1_ready x3_ready sq_summed ulo_pool y_ready x_pool x_new""".split()
    S = {n: sem(n) for n in names}
    raw_in = [S[f"raw_in{i}"] for i in range(RAW_PAIRS)]
    taken = [S[f"taken{i}"] for i in range(4)]
    ada_in = [S[f"ada_in{i}"] for i in range(4)]

    def col(name, i=0):
        return vec[:, COLS[name] + i:COLS[name] + i + 1]

    maps = []
    for h in range(NH):
        for m in range(2):
            maps.append(("a", h, m))
    maps += [("b", h, 0) for h in range(NH)] + [("c", h, 0) for h in range(NH)]
    heads = [("a", h) for h in range(NH)] + [("b", h) for h in range(NH)] + [("c", h) for h in range(NH)]
    maps_of = {r: [i for i, m in enumerate(maps) if m[:2] == heads[r]] for r in range(12)}
    s_at = {12 + 3 * r: r for r in range(12)}
    exp_at = {c + 1: r for c, r in s_at.items()}
    norm_at = {c + 2: r for c, r in s_at.items()}
    t_at = {c + 3: r for c, r in s_at.items()}
    o_at = {c + 4: r for c, r in s_at.items()}
    SUB_AT = {17 + 3 * h: h for h in range(NH)}
    UV_AT = {29 + 3 * h: h for h in range(NH)}
    VT_AT = {13 + 3 * h: 1 + h for h in range(NH)} | {25: 5, 28: 6}
    ADA_AT = [c for c in range(1, 48) if c % 6 in (1, 2, 4)]
    MOD_AT = {ADA_AT[KC * (m - 1) - 1] + MOD_LAG[m - 2]: m for m in (GATE1, SHIFT2, SCALE2)}
    LOAD_AT = {ADA_AT[2 * (n - 10) + 1] + 1: n for n in range(10, 20)}
    assert len(ADA_AT) == 3 * KC
    TOPK_AT = {9: [0] * 3, 10: [0] * 3, 11: [0] * 2, 13: [1], 14: [1], 16: [1] * 2, 17: [1], 19: [1], 21: [1], 22: [1]}
    ROOT_AT, FIN_AT, OAH_AT, OAL_AT = 30, 31, 35, 37

    block = ctx.enter_context(nc.Block())

    def ada_slot(n):
        if n < 8:
            return (ada_raw if n % 4 < 2 else ada_more)[:, n % 2, :], n % 4, n // 4 + 1
        return ada_raw[:, n % 2, :], n % 2, n // 2 - 1

    def ada_load(eng, n):
        dst, q, _ = ada_slot(n)
        if n >= 4:
            eng.wait_ge(S["ada_used"], 2 * n - (6 if n < 8 else 2))
        eng.dma_start(dst, ada[n]).then_inc(ada_in[q], 16)

    @block.sync
    def _(sp):
        sp.dma_start(vec[:, :], cols).then_inc(S["small_in"], 16)
        sp.dma_start(relb_s[:, :], relb).then_inc(S["tab_in"], 16)
        sp.dma_start(hot[:, :], onehot).then_inc(S["tab_in"], 16)
        sp.dma_start(dlb[:, :], bass.AP(dl.tensor, 0, [[0, P], [1, 4 * HD]])).then_inc(S["dl_in"], 16)
        sp.dma_start(pos_i[:, :], bass.AP(positions.tensor, 0, [[0, P], [1, T]])).then_inc(S["pos_in"], 16)

        def load(g, p):
            src = weights[p] if g is None else weights[bass.ds(g * 4 + p, 1)].rearrange("o p n -> p (o n)")
            if p >= RAW_PAIRS:
                n = 2 * p - 2 * RAW_PAIRS + 2
                sp.wait_ge(S["lo_pool"], lin(g, 8, n))
                if n % 4 == 0:
                    sp.wait_ge(S["lo_dve"], lin(g, 8, n))
            both = 2 * p + 1 < UNITS
            width = (2 if both else 1) * KC * P
            sp.dma_start(raw[:, p % RAW_PAIRS, 0:width], src[:, 0:width]).then_inc(raw_in[p % RAW_PAIRS], 16)

        sp.dma_start(ident[:, :], ident_d).then_inc(S["ident_in"], 16)

        for n in range(8):
            ada_load(sp, n)
            if n == 3:
                sp.dma_start(x[:, :, :], xT).then_inc(S["x_in"], 16)
        for p in range(4):
            load(None, p)
        sp.dma_start(flip[:, :], flip_d).then_inc(S["start_in"], 16)
        sp.dma_start(cmask[:, :], cmask_d).then_inc(S["start_in"], 16)
        sp.dma_start(wuv[:, :, :], w_uv).then_inc(S["start_in"], 16)
        ada_load(sp, 8)
        ada_load(sp, 9)
        sp.wait_ge(S["tab_out"], 16)
        sp.dma_start(bias[:, :, :], bass.AP(tab_d.tensor, 0, [[1, P], [3 * P, 12], [1, T]]))\
            .then_inc(S["bias_in"], 16)
        sp.wait_ge(S["lo_first"], 1)
        n_loops = (UNITS // 2 - 4) // 4
        with sp.Fori(0, n_loops) as g:
            for i in range(4):
                load(g, 4 + i)
        for p in range(4 + 4 * n_loops, (UNITS + 1) // 2):
            load(None, p)
        for q in range(4):
            sp.wait_ge(S["x_new"], KC // 2 + q + 1)
            sp.wait_ge(S["x_pool"], KC // 2 + q + 1)
            sp.dma_start(out[:, 2 * q:2 * q + 2, :], x[:, 2 * q:2 * q + 2, :]).then_inc(S["stored"], 16)
        sp.wait_ge(S["stored"], 64)

    @block.gpsimd
    def _(pool):
        def low(g, c):
            if c % 4 == 3 or c == 1:
                return
            pool.wait_ge(S["hi_ready"], lin(g, 8, c + 1))
            if c >= SLOTS:
                pool.wait_ge(S["unit_done"], lin(g, 8, c - SLOTS + 1))
            r = raw[:, (c // 2) % RAW_PAIRS, (c % 2) * KC * P:(c % 2 + 1) * KC * P]
            s = c % SLOTS
            nc.gpsimd.tensor_tensor(w_lo[:, s, :], r, w_hi[:, s, :].bitcast(F32), ALU.subtract)\
                .then_inc(S["lo_pool"], 3 if c == 2 else 2 if c % 4 == 2 else 1)

        own = Chain(pool, S["pool_own"])
        G = nc.gpsimd
        G.memset(ones[:, :], 1.0).then_inc(S["ones_ready"], 1)
        pool.wait_ge(S["dl_in"], 16)
        for e in range(2):
            G.tensor_tensor(dlp[:, e * HD:(e + 1) * HD], dlb[:, 2 * e * HD:(2 * e + 1) * HD],
                            dlb[:, (2 * e + 1) * HD:(2 * e + 2) * HD], ALU.mult).then_inc(S["start_pool"], 1)
        pool.wait_ge(S["small_in"], 16)
        pool.wait_ge(S["pos_in"], 16)
        own(G.tensor_copy(pos_f[:, :], pos_i[:, :]))
        for e in range(2):
            own(G.tensor_scalar(ang[:, e, :], pos_f[:, :], col("freq", e), None, ALU.mult))
        big = 12582912.0
        own(G.tensor_scalar(turns[:, :, :], ang[:, :, :], 1.0 / (2 * math.pi), big, ALU.mult, ALU.add))
        own(G.tensor_scalar(turns[:, :, :], turns[:, :, :], big, None, ALU.subtract))
        for cst in TWO_PI_PARTS:
            own(G.tensor_scalar(part_turn[:, :, :], turns[:, :, :], cst, None, ALU.mult))
            own(G.tensor_tensor(ang[:, :, :], ang[:, :, :], part_turn[:, :, :], ALU.subtract))
        G.tensor_scalar(ang[:, :, :], ang[:, :, :], PI_BELOW, -PI_BELOW, ALU.min, ALU.max)\
            .then_inc(S["start_pool"], 1)
        pool.wait_ge(S["x_squared"], 1)
        own(G.tensor_tensor(x_sum[:, :], x_sq[:, 0, :], x_sq[:, 1, :], ALU.add))
        for k in range(2, KC - 1):
            own(G.tensor_tensor(x_sum[:, :], x_sum[:, :], x_sq[:, k, :], ALU.add))
        G.tensor_tensor(x_sum[:, :], x_sum[:, :], x_sq[:, KC - 1, :], ALU.add).then_inc(S["x_summed"], 1)
        pool.wait_ge(S["start_act"], 4)
        own(G.tensor_tensor(cosT[:, :], cosT[:, :], cosT[:, :], ALU.mult))
        own(G.tensor_scalar(cosT[:, :], cosT[:, :], -2.0, 1.0, ALU.mult, ALU.add))

        def lows(a, b):
            turns = (b - a) // 8
            if turns:
                with pool.Fori(0, turns) as g:
                    for i in range(8):
                        low(g, a + i)
            for c in range(a + 8 * turns, b):
                low(None, c)

        def u_lows(m):
            for k in range(1, KC, 2):
                pool.wait_ge(S["uhi_ready"], KC * m + k + 1)
                G.tensor_tensor(u_lo[:, k, :], t_u[:, k % 2, :], u_hi[:, k, :].bitcast(F32), ALU.subtract)\
                    .then_inc(S["ulo_pool"], 1)

        def x_adds(l):
            pool.wait_ge(S["x3_ready"], KC)
            for j in range(1, KC, 2):
                pool.wait_ge(S["y_ready"], KC * l + j + 1)
                G.tensor_tensor(x[:, j, :], x[:, j, :], o_out[:, j, :], ALU.add).then_inc(S["x_pool"], 1)

        for c in range(SLOTS):
            low(None, c)
        lows(SLOTS, U_LAYER + SLOTS)
        u_lows(2)
        lows(U_LAYER + SLOTS, U_LAYER + LAYER_UNITS + SLOTS)
        x_adds(0)
        u_lows(3)
        lows(U_LAYER + LAYER_UNITS + SLOTS, UNITS)
        x_adds(1)

    @block.tensor
    def _(pe):
        def unit(g, c, o, rhs_hi, rhs_lo, ready=None, parts=1, first=True, last=True, turn=(8, 2)):
            s = c % SLOTS
            per_c, per_o = turn
            pe.wait_ge(S["hi_ready"], lin(g, per_c, c + 1))
            pe.wait_ge(S["lo_dve" if c % 4 == 3 else "lo_pool"], lin(g, per_c, c + 1))
            per = KC // parts
            for q in range(parts):
                oo = o + q
                if first and oo >= 4:
                    pe.wait_ge(taken[oo % 4], lin(g, per_o, oo // 4))
                for k in range(per):
                    t = q * per + k
                    if ready is not None:
                        ready(k, t)
                    dst = mm[oo % 4][:, 0:T]
                    wh = w_hi[:, s, t * P:(t + 1) * P]
                    wl = w_lo[:, s, t * P:(t + 1) * P]
                    a, b = (first and k == 0), (last and k == per - 1)
                    nc.tensor.matmul(dst, wh, rhs_hi(k), start=a, stop=False)
                    nc.tensor.matmul(dst, wh, rhs_lo(k), start=False, stop=False)
                    i = nc.tensor.matmul(dst, wl, rhs_hi(k), start=False, stop=b)
                i.then_inc(S["unit_done"] if q == parts - 1 else S["part_done"], 1)


        def first_units(n, c, o, ready, hi=u_hi, lo=u_lo):
            for q in range(n):
                pe.wait_ge(S["hi_ready"], c + q + 1)
                if c + q == 1:
                    pe.wait_ge(S["lo_first"], 1)
                else:
                    pe.wait_ge(S["lo_dve" if (c + q) % 4 == 3 else "lo_pool"], c + q + 1)
                if o + q >= 4:
                    pe.wait_ge(taken[(o + q) % 4], (o + q) // 4)
            for k in range(KC):
                ready(k, k)
                for q in range(n):
                    dst, s = mm[(o + q) % 4][:, 0:T], (c + q) % SLOTS
                    wh, wl = w_hi[:, s, k * P:(k + 1) * P], w_lo[:, s, k * P:(k + 1) * P]
                    nc.tensor.matmul(dst, wh, hi[:, k, :], start=k == 0, stop=False)
                    nc.tensor.matmul(dst, wh, lo[:, k, :], start=False, stop=False)
                    i = nc.tensor.matmul(dst, wl, hi[:, k, :], start=False, stop=k == KC - 1)
                    if k == KC - 1:
                        i.then_inc(S["unit_done"], 1)

        def keep_warm(n, o):
            if o:
                pe.wait_ge(taken[o % 4], o // 4)
            for _ in range(n):
                nc.tensor.matmul(mm[o % 4][:, 0:P], ones[:, :], ident[:, :], start=True, stop=True)

        def one_at_a_time(first, value):
            last = [first, value]

            def wait(*reader):
                pe.wait_ge(S[last[0]], last[1])
                if reader:
                    last[:] = reader
            return wait

        t_wait = one_at_a_time("tab_evac", 1)
        o_wait = one_at_a_time("ones_ready", 1)

        pe.wait_ge(S["tab_in"], 2 * 16)
        nc.tensor.matmul(ps_t[0:12, 0:3 * P], relb_s[:, :], hot[:, :], start=True, stop=True)\
            .then_inc(S["tab_done"], 1)
        pe.wait_ge(S["ones_ready"], 1)

        def mod_columns(m):
            pe.wait_ge(S["ada_used"], KC * (m + 1))
            t_wait("mod_ready", m + 1)
            for j in range(KC):
                ins = nc.tensor.matmul(ps_t[:, 496 + j:497 + j], ada_acc[:, m % 2, j * P:(j + 1) * P], ones[:, 0:1],
                                       start=True, stop=True)
            ins.then_inc(S["mod_done"], 1)

        def spread(n):
            pe.wait_ge(S["diag_ready"], DIAGS[n])
            o_wait(*SPREAD_USED[n])
            e = 1 if n == 2 else 0
            nc.tensor.matmul(ps_o[:, 0:T], ones[:, :], diag[:, 2 * e:2 * e + 2, :], start=True, stop=True)\
                .then_inc(S["rstd_ready"], 1)
            if n == 2:
                pe.wait_ge(S["diag_ready"], DIAGS[n] + 1)
                nc.tensor.matmul(ps_s[1][:, 0:T], ones[:, :], diag[:, 0:2, :], start=True, stop=True)\
                    .then_inc(S["r1_ready"], 1)

        mod_columns(SCALE1)
        pe.wait_ge(S["x_summed"], 1)
        o_wait("var_ready", 1)
        for t in range(QT):
            i = nc.tensor.matmul(ps_o[:, t:t + 1], x_sum[:, t * P:(t + 1) * P], ones[:, 0:1], start=True, stop=True)
        i.then_inc(S["stat_done"], 1)
        spread(0)
        keep_warm(WARM[4], 0)
        mod_columns(SHIFT1)
        keep_warm(WARM[2], 0)

        def iw_transpose():
            pe.wait_ge(taken[C_IW % 4], 1)
            pe.wait_ge(S["ident_in"], 16)
            pe.wait_ge(S["start_in"], 3 * 16)
            t_wait("iw_ready", 1)
            for t in range(QT):
                i = nc.tensor.transpose(ps_t[:, 8 * t:8 * t + 8], iwf[:, t * P:(t + 1) * P], ident[0:8, 0:8])
            i.then_inc(S["iw_tr"], 1)

        def index_scores(n):
            t, hh = n // 4, n % 4
            if n == 0:
                for c in (C_IQ, C_IQ + 1, C_IK):
                    pe.wait_ge(taken[c % 4], c // 4 + 1)
            if n >= 2:
                pe.wait_ge(S["relu_ready"], n - 1)
            nk = P * (t + 1)
            for half in range(2):
                i = nc.tensor.matmul(ps_s[n % 2][:, half * T:half * T + nk],
                                     iqT[32 * hh:32 * hh + 32, half, t * P:(t + 1) * P],
                                     ikT[32 * hh:32 * hh + 32, 0:nk], start=True, stop=True)
            i.then_inc(S["idx_done"], 1)

        def kv_stat():
            pe.wait_ge(S["kv_squared"], 1)
            o_wait("kv_var", 1)
            nc.tensor.matmul(ps_o[:, 0:T], ones[:, :], kv_sq[:, :], start=True, stop=True)\
                .then_inc(S["kv_stat"], 1)

        def kv_transpose():
            pe.wait_ge(S["kvT_ready"], 1)
            t_wait("kv_tok_ready", 1)
            for t in range(QT):
                i = nc.tensor.transpose(ps_t[:, t * P:(t + 1) * P], kvT[:, t * P:(t + 1) * P], ident[:, :])
            i.then_inc(S["kv_tr"], 1)

        vt_users = [("kv", 0)] + [("a", h) for h in range(NH)] + [("c", j) for j in range(2)]

        def v_transpose(n):
            kind, h = vt_users[n]
            c = C_A + 3 * h + 2 if kind == "a" else C_C + 3 * h + 2
            pe.wait_ge(taken[c % 4], c // 4 + 1)
            t_wait("vt_ready", n)
            for t in range(QT):
                i = nc.tensor.transpose(ps_t[:, t * P:(t + 1) * P], vf[:, n % 2, t * P:(t + 1) * P], ident[:, :])
            i.then_inc(S["vt_done"], 1)

        def q_and_k(r, m):
            kind, h = heads[r]
            if kind == "a":
                return aqT[m * HD:(m + 1) * HD, h % 2, :], akT[m * HD:(m + 1) * HD, h % 2, :]
            if kind == "b":
                return bqT[:, h, :], kvT[:, :]
            j, e = h // 2, h % 2
            return cqT[e * HD:(e + 1) * HD, j, :], ckT[e * HD:(e + 1) * HD, j, :]

        def scores(r):
            kind, h = heads[r]
            last_c = {"a": C_A + 3 * h + 1, "b": C_BQ + h, "c": C_C + 3 * (h // 2) + 1}[kind]
            for c in (last_c - 1, last_c):
                pe.wait_ge(taken[c % 4], c // 4 + 1)
            if r == 0:
                pe.wait_ge(S["relu_ready"], 8)
            for e, m in enumerate(maps_of[r]):
                q, k = q_and_k(r, e)
                if m >= 2:
                    pe.wait_ge(S["s_taken"], m - 1)
                bank = ps_s[m % 2]
                nc.tensor.matmul(bank[:, 0:T], q[:, P:T], k, start=True, stop=True)
                nc.tensor.matmul(bank[:, T:T + P], q[:, 0:P], k[:, 0:P], start=True, stop=True)\
                    .then_inc(S["s_done"], 1)

        def prob_transpose(r):
            pe.wait_ge(S["p_ready"], r + 1)
            t_wait("pt_ready", r + 1)
            pm = prob[:, maps_of[r][-1] % 4, :]
            nc.tensor.transpose(ps_t[:, 0:P], pm[:, T:T + P], flip[:, :])
            nc.tensor.transpose(ps_t[:, P:T], pm[:, 0:P], flip[:, :])
            nc.tensor.transpose(ps_t[:, T:T + P], pm[:, P:T], flip[:, :]).then_inc(S["t_done"], 1)

        def outputs(r):
            kind, h = heads[r]
            pe.wait_ge(S["pt_ready"], r + 1)
            o_wait("o_taken", r + 1)
            pt = probT[:, r % 2, :]
            if kind == "a":
                v, dst = v_tok[:, h, :, :], ps_o[:, 0:T]
            elif kind == "b":
                v, dst = kv_tok[:, :, :], ps_o[:, 0:T]
            else:
                e = h % 2
                v, dst = cv_tok[:, h // 2, :, e * HD:(e + 1) * HD], ps_o[e * HD:(e + 1) * HD, 0:T]
            nc.tensor.matmul(dst, v[:, 0, :], pt[:, 0:T], start=True, stop=False)
            nc.tensor.matmul(dst[:, P:T], v[:, 1, :], pt[:, T:T + P], start=False, stop=True)\
                .then_inc(S["o_done"], 1)

        def up_values(h):
            pe.wait_ge(S["o_taken"], NH + h + 1)
            t_wait("uv_taken", h + 1)
            dst = ps_t[HD * (h % 2):HD * (h % 2) + HD, 0:T]
            nc.tensor.matmul(dst, wuv[:, h, :], o_mid[:, :], start=True, stop=True).then_inc(S["uv_done"], 1)

        def subln_stat(h):
            pe.wait_ge(S["osq_ready"], h + 1)
            o_wait("ovar_ready", h + 1)
            nc.tensor.matmul(ps_o[:, 0:T], ones[:, :], o_var[:, h, :], start=True, stop=True)\
                .then_inc(S["ostat_done"], 1)

        def u_ready(m):
            def wait(k, t):
                if m < 2:
                    pe.wait_ge(S["ulo_ready"], KC * m + k + 1)
                elif k % 2:
                    pe.wait_ge(S["ulo_pool"], KC // 2 * (m - 2) + k // 2 + 1)
                else:
                    pe.wait_ge(S["ulo_ready"], KC * 2 + KC // 2 * (m - 2) + k // 2 + 1)
            return wait

        uh = lambda k: u_hi[:, k, :]
        ul = lambda k: u_lo[:, k, :]
        for c in range(N_QKV + N_GATE):
            if c == 0:
                first_units(FIRST, c, c, u_ready(0))
            elif c >= FIRST:
                unit(None, c, c, uh, ul)
            if c == 1:
                iw_transpose()
            if 4 <= c <= 11:
                index_scores(c - 4)
            if c == 5:
                kv_stat()
            if c == 9:
                kv_transpose()
            if c in VT_AT:
                v_transpose(VT_AT[c])
            if c in MOD_AT:
                mod_columns(MOD_AT[c])
            if c in s_at:
                scores(s_at[c])
            if c in o_at:
                outputs(o_at[c])
            if c in t_at:
                prob_transpose(t_at[c])
            if c in UV_AT:
                up_values(UV_AT[c])
            if c in SUB_AT:
                subln_stat(SUB_AT[c])

        o = O_BR
        for n, (kind, q) in enumerate(BR_UNITS):
            src_hi, src_lo = {"a": (oa_hi, oa_lo), "b": (ob_hi, ob_lo), "c": (oc_hi, oc_lo)}[kind]
            if n == 0:
                pe.wait_ge(S["oal_ready"], NH)
            if kind == "b":
                pe.wait_ge(S["uv_taken"], NH)
            if kind == "c":
                pe.wait_ge(S["o_taken"], 12)
            parts = 2 if kind == "a" else 4
            unit(None, U_BR + n, o, lambda k: src_hi[:, k, :], lambda k: src_lo[:, k, :], parts=parts)
            o += parts
        for j in range(KC):
            unit(None, U_WO + j, O_WO + j, lambda k: m_hi[:, k, :], lambda k: m_lo[:, k, :],
                 ready=(lambda k, t: pe.wait_ge(S["ml_ready"], k + 1)) if j == 0 else None)

        def norm_stat(n, o, two=False):
            keep_warm(WARM[0], o)
            pe.wait_ge(S["sq_used"], SQ_ADDED[n] + KC - 1)
            pe.wait_ge(S["sq_ready"], SQ_BASE[n] + KC)
            o_wait("var_ready", n + 1)
            for e in range(2 if two else 1):
                for t in range(QT):
                    col_, tok = ps_o[:, 2 * e + t:2 * e + t + 1], slice(t * P, (t + 1) * P)
                    nc.tensor.matmul(col_, acc[:, e, tok], ones[:, 0:1], start=True, stop=False)
                    i = nc.tensor.matmul(col_, sq[:, 1, e, tok], ones[:, 0:1], start=False, stop=True)
            i.then_inc(S["stat_done"], 1)
            keep_warm(WARM[1], o)
            spread(n)
            keep_warm(WARM[2], o)

        norm_stat(1, O_F1)
        first_units(FIRST, U_F1, O_F1, u_ready(1))
        mod_columns(GATE2)
        for i in range(FIRST, 8):
            unit(None, U_F1 + i, O_F1 + i, uh, ul)
        with pe.Fori(0, 3) as g:
            for i in range(8):
                unit(g, U_F1 + 8 + i, O_F1 + 8 + i, uh, ul)
        with pe.Fori(0, 2) as g:
            for j in range(4):
                for q in range(4):
                    if j == 0:
                        pe.wait_ge(S["hl_ready"], KC * (q + 1))
                    unit(g, U_F2 + 4 * j + q, O_F2 + j, lambda k: h_hi[:, q * KC + k, :],
                         lambda k: h_lo[:, q * KC + k, :], first=q == 0, last=q == 3, turn=(16, 1))
        norm_stat(2, O_LAYER, two=True)

        for l in range(LAYERS):
            uA = U_LAYER + LAYER_UNITS * l
            oA = O_LAYER + LAYER_OUTS * l

            def v_tr(g, o, H, h):
                pe.wait_ge(taken[o % 4], lin(g, 2, o // 4 + 1))
                if h + H:
                    pe.wait_ge(S["rv_ready"], lin(g, 2, H + h))
                else:
                    t_wait("rv_ready", 1)
                for t in range(QT):
                    n = nc.tensor.transpose(ps_t[:, t * P:(t + 1) * P], vfr[:, h % 2, t * P:(t + 1) * P], ident[:, :])
                n.then_inc(S["rv_tr"], 1)

            def ret_scores(g, H, h):
                pe.wait_ge(S["rot_ready"], lin(g, 4, 2 * (H + h) + 2))
                if H + h >= 2:
                    pe.wait_ge(S["rs_taken"], lin(g, 2, H + h - 1))
                if H + h == 1:
                    pe.wait_ge(S["x3_ready"], KC)
                b = ps_s[h % 2]
                nc.tensor.matmul(b[:, 0:T], kr[:, h % 2, 0:P], qr[:, h % 2, :], start=True, stop=True)
                nc.tensor.matmul(b[:, T:T + P], kr[:, h % 2, P:T], qr[:, h % 2, P:T], start=True, stop=True)\
                    .then_inc(S["rs_done"], 1)

            def ret_out(g, H, h):
                if H + h == 0:
                    o_wait("ret_taken", 1)
                if H + h:
                    if h == 0 and (H + h) >= 4:
                        pe.wait_ge(S["rvar_ready"], lin(g, 1, H // 2 - 1))
                pe.wait_ge(S["rs_taken"], lin(g, 2, H + h + 1))
                pe.wait_ge(S["rv_ready"], lin(g, 2, H + h + 1))
                if H + h:
                    pe.wait_ge(S["ret_taken"], lin(g, 2, H + h))
                nc.tensor.matmul(ps_o[:, 0:T], vtr[:, h % 2, 0, :], sdec[:, h % 2, 0:T], start=True, stop=False)
                nc.tensor.matmul(ps_o[:, P:T], vtr[:, h % 2, 1, :], sdec[:, h % 2, T:T + P], start=False, stop=True)\
                    .then_inc(S["ro_done"], 1)

            def turn(g, n0):
                c0, o0, H = uA + 8 * n0, oA + 8 * n0, RH * l + 2 * n0
                for i in range(8):
                    if n0 + i == 0:
                        first_units(2, c0, o0, u_ready(2 + l))
                    elif n0 or i >= 2:
                        unit(g, c0 + i, o0 + i, uh, ul)
                    if i == 1:
                        v_tr(g, o0, H, 0)
                    if i == 2 and n0:
                        head_stat(g, H // 2 - 1)
                    if i == 3:
                        ret_scores(g, H, 0)
                    if i == 4:
                        v_tr(g, o0 + 3, H, 1)
                    if i == 5:
                        ret_out(g, H, 0)
                    if i == 6:
                        ret_scores(g, H, 1)
                    if i == 7:
                        ret_out(g, H, 1)

            def head_stat(g, n):
                pe.wait_ge(S["retsq_ready"], lin(g, 2, 2 * n + 2))
                if n % 4 == 3:
                    src = ret_sq[:, 6:8, :]
                elif g is None:
                    src = ret_sq[:, 2 * (n % 4):2 * (n % 4) + 2, :]
                else:
                    src = ret_sq[:, bass.ds(g * 2 + 2 * (n % 4), 2), :]
                nc.tensor.matmul(ps_o[:, :], ones[:, :], src, start=True, stop=True).then_inc(S["rstat_done"], 1)

            turn(None, 0)
            with pe.Fori(0, 3) as g:
                turn(g, 1)
            for i in range(8):
                unit(None, uA + 32 + i, oA + 32 + i, uh, ul)
                if i == 0:
                    head_stat(None, 4 * l + 3)
            with pe.Fori(0, 3) as g:
                for i in range(8):
                    unit(g, uA + 40 + i, oA + 40 + i, uh, ul)
            for j in range(KC):
                for q in range(2):
                    off = KC if q == 0 else 0
                    rd = None
                    if j == 0:
                        rd = (lambda s: lambda k, t: pe.wait_ge(S[s], KC * l + k + 1))("mixr_ready" if q == 0 else "mixc_ready")
                    unit(None, uA + 64 + 2 * j + q, oA + 64 + j,
                         (lambda off: lambda k: mix_hi[:, off + k, :])(off),
                         (lambda off: lambda k: mix_lo[:, off + k, :])(off), ready=rd, first=q == 0, last=q == 1)
            norm_stat(3 + 2 * l, oA + LAYER_OUTS)
            if l + 1 < LAYERS:
                for j in range(KC):
                    pe.wait_ge(S["sq_ready"], SQ_BASE[4] + j + 1)
                    for t in range(QT):
                        i = nc.tensor.matmul(ps_s[t][:, 0:1], sq[:, j % 2, j // 2 % 2, t * P:(t + 1) * P], ones[:, 0:1],
                                             start=j == 0, stop=j == KC - 1)
                    i.then_inc(S["sq_summed"], 1)
                    keep_warm(WARM[3], oA + LAYER_OUTS)
                keep_warm(WARM[1], oA + LAYER_OUTS)
                spread(4)
                keep_warm(WARM[2], oA + LAYER_OUTS)

    @block.scalar
    def _(act):
        own = Chain(act, S["act_own"])
        A = nc.scalar.activation

        def high(g, c):
            if c >= UNITS:
                return
            act.wait_ge(raw_in[(c // 2) % RAW_PAIRS], lin(g, 16, 16 * (c // 2 // RAW_PAIRS + 1)))
            if c >= SLOTS:
                act.wait_ge(S["unit_done"], lin(g, 8, c - SLOTS + 1))
            r = raw[:, (c // 2) % RAW_PAIRS, (c % 2) * KC * P:(c % 2 + 1) * KC * P]
            A(w_hi[:, c % SLOTS, :], r, ACT.Copy).then_inc(S["hi_ready"], 1)

        act.wait_ge(S["small_in"], 16)
        A(cond[:, :], vec[:, COLS["c"]:COLS["c"] + KC], ACT.Exp, scale=-1.0).then_inc(S["start_act"], 1)
        act.wait_ge(S["tab_done"], 1)
        A(tab_s[:, :], ps_t[0:12, 0:3 * P], ACT.Copy).then_inc(S["tab_evac"], 1)
        act.wait_ge(S["tab_evac"], 1)
        act.dma_start(tab_d, tab_s[:, :]).then_inc(S["tab_out"], 16)
        act.wait_ge(S["start_dve"], 1)
        A(lam[:, 2:4], lam[:, 0:2], ACT.Exp).then_inc(S["start_act"], 1)
        act.wait_ge(S["x_in"], 16)
        A(x_sq[:, :, :], x[:, :, :], ACT.Square).then_inc(S["x_squared"], 1)

        def root(n):
            act.wait_ge(S["var_ready"], n + 1)
            w = 4 if n == 2 else 2
            A(tok_r[:, 0:w], tok_v[:, 0:w], ACT.Sqrt).then_inc(S["root_ready"], 1)

        def make_u_hi(m, shift):
            for k in range(KC):
                act.wait_ge(S["t_ready"], KC * m + k + 1)
                if shift is None:
                    A(u_hi[:, k, :], t_u[:, k % 2, :], ACT.Copy).then_inc(S["uhi_ready"], 1)
                else:
                    A(u_hi[:, k, :], t_u[:, k % 2, :], ACT.Identity, bias=mod[:, shift, k:k + 1])\
                        .then_inc(S["uhi_ready"], 1)

        root(0)
        act.wait_ge(S["start_pool"], 3)
        A(sinT[:, :], ang[:, 1, :], ACT.Sin).then_inc(S["start_act"], 1)
        A(cosT[:, :], ang[:, 0, :], ACT.Sin, scale=0.5).then_inc(S["start_act"], 1)
        for c in range(FIRST):
            high(None, c)
        make_u_hi(0, SHIFT1)
        for c in range(FIRST, SLOTS):
            high(None, c)

        def take(c, dst, w=P):
            A(dst, mm[c % 4][0:w, 0:T], ACT.Copy).then_inc(taken[c % 4], 1)

        def take_reversed(c, dst, w=P):
            src = mm[c % 4][0:w, 0:T].rearrange("p (t q) -> p t q", t=QT)[:, :, ::-1]
            A(dst.rearrange("p (t q) -> p t q", t=QT), src, ACT.Copy).then_inc(taken[c % 4], 1)

        def qkv_evac(c):
            if c == C_IW:
                take_reversed(c, iwf[:, :], 8)
            elif c < C_IK:
                take_reversed(c, iqT[:, c - C_IQ, :])
            elif c == C_IK:
                take(c, ikT[:, :])
            elif c == C_KV:
                take(c, kvf[:, :])
                act.wait_ge(taken[c % 4], c // 4 + 1)
                A(kv_sq[:, :], kvf[:, :], ACT.Square).then_inc(S["kv_squared"], 1)
            elif c < C_A:
                take_reversed(c, bqT[:, c - C_BQ, :])
            elif c < C_C:
                h, e = (c - C_A) // 3, (c - C_A) % 3
                if e < 2 and h >= 2:
                    act.wait_ge(S["s_done"], 2 * (h - 2) + 2)
                if e == 2:
                    n = 1 + h
                    if n >= 3:
                        act.wait_ge(S["vt_done"], n - 2)
                    take(c, vf[:, n % 2, :])
                else:
                    (take_reversed, take)[e](c, (aqT, akT)[e][:, h % 2, :])
            else:
                j, e = (c - C_C) // 3, (c - C_C) % 3
                if e == 2:
                    n = 1 + NH + j
                    act.wait_ge(S["vt_done"], n - 2)
                    take(c, vf[:, n % 2, :])
                else:
                    (take_reversed, take)[e](c, (cqT, ckT)[e][:, j, :])

        def act_iw():
            act.wait_ge(S["iw_tr"], 1)
            A(iw[:, :, :], ps_t[:, 0:16], ACT.Copy).then_inc(S["iw_ready"], 1)

        def act_relu(n):
            t = n // 4
            act.wait_ge(S["idx_done"], n + 1)
            if n >= 2:
                act.wait_ge(S["idx_used"], n - 1)
            nk = P * (t + 1)
            src = ps_s[n % 2][:, :].rearrange("p (e k) -> p e k", e=2)[:, :, 0:nk]
            dst = relu_s[:, n % 2, :].rearrange("p (e k) -> p e k", e=2)[:, :, 0:nk]
            A(dst, src, ACT.Relu).then_inc(S["relu_ready"], 1)

        def act_kv_tok():
            act.wait_ge(S["kv_tr"], 1)
            A(kv_tok[:, :, :], ps_t[:, 0:T], ACT.Copy).then_inc(S["kv_tok_ready"], 1)

        def act_vt(n):
            kind, h = ("a", n - 1) if n <= NH else ("c", n - 1 - NH)
            act.wait_ge(S["vt_done"], n)
            A(v_tok[:, h, :, :] if kind == "a" else cv_tok[:, h, :, :], ps_t[:, 0:T], ACT.Copy)\
                .then_inc(S["vt_ready"], 1)

        def act_exp(m):
            act.wait_ge(S["max_ready"], m + 1)
            p = prob[:, m % 4, :]
            own(A(p[:, 0:T], p[:, 0:T], ACT.Exp, bias=nmax[:, m, 0:1], accum_out=psum_[:, m, 0:1]))
            A(p[:, T:T + P], p[:, T:T + P], ACT.Exp, bias=nmax[:, m, 1:2], accum_out=psum_[:, m, 1:2])\
                .then_inc(S["exp_ready"], 1)

        def act_pt(r):
            act.wait_ge(S["t_done"], r + 1)
            if r >= 2:
                act.wait_ge(S["o_done"], r - 1)
            A(probT[:, r % 2, :], ps_t[:, 0:3 * P], ACT.Copy).then_inc(S["pt_ready"], 1)

        def act_o(r):
            kind, h = heads[r]
            act.wait_ge(S["o_done"], r + 1)
            if kind == "a":
                A(o_raw[:, h, :], ps_o[:, 0:T], ACT.Copy).then_inc(S["o_taken"], 1)
                act.wait_ge(S["o_taken"], r + 1)
                A(o_var[:, h, :], o_raw[:, h, :], ACT.Square).then_inc(S["osq_ready"], 1)
            elif kind == "b":
                if h:
                    act.wait_ge(S["uv_done"], h)
                A(o_mid[:, :], ps_o[:, 0:T], ACT.Copy).then_inc(S["o_taken"], 1)
            else:
                e = h % 2
                A(oc_hi[e * HD:(e + 1) * HD, h // 2, :], ps_o[e * HD:(e + 1) * HD, 0:T], ACT.Copy)\
                    .then_inc(S["och_ready"], 1)

        def act_uv(h):
            e = h % 2
            act.wait_ge(S["uv_done"], h + 1)
            A(ob_hi[e * HD:(e + 1) * HD, h // 2, :], ps_t[e * HD:(e + 1) * HD, 0:T], ACT.Copy)\
                .then_inc(S["obh_ready"], 1)

        def act_gate(c):
            j = c - N_QKV
            A(gates[:, j, :], mm[c % 4][:, 0:T], ACT.Tanh, scale=0.5, bias=half_gb[:, j:j + 1])\
                .then_inc(taken[c % 4], 1)

        for c in range(N_QKV + N_GATE):
            act.wait_ge(S["unit_done"], c + 1)
            (qkv_evac if c < N_QKV else act_gate)(c)
            high(None, c + SLOTS)
            if c in LOAD_AT:
                ada_load(act, LOAD_AT[c])
            if c == 1:
                act_iw()
            if 4 <= c <= 11:
                act_relu(c - 4)
            if c == 6:
                act.wait_ge(S["kv_var"], 1)
                A(kv_r[:, :], kv_v[:, :], ACT.Sqrt).then_inc(S["kv_rstd"], 1)
            if c == 9:
                act_kv_tok()
            if c in exp_at:
                for m in maps_of[exp_at[c]]:
                    act_exp(m)
            if c in VT_AT:
                act_vt(VT_AT[c])
            if c in o_at:
                act_o(o_at[c])
            if c in t_at:
                act_pt(t_at[c])
            if c in UV_AT:
                act_uv(UV_AT[c])
            if c == ROOT_AT:
                act.wait_ge(S["ovar_ready"], NH)
                A(o_var[:, :, :], o_var[:, :, :], ACT.Sqrt).then_inc(S["orstd_ready"], 1)
            if OAH_AT <= c < OAH_AT + NH:
                h = c - OAH_AT
                act.wait_ge(S["ofin_ready"], h + 1)
                A(oa_hi[:, h, :], o_raw[:, h, :], ACT.Copy).then_inc(S["oah_ready"], 1)

        for n, (kind, q) in enumerate(BR_UNITS):
            act.wait_ge(S["unit_done"], U_BR + n + 1)
            high(None, U_BR + n + SLOTS)
            if n < 2:
                ada_load(act, 20 + n)
            if kind == "c":
                for j in range(4 * q, 4 * q + 4):
                    act.wait_ge(S["m_ready"], j + 1)
                    A(m_hi[:, j, :], merged[:, j, :], ACT.Copy, scale=0.5).then_inc(S["mh_ready"], 1)

        def square_x(n, j, src, scale=None):
            if n == 4 and j >= 2:
                if j >= 4:
                    act.wait_ge(S["sq_summed"], j - 3)
            elif n == 5 and j < 2:
                act.wait_ge(S["sq_summed"], KC - 1 + j)
            elif j != 1 and SQ_ADDED[n] + j:
                act.wait_ge(S["sq_used"], SQ_ADDED[n] + max(j - 1, 0))
            elif n > 1:
                act.wait_ge(S["stat_done"], n)
            if scale is None:
                A(sq[:, j % 2, j // 2 % 2 if n == 4 else 0, :], src, ACT.Square).then_inc(S["sq_ready"], 1)
            else:
                own(A(sq[:, j % 2, 0, :], src, ACT.Square))
                A(sq[:, j % 2, 1, :], src, ACT.Square, scale=scale).then_inc(S["sq_ready"], 1)

        for j in range(KC):
            o = O_WO + j
            act.wait_ge(S["unit_done"], U_WO + j + 1)
            high(None, U_WO + j + SLOTS)
            if j in (2, 4):
                ada_load(act, 21 + j // 2)
            act.wait_ge(taken[o % 4], o // 4 + 1)
            square_x(1, j, x[:, j, :])
        root(1)
        make_u_hi(1, SHIFT2)

        def up_turn(g, base):
            for i in range(8):
                c, o, f = U_F1 + base + i, O_F1 + base + i, base + i
                act.wait_ge(S["unit_done"], lin(g, 8, c + 1))
                if f >= 2:
                    act.wait_ge(S["hl_ready"], lin(g, 8, f - 1))
                A(relu_h[:, f % 2, :], mm[o % 4][:, 0:T], ACT.Relu).then_inc(taken[o % 4], 1)
                high(g, c + SLOTS)
                act.wait_ge(taken[o % 4], lin(g, 2, o // 4 + 1))
                dst = h_hi[:, f, :] if g is None else h_hi[:, bass.ds(g * 8 + f, 1), :][:, 0, :]
                A(dst, relu_h[:, f % 2, :], ACT.Square).then_inc(S["hh_ready"], 1)

        up_turn(None, 0)
        with act.Fori(0, 3) as g:
            up_turn(g, 8)

        act.wait_ge(S["mod_ready"], 6)
        act.dma_start(dec[:, :, :], decay).then_inc(S["decay_in"], 16)
        for j in range(KC):
            for q in range(4):
                c = U_F2 + 4 * j + q
                act.wait_ge(S["unit_done"], c + 1)
                high(None, c + SLOTS)
            o = O_F2 + j
            act.wait_ge(taken[o % 4], o // 4 + 1)
            square_x(2, j, x[:, j, :], scale=col("norm_final", j))
        root(2)
        make_u_hi(2, None)

        for l in range(LAYERS):
            uA = U_LAYER + LAYER_UNITS * l
            oA = O_LAYER + LAYER_OUTS * l
            H = RH * l

            def a_turn(g, n0):
                c0, o0, hb = uA + 8 * n0, oA + 8 * n0, H + 2 * n0

                def step(i):
                    act.wait_ge(S["unit_done"], lin(g, 8, c0 + i + 1))

                def v_copy(i, h):
                    if hb + h >= 2:
                        act.wait_ge(S["rv_tr"], lin(g, 2, hb + h - 1))
                    A(vfr[:, h, :], mm[(o0 + i) % 4][:, 0:T], ACT.Copy).then_inc(taken[(o0 + i) % 4], 1)

                def vt_copy(h):
                    act.wait_ge(S["rv_tr"], lin(g, 2, hb + h + 1))
                    if hb + h >= 2:
                        act.wait_ge(S["ro_done"], lin(g, 2, hb + h - 1))
                    A(vtr[:, h, :, :], ps_t[:, 0:T], ACT.Copy).then_inc(S["rv_ready"], 1)

                def z_tanh(i, h):
                    act.wait_ge(taken[(o0 + i) % 4], lin(g, 2, (o0 + i) // 4 - 1))
                    A(th[:, h, :], mm[(o0 + i) % 4][:, 0:T], ACT.Tanh, scale=0.5).then_inc(S["th_ready"], 1)

                def o_copy(h):
                    act.wait_ge(S["ro_done"], lin(g, 2, hb + h + 1))
                    n = 2 * n0 + h
                    dst = ret[:, n, :] if g is None else ret[:, bass.ds(g * 2 + n, 1), :][:, 0, :]
                    ds2 = ret_sq[:, n, :] if g is None else ret_sq[:, bass.ds(g * 2 + n, 1), :][:, 0, :]
                    A(dst, ps_o[:, 0:T], ACT.Copy).then_inc(S["ret_taken"], 1)
                    act.wait_ge(S["ret_taken"], lin(g, 2, hb + h + 1))
                    A(ds2, dst, ACT.Square).then_inc(S["retsq_ready"], 1)

                for i in range(8):
                    step(i)
                    if i in (0, 3):
                        v_copy(i, i // 3)
                    if i >= 6:
                        z_tanh(i, i - 6)
                    if i in (1, 4):
                        vt_copy(i // 4)
                    high(g, c0 + i + SLOTS)
                    if i in (5, 7):
                        o_copy(i // 7)

            a_turn(None, 0)
            with act.Fori(0, 3) as g:
                a_turn(g, 1)

            def conv_high(g, n):
                act.wait_ge(S["yc_ready"], lin(g, 2, 8 * l + n + 1))
                dst = mix_hi[:, n, :] if g is None else mix_hi[:, bass.ds(g * 2 + n, 1), :][:, 0, :]
                A(dst, cy[:, n % 2, :], ACT.Copy, scale=0.5).then_inc(S["ych_ready"], 1)

            def b_turn(g, n0):
                c0, o0 = uA + 32 + 8 * n0, oA + 32 + 8 * n0
                for e in range(2):
                    n = 2 * n0 + e
                    for i in range(4):
                        ii = 4 * e + i
                        o = o0 + ii
                        act.wait_ge(S["unit_done"], lin(g, 8, c0 + ii + 1))
                        if i == 0:
                            act.wait_ge(taken[(o + 1) % 4], lin(g, 2, (o + 1) // 4 - 1))
                            A(cc[:, e, :], mm[o % 4][:, 0:T], ACT.Copy).then_inc(taken[o % 4], 1)
                        if i == 3:
                            act.wait_ge(taken[o % 4], lin(g, 2, o // 4 - 1))
                            A(th_c[:, e, :], mm[o % 4][:, 0:T], ACT.Tanh, scale=0.5).then_inc(S["th_ready"], 1)
                        high(g, c0 + ii + SLOTS)
                        if i == 0 and n:
                            conv_high(g, n - 1)
                        if ii == 1 and n0 == 0:
                            act.wait_ge(S["rvar_ready"], 4 * l + 4)
                            A(ret_sq[:, :, :], ret_sq[:, :, :], ACT.Sqrt).then_inc(S["rrstd_ready"], 1)
                        if i == 2:
                            act.wait_ge(S["yr_ready"], lin(g, 2, 8 * l + n + 1))
                            dst = mix_hi[:, KC + n, :] if g is None else mix_hi[:, bass.ds(g * 2 + KC + n, 1), :][:, 0, :]
                            A(dst, qr[:, e, :], ACT.Copy, scale=0.5).then_inc(S["yrh_ready"], 1)

            b_turn(None, 0)
            with act.Fori(0, 3) as g:
                b_turn(g, 1)
            conv_high(None, KC - 1)
            for j in range(KC):
                for q in range(2):
                    c = uA + 64 + 2 * j + q
                    act.wait_ge(S["unit_done"], c + 1)
                    if q == 1:
                        o = oA + 64 + j
                        square_x(3 + 2 * l, j, mm[o % 4][:, 0:T])
                        A(o_out[:, j, :], mm[o % 4][:, 0:T], ACT.Identity, scale=col("post", KC * l + j))\
                            .then_inc(taken[o % 4], 1)
                    high(None, c + SLOTS)
            root(3 + 2 * l)
            if l + 1 < LAYERS:
                for j in range(KC):
                    act.wait_ge(S["x_pool" if j % 2 else "x_new"], j // 2 + 1)
                    square_x(4 + 2 * l, j, x[:, j, :])
                root(4 + 2 * l)
                make_u_hi(3 + l, None)

    @block.vector
    def _(dve):
        own = Chain(dve, S["dve_own"])
        V = nc.vector

        def low(g, c):
            if c % 4 != 3 or c >= UNITS:
                return
            dve.wait_ge(S["hi_ready"], lin(g, 8, c + 1))
            if c >= SLOTS:
                dve.wait_ge(S["unit_done"], lin(g, 8, c - SLOTS + 1))
            r = raw[:, (c // 2) % RAW_PAIRS, (c % 2) * KC * P:(c % 2 + 1) * KC * P]
            s = c % SLOTS
            V.tensor_tensor(w_lo[:, s, :], r, w_hi[:, s, :].bitcast(F32), ALU.subtract).then_inc(S["lo_dve"], 4)

        dve.wait_ge(S["start_act"], 1)
        own(V.tensor_scalar(cond[:, :], cond[:, :], 1.0, None, ALU.add))
        own(V.reciprocal(cond[:, :], cond[:, :]))
        own(V.tensor_tensor(cond[:, :], cond[:, :], vec[:, COLS["c"]:COLS["c"] + KC], ALU.mult))

        def ada_step(a):
            part_, k = a // KC, a % KC
            n = a // 2
            slot, q, seen = ada_slot(n)
            dve.wait_ge(ada_in[q], 16 * seen)
            src = slot[:, (a % 2) * D:(a % 2 + 1) * D]
            if k == 0:
                if part_ >= 2:
                    dve.wait_ge(S["mod_done"], part_ - 1)
                ins = V.tensor_scalar(ada_acc[:, part_ % 2, :], src, cond[:, k:k + 1], None, ALU.mult)
            else:
                ins = V.scalar_tensor_tensor(ada_acc[:, part_ % 2, :], src, cond[:, k:k + 1],
                                             ada_acc[:, part_ % 2, :], ALU.mult, ALU.add)
            ins.then_inc(S["ada_used"], 1)
            dve.wait_ge(S["ada_used"], a + 1)

        def mod_take(m):
            dve.wait_ge(S["mod_done"], m + 1)
            V.tensor_tensor(mod[:, m, :], ps_t[:, 496:504], vec[:, COLS["ada_b"] + KC * m:COLS["ada_b"] + KC * (m + 1)],
                            ALU.add).then_inc(S["mod_ready"], 1)

        def variance(n):
            if n == 4:
                dve.wait_ge(S["sq_summed"], KC)
                for t in range(QT):
                    own(V.tensor_scalar(tok_v[:, t:t + 1], ps_s[t][:, 0:1], 1.0 / D, EPS, ALU.mult, ALU.add))
            else:
                dve.wait_ge(S["stat_done"], n + 1 if n < 4 else n)
                own(V.tensor_scalar(tok_v[:, 0:2], ps_o[:, 0:2], 1.0 / D, EPS, ALU.mult, ALU.add))
            inverse = V.reciprocal(tok_v[:, 0:2], tok_v[:, 0:2])
            if n == 2:
                own(inverse)
                own(V.scalar_tensor_tensor(tok_v[:, 2:4], ps_o[:, 2:4], 1.0 / D, tok_v[:, 0:2], ALU.mult, ALU.mult))
                own(V.tensor_scalar(tok_v[:, 2:4], tok_v[:, 2:4], EPS, None, ALU.add))
                own(V.reciprocal(tok_v[:, 2:4], tok_v[:, 2:4]))
                inverse = V.tensor_tensor(tok_v[:, 2:4], tok_v[:, 2:4], tok_v[:, 0:2], ALU.mult)
            inverse.then_inc(S["var_ready"], 1)
            dve.wait_ge(S["root_ready"], n + 1)
            for e in ((1, 0) if n == 2 else (0,)):
                for t in range(QT):
                    c = 2 * e + t
                    ins = V.tensor_scalar(diag[:, c, :], ident[:, :], tok_r[:, c:c + 1], None, ALU.mult)
                ins.then_inc(S["diag_ready"], 1)

        def make_u(m, scale, shift):
            r = ps_o[:, 0:T]
            def lo(k):
                if m >= 2 and k % 2:
                    return
                dve.wait_ge(S["uhi_ready"], KC * m + k + 1)
                hi = u_hi[:, k, :].bitcast(F32)
                if shift is None:
                    V.tensor_tensor(u_lo[:, k, :], t_u[:, k % 2, :], hi, ALU.subtract).then_inc(S["ulo_ready"], 1)
                else:
                    V.scalar_tensor_tensor(u_lo[:, k, :], t_u[:, k % 2, :], mod[:, shift, k:k + 1], hi,
                                           ALU.add, ALU.subtract).then_inc(S["ulo_ready"], 1)

            def slot_read(k):
                if m < 2:
                    if KC * m + k >= 2:
                        dve.wait_ge(S["ulo_ready"], KC * m + k - 1)
                elif k % 2 == 0:
                    dve.wait_ge(S["ulo_ready"], KC * 2 + KC // 2 * (m - 2) + k // 2)
                elif KC // 2 * (m - 2) + k // 2:
                    dve.wait_ge(S["ulo_pool"], KC // 2 * (m - 2) + k // 2)

            for k in range(KC):
                slot_read(k)
                V.scalar_tensor_tensor(t_u[:, k % 2, :], x[:, k, :], scale(k), r, ALU.mult, ALU.mult)\
                    .then_inc(S["t_ready"], 1)
                if k:
                    lo(k - 1)
            lo(KC - 1)

        for a in range(2 * KC):
            ada_step(a)
            if a == 1:
                dve.wait_ge(S["start_pool"], 2)
                V.tensor_reduce(lam[:, 0:2], dlp[:, :].rearrange("p (a d) -> p a d", a=2), AX.X, ALU.add)\
                    .then_inc(S["start_dve"], 1)
                own(V.tensor_scalar(half_gb[:, :], vec[:, COLS["gate_b"]:COLS["gate_b"] + 24], 0.5, None, ALU.mult))
                own(V.tensor_scalar(subln[:, :], col("subln"), 1.0 - LAM_INIT, None, ALU.mult))
            if a == 3:
                dve.wait_ge(S["start_act"], 2)
                own(V.tensor_tensor(lam[:, 4:5], lam[:, 3:4], lam[:, 2:3], ALU.subtract))
                own(V.tensor_scalar(lam[:, 5:6], lam[:, 4:5], LAM_INIT, None, ALU.subtract))
            if a == KC:
                mod_take(SCALE1)
                dve.wait_ge(S["mod_ready"], 1)
                own(V.scalar_tensor_tensor(a_mix[:, 0, :], mod[:, SCALE1, :], 1.0,
                                           vec[:, COLS["norm_mix"]:COLS["norm_mix"] + KC], ALU.add, ALU.mult))
            if a == KC + 5:
                dve.wait_ge(S["ident_in"], 16)
                variance(0)
        dve.wait_ge(S["hi_ready"], 2)
        V.tensor_tensor(w_lo[:, 1, :], raw[:, 0, KC * P:2 * KC * P], w_hi[:, 1, :].bitcast(F32), ALU.subtract)\
            .then_inc(S["lo_first"], 1)
        mod_take(SHIFT1)
        dve.wait_ge(S["rstd_ready"], 1)
        dve.wait_ge(S["x_in"], 16)
        make_u(0, lambda k: a_mix[:, 0, k:k + 1], SHIFT1)
        low(None, 3)

        def score_tile(t):
            return score[:, 0:T] if t else score[:, T:T + P]

        def idx_add(n):
            t, hh = n // 4, n % 4
            dve.wait_ge(S["relu_ready"], n + 1)
            if n == 0:
                dve.wait_ge(S["start_in"], 3 * 16)
                dve.wait_ge(S["iw_ready"], 1)
            nk = P * (t + 1)
            dst = score_tile(t)
            for e in range(2):
                src = relu_s[:, n % 2, e * T:e * T + nk]
                prev = dst if (hh or e) else (cmask[:, :] if t else cmask[:, P:T])
                ins = V.scalar_tensor_tensor(dst, src, iw[:, t, hh + 4 * e:hh + 4 * e + 1], prev, ALU.mult, ALU.add)
                if e == 0:
                    own(ins)
                else:
                    ins.then_inc(S["idx_used"], 1)
                    dve.wait_ge(S["idx_used"], n + 1)

        def topk_round(t):
            dst = score_tile(t)
            own(V.max(top8[:, :], dst))
            own(V.match_replace(dst, top8[:, :], dst, TAKEN))

        def kv_norm_var():
            dve.wait_ge(S["kv_stat"], 1)
            own(V.tensor_scalar(kv_v[:, :], ps_o[:, 0:T], 1.0 / P, EPS, ALU.mult, ALU.add))
            V.reciprocal(kv_v[:, :], kv_v[:, :]).then_inc(S["kv_var"], 1)

        def kv_norm():
            dve.wait_ge(S["kv_rstd"], 1)
            V.scalar_tensor_tensor(kvT[:, :], kvf[:, :], col("kv_norm"), kv_r[:, :], ALU.mult, ALU.mult)\
                .then_inc(S["kvT_ready"], 1)

        SCALE = {"a": HD ** -0.5, "b": P ** -0.5, "c": HD ** -0.5}
        BIAS = {"a": 0, "b": NH, "c": 2 * NH}

        def logits(m):
            kind, h, _ = maps[m]
            r = heads.index((kind, h))
            dve.wait_ge(S["s_done"], m + 1)
            if m == 0:
                dve.wait_ge(S["bias_in"], 16)
            if m >= 4:
                dve.wait_ge(S["t_done"], heads.index(maps[m - 4][:2]) + 1)
            p, b, ps = prob[:, m % 4, :], bias[:, BIAS[kind] + h, :], ps_s[m % 2]
            own(V.scalar_tensor_tensor(p[:, 0:T], ps[:, 0:T], SCALE[kind], b, ALU.mult, ALU.add))
            V.scalar_tensor_tensor(p[:, T:T + P], ps[:, T:T + P], SCALE[kind], b[:, P:T], ALU.mult, ALU.add)\
                .then_inc(S["s_taken"], 1)
            dve.wait_ge(S["s_taken"], m + 1)
            if kind == "b":
                own(V.tensor_tensor(p, p, score[:, :], ALU.add))
            own(V.tensor_reduce(nmax[:, m, 0:1], p[:, 0:T], AX.X, ALU.max, negate=True))
            V.tensor_reduce(nmax[:, m, 1:2], p[:, T:T + P], AX.X, ALU.max, negate=True).then_inc(S["max_ready"], 1)

        def normalise(r):
            ms = maps_of[r]
            m = ms[-1]
            dve.wait_ge(S["exp_ready"], m + 1)
            for q in ms:
                own(V.reciprocal(rsum[:, q, :], psum_[:, q, :]))
            p = prob[:, m % 4, :]
            if len(ms) == 1:
                own(V.tensor_scalar(p[:, 0:T], p[:, 0:T], rsum[:, m, 0:1], None, ALU.mult))
                V.tensor_scalar(p[:, T:T + P], p[:, T:T + P], rsum[:, m, 1:2], None, ALU.mult)\
                    .then_inc(S["p_ready"], 1)
                return
            p0 = prob[:, ms[0] % 4, :]
            own(V.tensor_scalar(lnorm[:, r, :], rsum[:, m, :], lam[:, 5:6], None, ALU.mult))
            own(V.tensor_scalar(p[:, 0:T], p[:, 0:T], lnorm[:, r, 0:1], None, ALU.mult))
            own(V.tensor_scalar(p[:, T:T + P], p[:, T:T + P], lnorm[:, r, 1:2], None, ALU.mult))
            own(V.scalar_tensor_tensor(p[:, 0:T], p0[:, 0:T], rsum[:, ms[0], 0:1], p[:, 0:T], ALU.mult, ALU.add))
            V.scalar_tensor_tensor(p[:, T:T + P], p0[:, T:T + P], rsum[:, ms[0], 1:2], p[:, T:T + P],
                                   ALU.mult, ALU.add).then_inc(S["p_ready"], 1)

        def sub_var(h):
            dve.wait_ge(S["ostat_done"], h + 1)
            own(V.tensor_scalar(o_var[:, h, :], ps_o[:, 0:T], 1.0 / P, EPS, ALU.mult, ALU.add))
            V.reciprocal(o_var[:, h, :], o_var[:, h, :]).then_inc(S["ovar_ready"], 1)

        def c_low(h):
            e = h % 2
            s = slice(e * HD, (e + 1) * HD)
            dve.wait_ge(S["och_ready"], h + 1)
            V.tensor_tensor(oc_lo[s, h // 2, :], ps_o[s, 0:T], oc_hi[s, h // 2, :].bitcast(F32), ALU.subtract)\
                .then_inc(S["o_taken"], 1)

        def b_low(h):
            e = h % 2
            s = slice(e * HD, (e + 1) * HD)
            dve.wait_ge(S["obh_ready"], h + 1)
            V.tensor_tensor(ob_lo[s, h // 2, :], ps_t[s, 0:T], ob_hi[s, h // 2, :].bitcast(F32), ALU.subtract)\
                .then_inc(S["uv_taken"], 1)

        for c in range(N_QKV + N_GATE):
            dve.wait_ge(S["unit_done"], c + 1)
            if c == 5:
                kv_norm_var()
            if c == 7:
                kv_norm()
            if 5 <= c <= 12:
                idx_add(c - 5)
            if c in norm_at:
                normalise(norm_at[c])
            if c in s_at:
                for m in maps_of[s_at[c]]:
                    logits(m)
            if c in o_at and heads[o_at[c]][0] == "c":
                c_low(heads[o_at[c]][1])
            if c in UV_AT:
                b_low(UV_AT[c])
            if c in SUB_AT:
                sub_var(SUB_AT[c])
            low(None, c + SLOTS)
            if c in MOD_AT:
                mod_take(MOD_AT[c])
            for t in TOPK_AT.get(c, []):
                topk_round(t)
            if c == 22:
                own(V.tensor_scalar(score[:, :], score[:, :], TAKEN / 2, NEG, ALU.is_gt, ALU.mult))
            if c in ADA_AT:
                ada_step(2 * KC + ADA_AT.index(c))
            if FIN_AT <= c < FIN_AT + NH:
                h = c - FIN_AT
                dve.wait_ge(S["orstd_ready"], 1)
                V.scalar_tensor_tensor(o_raw[:, h, :], o_raw[:, h, :], subln[:, 0:1], o_var[:, h, :], ALU.mult, ALU.mult)\
                    .then_inc(S["ofin_ready"], 1)
            if OAL_AT <= c < OAL_AT + NH:
                h = c - OAL_AT
                dve.wait_ge(S["oah_ready"], h + 1)
                V.tensor_tensor(oa_lo[:, h, :], o_raw[:, h, :], oa_hi[:, h, :].bitcast(F32), ALU.subtract)\
                    .then_inc(S["oal_ready"], 1)
        dve.wait_ge(S["mod_ready"], 5)
        own(V.scalar_tensor_tensor(a_mix[:, 1, :], mod[:, SCALE2, :], 1.0, vec[:, COLS["norm_mlp"]:COLS["norm_mlp"] + KC],
                                   ALU.add, ALU.mult))

        o = O_BR
        parts_seen = 0
        for n, (kind, q) in enumerate(BR_UNITS):
            parts = 2 if kind == "a" else 4
            for e in range(parts):
                j = parts * q + e
                if e < parts - 1:
                    parts_seen += 1
                    dve.wait_ge(S["part_done"], parts_seen)
                else:
                    dve.wait_ge(S["unit_done"], U_BR + n + 1)
                g_ = gates[:, {"a": 0, "b": KC, "c": 2 * KC}[kind] + j, :]
                if kind == "a":
                    V.scalar_tensor_tensor(merged[:, j, :], g_, 1.0, mm[o % 4][:, 0:T], ALU.add, ALU.mult)\
                        .then_inc(taken[o % 4], 1)
                else:
                    V.scalar_tensor_tensor(part[:, o % 2, :], g_, 1.0, mm[o % 4][:, 0:T], ALU.add, ALU.mult)\
                        .then_inc(taken[o % 4], 1)
                    dve.wait_ge(taken[o % 4], o // 4 + 1)
                    ins = V.tensor_tensor(merged[:, j, :], merged[:, j, :], part[:, o % 2, :], ALU.add)
                    if kind == "b":
                        own(ins)
                    else:
                        ins.then_inc(S["m_ready"], 1)
                o += 1
            low(None, U_BR + n + SLOTS)
            if kind == "c":
                for j in range(4 * q, 4 * q + 4):
                    dve.wait_ge(S["mh_ready"], j + 1)
                    V.scalar_tensor_tensor(m_lo[:, j, :], merged[:, j, :], 0.5, m_hi[:, j, :].bitcast(F32),
                                           ALU.mult, ALU.subtract).then_inc(S["ml_ready"], 1)

        def add_square(n, j, two=False):
            dve.wait_ge(S["sq_ready"], SQ_BASE[n] + j + 1)
            w = 2 if two else 1
            if j == 0:
                ins = V.tensor_copy(acc[:, 0:w, :], sq[:, 0, 0:w, :])
            else:
                ins = V.tensor_tensor(acc[:, 0:w, :], acc[:, 0:w, :], sq[:, j % 2, 0:w, :], ALU.add)
            ins.then_inc(S["sq_used"], 1)
            dve.wait_ge(S["sq_used"], SQ_ADDED[n] + j + 1)

        for j in range(KC):
            o = O_WO + j
            dve.wait_ge(S["unit_done"], U_WO + j + 1)
            V.scalar_tensor_tensor(x[:, j, :], mm[o % 4][:, 0:T], mod[:, GATE1, j:j + 1], x[:, j, :], ALU.mult, ALU.add)\
                .then_inc(taken[o % 4], 1)
            low(None, U_WO + j + SLOTS)
            if j:
                add_square(1, j - 1)
            if j < KC - 1:
                ada_step(5 * KC + j)
        variance(1)
        dve.wait_ge(S["rstd_ready"], 2)
        make_u(1, lambda k: a_mix[:, 1, k:k + 1], SHIFT2)

        ada_step(6 * KC - 1)
        def up_turn(g, base):
            for i in range(8):
                c, o, f = U_F1 + base + i, O_F1 + base + i, base + i
                dve.wait_ge(taken[o % 4], lin(g, 2, o // 4 + 1))
                own(V.tensor_tensor(h_full[:, f % 2, :], relu_h[:, f % 2, :], relu_h[:, f % 2, :], ALU.mult))
                dve.wait_ge(S["hh_ready"], lin(g, 8, f + 1))
                sl = (lambda t: t[:, f, :]) if g is None else (lambda t: t[:, bass.ds(g * 8 + f, 1), :][:, 0, :])
                V.tensor_tensor(sl(h_lo), h_full[:, f % 2, :], sl(h_hi).bitcast(F32), ALU.subtract)\
                    .then_inc(S["hl_ready"], 1)
                low(g, c + SLOTS)

        up_turn(None, 0)
        mod_take(GATE2)
        with dve.Fori(0, 3) as g:
            own.enter(g, 8)
            up_turn(g, 8)
            own.leave(3)
        dve.wait_ge(S["mod_ready"], 6)
        for j in range(KC):
            for q in range(4):
                c = U_F2 + 4 * j + q
                dve.wait_ge(S["unit_done"], c + 1)
                if q == 3:
                    o = O_F2 + j
                    V.scalar_tensor_tensor(x[:, j, :], mm[o % 4][:, 0:T], mod[:, GATE2, j:j + 1], x[:, j, :],
                                           ALU.mult, ALU.add).then_inc(taken[o % 4], 1)
                low(None, c + SLOTS)
                if q == 0 and j:
                    add_square(2, j - 1, two=True)
        own(V.tensor_tensor(nf_pre[:, :], vec[:, COLS["norm_final"]:COLS["norm_final"] + KC],
                            vec[:, COLS["pre"]:COLS["pre"] + KC], ALU.mult))
        variance(2)
        dve.wait_ge(S["rstd_ready"], 3)
        make_u(2, lambda k: nf_pre[:, k:k + 1], None)
        own(V.memset(cv[:, :, 0:2], 0.0))

        for l in range(LAYERS):
            uA = U_LAYER + LAYER_UNITS * l
            oA = O_LAYER + LAYER_OUTS * l
            H = RH * l

            def a_turn(g, n0):
                c0, o0, hb = uA + 8 * n0, oA + 8 * n0, H + 2 * n0

                def rotate(i, h, is_k):
                    ps, dst = mm[(o0 + i) % 4], (kr if is_k else qr)[:, h, :]
                    if hb + h >= 2:
                        dve.wait_ge(S["rs_done"], lin(g, 2, hb + h - 1))
                    own(V.tensor_tensor(rt1[:, :], ps[:, 0:T], cosT[:, :], ALU.mult))
                    own(V.tensor_tensor(rt2[0:HD, :], ps[HD:P, 0:T], sinT[HD:P, :], ALU.mult))
                    V.tensor_tensor(rt2[HD:P, :], ps[0:HD, 0:T], sinT[0:HD, :], ALU.mult)\
                        .then_inc(taken[(o0 + i) % 4], 1)
                    dve.wait_ge(taken[(o0 + i) % 4], lin(g, 2, (o0 + i) // 4 + 1))
                    V.tensor_tensor(dst, rt1[:, :], rt2[:, :], ALU.add).then_inc(S["rot_ready"], 1)
                    n = 2 * (hb + h) + (2 if is_k else 1)
                    dve.wait_ge(S["rot_ready"], lin(g, 4, n))

                def decayed(h):
                    dve.wait_ge(S["rs_done"], lin(g, 2, hb + h + 1))
                    if hb + h >= 2:
                        dve.wait_ge(S["ro_done"], lin(g, 2, hb + h - 1))
                    n = 2 * n0 + h
                    d = dec[:, n, :] if g is None else dec[:, bass.ds(g * 2 + n, 1), :][:, 0, :]
                    V.tensor_tensor(sdec[:, h, :], ps_s[h][:, 0:3 * P], d, ALU.mult).then_inc(S["rs_taken"], 1)

                def silu_z(i, h):
                    n = 2 * n0 + h
                    dst = zsil[:, n, :] if g is None else zsil[:, bass.ds(g * 2 + n, 1), :][:, 0, :]
                    dve.wait_ge(S["th_ready"], lin(g, 2, ZU[l] + 2 * n0 + h + 1))
                    V.scalar_tensor_tensor(dst, th[:, h, :], 1.0, mm[(o0 + i) % 4][:, 0:T], ALU.add, ALU.mult)\
                        .then_inc(taken[(o0 + i) % 4], 1)
                    dve.wait_ge(taken[(o0 + i) % 4], lin(g, 2, (o0 + i) // 4 + 1))

                for i in range(8):
                    if l == 0 and n0 == 0 and 2 <= i < 6:
                        dve.wait_ge(S["r1_ready"], 1)
                        for k in (2 * i - 4, 2 * i - 3):
                            V.scalar_tensor_tensor(x[:, k, :], x[:, k, :], col("norm_final", k), ps_s[1][:, 0:T],
                                                   ALU.mult, ALU.mult).then_inc(S["x3_ready"], 1)
                    dve.wait_ge(S["unit_done"], lin(g, 8, c0 + i + 1))
                    if i in (1, 2, 4, 5):
                        rotate(i, i // 3, i in (2, 5))
                    if i >= 6:
                        silu_z(i, i - 6)
                    if i == 3:
                        decayed(0)
                    if i == 6:
                        decayed(1)
                    low(g, c0 + i + SLOTS)
                    if i == 2 and n0:
                        head_var(g, hb // 2 - 1)

            def head_var(g, n):
                dve.wait_ge(S["rstat_done"], lin(g, 1, n + 1))
                q = 2 * (n % 4)
                dst = ret_sq[:, q:q + 2, :] if g is None else ret_sq[:, bass.ds(g * 2 + q, 2), :]
                own(V.tensor_scalar(rv[:, :, :], ps_o[:, :].rearrange("p (a t) -> p a t", a=2), 1.0 / P, EPS, ALU.mult, ALU.add))
                V.reciprocal(dst, rv[:, :, :]).then_inc(S["rvar_ready"], 1)
                dve.wait_ge(S["rvar_ready"], lin(g, 1, n + 1))

            if l == 0:
                dve.wait_ge(S["decay_in"], 16)
            a_turn(None, 0)
            with dve.Fori(0, 3) as g:
                own.enter(g, 9)
                a_turn(g, 1)
                own.leave(3)

            def conv_low(g, n):
                dve.wait_ge(S["ych_ready"], lin(g, 2, 8 * l + n + 1))
                row = (lambda t: t[:, n, :]) if g is None else (lambda t: t[:, bass.ds(g * 2 + n, 1), :][:, 0, :])
                V.scalar_tensor_tensor(row(mix_lo), cy[:, n % 2, :], 0.5, row(mix_hi).bitcast(F32),
                                       ALU.mult, ALU.subtract).then_inc(S["mixc_ready"], 1)
                dve.wait_ge(S["mixc_ready"], lin(g, 2, 8 * l + n + 1))

            def b_turn(g, n0):
                c0, o0 = uA + 32 + 8 * n0, oA + 32 + 8 * n0

                def row(t, n):
                    return t[:, n, :] if g is None else t[:, bass.ds(g * 2 + n, 1), :][:, 0, :]

                for e in range(2):
                    n = 2 * n0 + e

                    def wcol(tap):
                        at = COLS["conv"] + 24 * l + 8 * tap + n
                        return vec[:, at:at + 1] if g is None else vec[:, bass.ds(g * 2 + at, 1)]

                    for i in range(4):
                        ii = 4 * e + i
                        o = o0 + ii
                        ps = mm[o % 4][:, 0:T]
                        tk, tv = taken[o % 4], lin(g, 2, o // 4 + 1)
                        dve.wait_ge(S["unit_done"], lin(g, 8, c0 + ii + 1))
                        if i == 1:
                            dve.wait_ge(taken[(o - 1) % 4], lin(g, 2, (o - 1) // 4 + 1))
                            V.tensor_tensor(cv[:, e, 2:T + 2], cc[:, e, :], ps, ALU.mult).then_inc(tk, 1)
                            dve.wait_ge(tk, tv)
                            own(V.tensor_scalar(cy[:, e, :], cv[:, e, 0:T], wcol(0), None, ALU.mult))
                            for tap in (1, 2):
                                own(V.scalar_tensor_tensor(cy[:, e, :], cv[:, e, tap:tap + T], wcol(tap), cy[:, e, :],
                                                           ALU.mult, ALU.add))
                        if i == 2:
                            V.tensor_tensor(cy[:, e, :], cy[:, e, :], ps, ALU.mult).then_inc(tk, 1)
                            dve.wait_ge(tk, tv)
                        if i == 3:
                            dve.wait_ge(S["th_ready"], lin(g, 2, ZU[l] + 8 + n + 1))
                            V.scalar_tensor_tensor(rt2[:, :], th_c[:, e, :], 1.0, ps, ALU.add, ALU.mult).then_inc(tk, 1)
                            dve.wait_ge(tk, tv)
                            V.tensor_tensor(cy[:, e, :], cy[:, e, :], rt2[:, :], ALU.mult).then_inc(S["yc_ready"], 1)
                            dve.wait_ge(S["yc_ready"], lin(g, 2, 8 * l + n + 1))
                        low(g, c0 + ii + SLOTS)
                        if ii == 0 and n0 == 0:
                            head_var(None, 4 * l + 3)
                        if i == 1:
                            if n == 0:
                                dve.wait_ge(S["rrstd_ready"], l + 1)
                            own(V.tensor_tensor(rt1[:, :], row(ret, n), row(ret_sq, n), ALU.mult))
                            V.tensor_tensor(qr[:, e, :], rt1[:, :], row(zsil, n), ALU.mult).then_inc(S["yr_ready"], 1)
                            dve.wait_ge(S["yr_ready"], lin(g, 2, 8 * l + n + 1))
                            if n:
                                conv_low(g, n - 1)
                        if i == 3:
                            dve.wait_ge(S["yrh_ready"], lin(g, 2, 8 * l + n + 1))
                            V.scalar_tensor_tensor(row(mix_lo, KC + n), qr[:, e, :], 0.5,
                                                   row(mix_hi, KC + n).bitcast(F32), ALU.mult, ALU.subtract)\
                                .then_inc(S["mixr_ready"], 1)

            b_turn(None, 0)
            with dve.Fori(0, 3) as g:
                own.enter(g, 8)
                b_turn(g, 1)
                own.leave(3)
            conv_low(None, KC - 1)
            n_out = 3 + 2 * l
            for j in range(KC):
                for q in range(2):
                    c = uA + 64 + 2 * j + q
                    dve.wait_ge(S["unit_done"], c + 1)
                    low(None, c + SLOTS)
                if j:
                    add_square(n_out, j - 1)
            variance(n_out)
            dve.wait_ge(S["rstd_ready"], n_out + 1)
            last = l + 1 == LAYERS
            dve.wait_ge(S["x3_ready"], KC)
            dve.wait_ge(taken[(oA + 71) % 4], (oA + 71) // 4 + 1)
            for j in range(KC):
                V.tensor_tensor(o_out[:, j, :], o_out[:, j, :], ps_o[:, 0:T], ALU.mult).then_inc(S["y_ready"], 1)
                if j % 2 == 0:
                    dve.wait_ge(S["y_ready"], KC * l + j + 1)
                    V.tensor_tensor(x[:, j, :], x[:, j, :], o_out[:, j, :], ALU.add).then_inc(S["x_new"], 1)
            dve.wait_ge(S["x_new"], KC // 2 * (l + 1))
            dve.wait_ge(S["x_pool"], KC // 2 * (l + 1))
            if not last:
                variance(n_out + 1)
                dve.wait_ge(S["rstd_ready"], n_out + 2)
                make_u(3 + l, lambda k: col("pre", KC * (l + 1) + k), None)


BR_UNITS = [("a", 0), ("a", 1), ("b", 0), ("a", 2), ("c", 0), ("a", 3), ("b", 1), ("c", 1)]
SQ_BASE = {1: 0, 2: KC, 3: 2 * KC, 4: 3 * KC, 5: 4 * KC}
SQ_ADDED = {1: 0, 2: KC - 1, 3: 2 * (KC - 1), 4: 3 * (KC - 1), 5: 3 * (KC - 1)}
DIAGS = {0: 1, 1: 2, 2: 3, 3: 5, 4: 6, 5: 7}
SPREAD_USED = {0: ("t_ready", KC), 1: ("t_ready", 2 * KC), 2: ("t_ready", 3 * KC), 3: ("y_ready", KC),
               4: ("t_ready", 4 * KC), 5: ("y_ready", 2 * KC)}
ZU = [0, 16]
TWO_PI_PARTS = []
_rest = 2 * math.pi
for _bits in (8, 11, 24):
    _q = 2.0 ** (math.floor(math.log2(_rest)) + 1 - _bits)
    TWO_PI_PARTS.append(math.floor(_rest / _q) * _q)
    _rest -= TWO_PI_PARTS[-1]
PI_BELOW = float(np.nextafter(np.float32(math.pi), np.float32(0)))


def _units(w, order=None):
    n = w.shape[1] // P
    return w.reshape(KC, P, n, P).transpose(2, 1, 0, 3).reshape(n, P, KC * P)


def _columns(v):
    return v.reshape(-1, P).T


def _stream(w_in, w_br_a, w_br_b, w_br_c, w_o, w_ff1, w_ff2, w_in_2, w_out_2):
    at = np.cumsum([0, 512, 512, 512, 512, 128, 256, 32, 8, 256, 256, 256, 3072])
    aq, ak, av, bq, bkv, biq, bik, biw, cq, ck, cv, gate = [w_in[:, a:b] for a, b in zip(at[:-1], at[1:])]
    parts = [_units(np.pad(biw, ((0, 0), (0, P - 8)))), _units(biq), _units(np.concatenate([bik] * 4, axis=1)),
             _units(bkv), _units(bq)]
    for h in range(NH):
        parts += [_units(m[:, h * P:(h + 1) * P]) for m in (aq, ak, av)]
    for j in range(2):
        parts += [_units(m[:, j * P:(j + 1) * P]) for m in (cq, ck, cv)]
    parts.append(_units(gate))
    for kind, q in BR_UNITS:
        w = {"a": w_br_a, "b": w_br_b, "c": w_br_c}[kind]
        k = w.shape[0] // P
        n = KC // k
        w = w[:, q * n * P:(q + 1) * n * P].reshape(k, P, n, P)
        parts.append(w.transpose(1, 2, 0, 3).reshape(1, P, KC * P))
    parts += [_units(w_o), _units(w_ff1)]
    f = [_units(w_ff2[q * D:(q + 1) * D]) for q in range(4)]
    parts.append(np.stack(f, axis=1).reshape(4 * KC, P, KC * P))
    for l in range(LAYERS):
        m = _units(w_in_2[l]).reshape(8, KC, P, KC * P)
        c_b, c_c, c_x, c_z, r_q, r_k, r_v, r_z = m
        heads = [(r_v, 0), (r_q, 0), (r_k, 0), (r_v, 1), (r_q, 1), (r_k, 1), (r_z, 0), (r_z, 1)]
        for h in range(0, RH, 2):
            parts.append(np.stack([w[h + e] for w, e in heads]))
        for j in range(KC):
            parts.append(np.stack([c_c[j], c_x[j], c_b[j], c_z[j]]))
        conv, ret = _units(w_out_2[l][:D]), _units(w_out_2[l][D:])
        parts.append(np.stack([ret, conv], axis=1).reshape(2 * KC, P, KC * P))
    s = np.concatenate(parts)
    assert s.shape[0] == UNITS
    s = np.concatenate([s, np.zeros_like(s[:UNITS % 2])])
    return np.ascontiguousarray(s.reshape(-1, 2, P, KC * P).transpose(0, 2, 1, 3).reshape(-1, P, 2 * KC * P))


def _constants():
    f = np.float32
    dist = T - 1 - np.arange(3 * P)
    n = np.maximum(dist, 0)
    half = N_BUCKETS // 2
    large = half + (np.log(np.maximum(n, 1).astype(f) / f(half)) / f(math.log(MAX_DISTANCE / half))
                    * f(N_BUCKETS - half)).astype(np.int32)
    bucket = np.where(dist < 0, N_BUCKETS, np.where(n < half, n, np.minimum(large, N_BUCKETS - 1)))
    onehot = (bucket[None] == np.arange(N_BUCKETS + 1)[:, None]).astype(f)
    i = np.arange(P)
    cmask = np.concatenate([np.zeros((P, P), f), np.where(i[None] > i[::-1, None], f(NEG), f(0))], axis=1).astype(f)
    lg = np.log1p(-np.exp2(-5.0 - np.arange(RH)))
    diff = i[None, :] - i[:, None]
    diag = np.where(diff >= 0, np.exp(lg[:, None, None] * np.maximum(diff, 0)), 0.0)
    off = np.exp(lg[:, None, None] * (diff + P))
    dec = (np.concatenate([diag, off, diag], axis=2) * P ** -0.5).transpose(1, 0, 2).astype(f)
    freq = (f(1.0) / f(10000.0) ** (np.arange(HD, dtype=f) / f(HD))).astype(f)
    freq = np.concatenate([freq, freq])
    sign = np.where(i < HD, f(1), f(-1))
    return dict(onehot=onehot, ident=np.eye(P, dtype=f), cmask=cmask, decay=np.ascontiguousarray(dec),
                freq=np.stack([freq, freq * sign], axis=1))


def kernel(**inp):
    import concourse.bacc as bacc
    from concourse.bass_utils import run_bass_kernel_spmd

    a = {k: np.asarray(v) for k, v in inp.items()}
    k = _constants()
    order = [1, 0, 2, 3, 4, 5]
    vec = [_columns(a["c"][0]), _columns(a["ada_b"][0].reshape(6, D)[order].reshape(-1)), _columns(a["norm_mix"][0]), _columns(a["gate_b"][0]),
           _columns(a["diff_subln"][0]), _columns(a["dsa_kv_norm"][0]), _columns(a["norm_mlp"][0]),
           _columns(a["norm_final"]), _columns(a["pre_norm_2"].reshape(-1)), _columns(a["post_norm_2"].reshape(-1)),
           _columns(a["conv_w_2"].reshape(-1)), k["freq"]]
    arrays = {
        "xT": a["x"][0].T.reshape(KC, P, T).transpose(1, 0, 2),
        "weights": _stream(a["w_in"][0], a["w_br_a"][0], a["w_br_b"][0], a["w_br_c"][0], a["w_o"][0], a["w_ff1"][0],
                           a["w_ff2"][0], a["w_in_2"], a["w_out_2"]),
        "ada": a["ada_w"][0].reshape(KC // 2, 2, P, 6, D).transpose(3, 0, 2, 1, 4)[order].reshape(24, P, 2 * D),
        "cols": np.concatenate(vec, axis=1),
        "dl": a["diff_lambda"][0].reshape(1, -1),
        "relb": np.concatenate([a["rel_bias"], np.full((1, 12), NEG, np.float32)]),
        "onehot": k["onehot"], "ident_d": k["ident"], "flip_d": k["ident"][::-1], "cmask_d": k["cmask"], "decay": k["decay"],
        "positions": a["positions_2"].astype(np.int32),
        "w_uv": a["dsa_w_uv"][0].transpose(1, 0, 2),
    }
    arrays = {n: np.ascontiguousarray(v) for n, v in arrays.items()}
    nc = bacc.Bacc("TRN2", target_bir_lowering=False, num_devices=1)
    aps = {n: nc.dram_tensor(n, v.shape, mybir.dt.from_np(v.dtype), kind="ExternalInput").ap()
           for n, v in arrays.items()}
    out = nc.dram_tensor("out", (P, KC, T), F32, kind="ExternalOutput").ap()
    build(nc, out=out, **aps)
    res = run_bass_kernel_spmd(nc, [arrays], core_ids=[0]).results[0]["out"]
    return res.transpose(1, 0, 2).reshape(D, T).T.reshape(1, T, D)
```
